# Optimizing a Trainium2 kernel written in Bass

```python
import jax
import jax.numpy as jnp
from jax import lax
import numpy as np

D_MODEL = 2048
BATCH = 1
SEQ = 256
DEPTH = 1

GRID_W = 64
CTX_LEN = 256
MIX_WIDTH = D_MODEL
ATT_WIDTH = MIX_WIDTH // 2
RWKV_WIDTH = MIX_WIDTH - ATT_WIDTH
ATT_HEAD_DIM = 128
N_Q_HEADS = ATT_WIDTH // ATT_HEAD_DIM
N_KV_HEADS = 2
GQA_GROUP = N_Q_HEADS // N_KV_HEADS
KV_WIDTH = N_KV_HEADS * ATT_HEAD_DIM
WINDOW = 128
BLOCK = 128
ROPE_BASE = 10000.0
RWKV_HEAD_DIM = 64
N_RWKV_HEADS = RWKV_WIDTH // RWKV_HEAD_DIM
LORA_W = 64
LORA_A = 64
LORA_G = 128
N_DIR = 2
ATT_IN = ATT_WIDTH + 2 * KV_WIDTH
RWKV_IN = 3 * RWKV_WIDTH + N_DIR * (LORA_W + LORA_A) + LORA_G
IN_WIDTH = ATT_IN + RWKV_IN
D_FF = 4 * D_MODEL
N_MOD = 6
NORM_EPS = 1e-6
GN_EPS = 64e-5

kernel_name = 'hybrid_swa_rwkv7_diffusion_block'

def rms_norm(x, g):
    xf = x.astype(jnp.float32)
    y = xf * lax.rsqrt(jnp.mean(xf * xf, axis=-1, keepdims=True) + NORM_EPS)
    return (y * g.astype(jnp.float32)).astype(x.dtype)

def modulate(x, g, shift, scale):
    return rms_norm(x, g) * (1 + scale) + shift

def squared_relu_mlp(h, w1, w2):
    return jnp.square(jax.nn.relu(h @ w1)) @ w2

def axial_rope_tables(n_tokens):
    rows = n_tokens // GRID_W
    row_pos = jnp.repeat(jnp.arange(rows, dtype=jnp.float32), GRID_W)
    col_pos = jnp.tile(jnp.arange(GRID_W, dtype=jnp.float32), rows)
    n_freq = ATT_HEAD_DIM // 4
    inv_freq = ROPE_BASE ** (-jnp.arange(n_freq, dtype=jnp.float32) / n_freq)
    ang_r = row_pos[:, None] * inv_freq[None, :]
    ang_c = col_pos[:, None] * inv_freq[None, :]
    return jnp.cos(ang_r), jnp.sin(ang_r), jnp.cos(ang_c), jnp.sin(ang_c)

def rope_rotate(x, cos, sin):
    n = cos.shape[-1]
    x1, x2 = x[..., :n], x[..., n:]
    cs, sn = cos[:, None, :], sin[:, None, :]
    return jnp.concatenate([x1 * cs - x2 * sn, x2 * cs + x1 * sn], axis=-1)

def apply_axial_rope(x, cos_r, sin_r, cos_c, sin_c):
    half = ATT_HEAD_DIM // 2
    out = jnp.concatenate([rope_rotate(x[..., :half], cos_r, sin_r),
                           rope_rotate(x[..., half:], cos_c, sin_c)], axis=-1)
    return out.astype(x.dtype)

def split_projection(p):
    B, T, _ = p.shape
    q = p[..., :ATT_WIDTH].reshape(B, T, N_Q_HEADS, ATT_HEAD_DIM)
    k = p[..., ATT_WIDTH:ATT_WIDTH + KV_WIDTH].reshape(B, T, N_KV_HEADS, ATT_HEAD_DIM)
    v = p[..., ATT_WIDTH + KV_WIDTH:ATT_IN].reshape(B, T, N_KV_HEADS, ATT_HEAD_DIM)
    return q, k, v, p[..., ATT_IN:]

def window_attention_with_context(q, k, v, kc, vc, sink):
    B, S = q.shape[:2]
    nb = S // BLOCK
    span = 3 * BLOCK
    scale = ATT_HEAD_DIM ** -0.5
    qb = q.reshape(B, nb, BLOCK, N_KV_HEADS, GQA_GROUP, ATT_HEAD_DIM)

    def band(t):
        tb = jnp.pad(t, ((0, 0), (BLOCK, BLOCK), (0, 0), (0, 0)))
        tb = tb.reshape(B, nb + 2, BLOCK, N_KV_HEADS, ATT_HEAD_DIM)
        return jnp.concatenate([tb[:, :-2], tb[:, 1:-1], tb[:, 2:]], axis=2)

    k_band, v_band = band(k), band(v)
    blk = jnp.arange(nb)[:, None, None]
    q_pos = blk * BLOCK + jnp.arange(BLOCK)[None, :, None]
    k_pos = (blk - 1) * BLOCK + jnp.arange(span)[None, None, :]
    valid = (jnp.abs(k_pos - q_pos) <= WINDOW) & (k_pos >= 0) & (k_pos < S)
    s_loc = jnp.einsum('bnqhgd,bnkhd->bnhgqk', qb, k_band).astype(jnp.float32) * scale
    s_loc = jnp.where(valid[None, :, None, None], s_loc, -jnp.inf)
    s_ctx = jnp.einsum('bnqhgd,bchd->bnhgqc', qb, kc).astype(jnp.float32) * scale
    s_sink = jnp.broadcast_to(sink.astype(jnp.float32).reshape(1, 1, N_KV_HEADS, GQA_GROUP, 1, 1),
                              s_ctx.shape[:-1] + (1,))
    p = jax.nn.softmax(jnp.concatenate([s_loc, s_ctx, s_sink], axis=-1), axis=-1).astype(v.dtype)
    o = (jnp.einsum('bnhgqk,bnkhd->bnqhgd', p[..., :span], v_band)
         + jnp.einsum('bnhgqc,bchd->bnqhgd', p[..., span:-1], vc))
    return o.reshape(B, S, ATT_WIDTH)

def context_self_attention(qc, kc, vc, sink):
    B, C = qc.shape[:2]
    scale = ATT_HEAD_DIM ** -0.5
    qg = qc.reshape(B, C, N_KV_HEADS, GQA_GROUP, ATT_HEAD_DIM)
    s = jnp.einsum('bqhgd,bkhd->bhgqk', qg, kc).astype(jnp.float32) * scale
    s_sink = jnp.broadcast_to(sink.astype(jnp.float32).reshape(1, N_KV_HEADS, GQA_GROUP, 1, 1),
                              s.shape[:-1] + (1,))
    p = jax.nn.softmax(jnp.concatenate([s, s_sink], axis=-1), axis=-1).astype(vc.dtype)
    o = jnp.einsum('bhgqk,bkhd->bqhgd', p[..., :-1], vc)
    return o.reshape(B, C, ATT_WIDTH)

def token_shift(x, mu_prev, mu_next):
    xp = jnp.pad(x[:, :-1], ((0, 0), (1, 0), (0, 0)))
    xn = jnp.pad(x[:, 1:], ((0, 0), (0, 1), (0, 0)))
    return x + mu_prev * (xp - x) + mu_next * (xn - x)

def rwkv_streams(slab, mu_prev, mu_next, w0, w2, a0, a2, g2, k_k, k_a):
    B, T, _ = slab.shape
    H, N, R = N_RWKV_HEADS, RWKV_HEAD_DIM, RWKV_WIDTH
    s = token_shift(slab, mu_prev, mu_next)
    r, k, v = s[..., :R], s[..., R:2 * R], s[..., 2 * R:3 * R]
    o1 = 3 * R + N_DIR * LORA_W
    o2 = o1 + N_DIR * LORA_A
    w_lo = s[..., 3 * R:o1].reshape(B, T, N_DIR, LORA_W)
    a_lo = s[..., o1:o2].reshape(B, T, N_DIR, LORA_A)
    g_lo = s[..., o2:]
    w_log = -jax.nn.softplus(-(w0 + jnp.einsum('btdl,dlr->btdr', jnp.tanh(w_lo), w2)).astype(jnp.float32)) - 0.5
    decay = jnp.exp(-jnp.exp(w_log))
    a = jax.nn.sigmoid((a0 + jnp.einsum('btdl,dlr->btdr', a_lo, a2)).astype(jnp.float32))
    g = jax.nn.sigmoid(g_lo) @ g2
    kkf = (k * k_k).astype(jnp.float32).reshape(B, T, H, N)
    kk = kkf / jnp.maximum(jnp.sqrt(jnp.sum(kkf * kkf, axis=-1, keepdims=True)), 1e-12)
    k_dir = k.astype(jnp.float32)[:, :, None, :] * (1 + (a - 1) * k_a.astype(jnp.float32))
    heads = lambda t: t.reshape(t.shape[:-1] + (H, N))
    return (heads(r), kk, heads(v), g, heads(decay), heads(a), heads(k_dir))

def rwkv_direction(state0, streams, d, emit):
    r, kk, v, g, decay, a, k_dir = streams
    xs = (r, decay[:, :, d], k_dir[:, :, d], v, -kk, kk * a[:, :, d])
    xs = tuple(jnp.moveaxis(t.astype(jnp.float32), 1, 0) for t in xs)

    def step(state, inp):
        r_t, w_t, k_t, v_t, a_t, b_t = inp
        sa = jnp.einsum('bhvk,bhk->bhv', state, a_t)
        state = (state * w_t[:, :, None, :] + sa[..., None] * b_t[:, :, None, :]
                 + v_t[..., None] * k_t[:, :, None, :])
        if emit:
            return state, jnp.einsum('bhvk,bhk->bhv', state, r_t)
        return state, None

    state, ys = lax.scan(step, state0, xs, reverse=(d == 1))
    if emit:
        ys = jnp.moveaxis(ys, 0, 1)
    return state, ys

def rwkv_readout(streams, y_f, y_b, r_k, ln_w, ln_b):
    r, kk, v, g, decay, a, k_dir = streams
    H, N = N_RWKV_HEADS, RWKV_HEAD_DIM
    y = y_f + y_b
    mu = jnp.mean(y, axis=-1, keepdims=True)
    var = jnp.mean(jnp.square(y - mu), axis=-1, keepdims=True)
    y = (y - mu) * lax.rsqrt(var + GN_EPS) * ln_w.astype(jnp.float32).reshape(H, N) + ln_b.astype(jnp.float32).reshape(H, N)
    k_bonus = 0.5 * (k_dir[:, :, 0] + k_dir[:, :, 1])
    y = y + jnp.sum(r.astype(jnp.float32) * k_bonus * r_k.astype(jnp.float32), axis=-1, keepdims=True) * v.astype(jnp.float32)
    B, T = y.shape[:2]
    return (y.reshape(B, T, RWKV_WIDTH) * g.astype(jnp.float32)).astype(g.dtype)

def setup_inputs(seed: int = 0) -> dict:
    key = jax.random.key(seed)
    ks = jax.random.split(key, 32)
    L, D, R = DEPTH, D_MODEL, RWKV_WIDTH
    f32 = jnp.float32

    def nrm(k, shape, scale):
        return jax.random.normal(k, shape, f32) * scale

    def gain(k, shape):
        return 1.0 + nrm(k, shape, 0.02)

    return {
        'x': nrm(ks[0], (BATCH, SEQ, D), 1.0),
        'c': nrm(ks[1], (BATCH, D), 1.0),
        'ctx': nrm(ks[2], (BATCH, CTX_LEN, D), 1.0),
        'c_ctx': nrm(ks[3], (D,), 1.0),
        'w_ada': nrm(ks[4], (L, D, N_MOD * D), D ** -0.5),
        'b_ada': nrm(ks[5], (L, N_MOD * D), 0.01),
        'g_pre_mix': gain(ks[6], (L, D)),
        'g_post_mix': gain(ks[7], (L, D)),
        'g_pre_mlp': gain(ks[8], (L, D)),
        'g_post_mlp': gain(ks[9], (L, D)),
        'w_in': nrm(ks[10], (L, D, IN_WIDTH), D ** -0.5),
        'attn_sink': nrm(ks[11], (L, N_Q_HEADS), 0.5),
        'rwkv_mu_prev': jax.random.uniform(ks[12], (L, RWKV_IN), f32, 0.0, 0.5),
        'rwkv_mu_next': jax.random.uniform(ks[13], (L, RWKV_IN), f32, 0.0, 0.5),
        'rwkv_w0': nrm(ks[14], (L, N_DIR, R), 0.5),
        'rwkv_w2': nrm(ks[15], (L, N_DIR, LORA_W, R), 0.5 * LORA_W ** -0.5),
        'rwkv_a0': nrm(ks[16], (L, N_DIR, R), 0.5),
        'rwkv_a2': nrm(ks[17], (L, N_DIR, LORA_A, R), 0.5 * LORA_A ** -0.5),
        'rwkv_g2': nrm(ks[18], (L, LORA_G, R), LORA_G ** -0.5),
        'rwkv_k_k': 0.85 + nrm(ks[19], (L, R), 0.05),
        'rwkv_k_a': 1.0 + nrm(ks[20], (L, R), 0.05),
        'rwkv_r_k': nrm(ks[21], (L, N_RWKV_HEADS, RWKV_HEAD_DIM), 0.1),
        'rwkv_ln_w': gain(ks[22], (L, R)),
        'rwkv_ln_b': nrm(ks[23], (L, R), 0.01),
        'w_out': nrm(ks[24], (L, D, D), D ** -0.5),
        'w_mlp_in': nrm(ks[25], (L, D, D_FF), D ** -0.5),
        'w_mlp_out': nrm(ks[26], (L, D_FF, D), D_FF ** -0.5),
    }

def reference(x, c, ctx, c_ctx, w_ada, b_ada, g_pre_mix, g_post_mix, g_pre_mlp, g_post_mlp,
              w_in, attn_sink, rwkv_mu_prev, rwkv_mu_next, rwkv_w0, rwkv_w2, rwkv_a0, rwkv_a2,
              rwkv_g2, rwkv_k_k, rwkv_k_a, rwkv_r_k, rwkv_ln_w, rwkv_ln_b, w_out, w_mlp_in, w_mlp_out):
    B, S, _ = x.shape
    rope = axial_rope_tables(S)
    silu_c = jax.nn.silu(c)
    silu_cc = jax.nn.silu(c_ctx)
    zero_state = jnp.zeros((B, N_RWKV_HEADS, RWKV_HEAD_DIM, RWKV_HEAD_DIM), jnp.float32)
    for l in range(DEPTH):
        last = l == DEPTH - 1
        mod = (silu_c @ w_ada[l] + b_ada[l])[:, None, :]
        sh1, sc1, gt1, sh2, sc2, gt2 = jnp.split(mod, N_MOD, axis=-1)
        cmod = silu_cc @ w_ada[l] + b_ada[l]
        csh1, csc1, cgt1, csh2, csc2, cgt2 = jnp.split(cmod, N_MOD, axis=-1)
        rwkv_p = (rwkv_mu_prev[l], rwkv_mu_next[l], rwkv_w0[l], rwkv_w2[l], rwkv_a0[l],
                  rwkv_a2[l], rwkv_g2[l], rwkv_k_k[l], rwkv_k_a[l])

        h = modulate(x, g_pre_mix[l], sh1, sc1)
        hc = modulate(ctx, g_pre_mix[l], csh1, csc1)
        q, k, v, slab = split_projection(h @ w_in[l])
        qc, kc, vc, slab_c = split_projection(hc @ w_in[l])
        q = apply_axial_rope(q, *rope)
        k = apply_axial_rope(k, *rope)
        att = window_attention_with_context(q, k, v, kc, vc, attn_sink[l])

        st_c = rwkv_streams(slab_c, *rwkv_p)
        sf_c, yf_c = rwkv_direction(zero_state, st_c, 0, not last)
        sb_c, yb_c = rwkv_direction(zero_state, st_c, 1, not last)
        st = rwkv_streams(slab, *rwkv_p)
        _, yf = rwkv_direction(sf_c, st, 0, True)
        _, yb = rwkv_direction(sb_c, st, 1, True)
        rec = rwkv_readout(st, yf, yb, rwkv_r_k[l], rwkv_ln_w[l], rwkv_ln_b[l])
        mix = jnp.concatenate([att, rec], axis=-1) @ w_out[l]

        if not last:
            att_c = context_self_attention(qc, kc, vc, attn_sink[l])
            rec_c = rwkv_readout(st_c, yf_c, yb_c, rwkv_r_k[l], rwkv_ln_w[l], rwkv_ln_b[l])
            mix_c = jnp.concatenate([att_c, rec_c], axis=-1) @ w_out[l]
            ctx = ctx + cgt1 * rms_norm(mix_c, g_post_mix[l])
            ff_c = squared_relu_mlp(modulate(ctx, g_pre_mlp[l], csh2, csc2), w_mlp_in[l], w_mlp_out[l])
            ctx = ctx + cgt2 * rms_norm(ff_c, g_post_mlp[l])

        x = x + gt1 * rms_norm(mix, g_post_mix[l])
        ff = squared_relu_mlp(modulate(x, g_pre_mlp[l], sh2, sc2), w_mlp_in[l], w_mlp_out[l])
        x = x + gt2 * rms_norm(ff, g_post_mlp[l])
    return x


_drawn_inputs = setup_inputs


def setup_inputs(seed=0):
    import zlib

    import numpy as np

    out = dict(_drawn_inputs(seed))
    spreads = {}
    factors = {'b_ada': 3.135,
     'g_pre_mix': 3.761,
     'g_post_mix': 4.946,
     'g_pre_mlp': 19.216,
     'g_post_mlp': 60.556,
     'attn_sink': 8.0,
     'rwkv_ln_w': 113.61,
     'rwkv_ln_b': 200.0,
     'rwkv_k_k': 4.992}
    for name, (base, spread) in spreads.items():
        noise = np.random.default_rng([zlib.crc32(name.encode()), seed]).standard_normal(out[name].shape)
        drawn = base * np.exp(spread * noise) if base else spread * noise
        out[name] = jnp.asarray(drawn.astype(out[name].dtype))
    for name, factor in factors.items():
        out[name] = (out[name] * factor).astype(out[name].dtype)
    return out
```

```python
from contextlib import ExitStack

import numpy as np

import concourse.bass as bass
from concourse import mybir

F32 = mybir.dt.float32
F32R = mybir.dt.float32r
ALU = mybir.AluOpType
ACT = mybir.ActivationFunctionType
AX = mybir.AxisListType

P = 128
D = 2048
KT = D // P
SEQ, CTX = 256, 256
TOK = CTX + SEQ
NQ, NKV, HD = 8, 2, 128
GQ = NQ // NKV
ATT_IN = NQ * HD + 2 * NKV * HD
N_ADA = 6 * D // P
SLAB = 27
T_R, T_K, T_V, T_W, T_A, T_G = 0, 8, 16, 24, 25, 26
FT = 8
L = 64
NCH = TOK // L
HC = NCH // 2
LEVELS = 5
F_FF = 4 * D // P
SLOT = 2048
EPS, GN_EPS = 1e-6, 64e-5
DECAY = float(np.exp(-0.5))
NEG = -1e30

P_MUP, P_MUN, P_FT = 0, 27, 54
N_PRM = P_FT + 9 * FT
C_KK, C_KA, C_RK, C_LNW, C_LNB, C_W0, C_A0 = 0, 1, 2, 3, 4, 5, 7
V_C, V_CC, V_GMIX, V_GMLP = 0, 16, 32, 48
M_SH1, M_SC1, M_GT1, M_SH2, M_SC2, M_GT2 = (16 * k for k in range(6))


def shape_constants():
    f = np.float32
    row = np.arange(P)
    head, t = row // L, row % L
    same = head[:, None] == head[None, :]
    ident = np.eye(P, dtype=f)
    ones_bd = same.astype(f)
    strict, incl, lv1, lvt, rst = [], [], [], [], []
    for d in range(2):
        s = t if d == 0 else L - 1 - t
        strict.append((same & (s[:, None] < s[None, :])).astype(f))
        s64 = s[:L]
        incl.append((s[:, None] <= s64[None, :]).astype(f))
        early, late = s[:, None], s[None, :]
        lv1.append((same & (early // 2 == late // 2) & (early < late)).astype(f))
        for level in range(LEVELS):
            b = 2 ** (level + 1)
            later, earlier = s[:, None], s[None, :]
            lvt.append((same & (later // (2 * b) == earlier // (2 * b))
                        & (later // b > earlier // b)).astype(f))
        r = np.ones(TOK, f)
        r[(0 if d == 0 else L - 1)::L] = 0
        rst.append(np.broadcast_to(r, (P, TOK)))
    rec = np.concatenate([ident, ones_bd, *strict, *incl, *lv1, *lvt, *rst], axis=1).astype(f)
    q, k = np.arange(P)[:, None], np.arange(SEQ)[None, :]
    att = np.zeros((P, 2, TOK), f)
    for qt in range(2):
        att[:, qt, CTX:] = np.where(np.abs(k - (q + qt * P)) <= 128, 0.0, NEG)
    n = HD // 4
    inv = (f(10000.0) ** (-np.arange(n, dtype=f) / f(n))).astype(f)
    pos = np.arange(SEQ)
    ar = (pos // 64).astype(f)[:, None] * inv[None]
    ac = (pos % 64).astype(f)[:, None] * inv[None]
    cos = np.concatenate([np.cos(ar), np.cos(ar), np.cos(ac), np.cos(ac)], axis=1)
    sin = np.concatenate([-np.sin(ar), np.sin(ar), -np.sin(ac), np.sin(ac)], axis=1)
    rope = np.stack([cos, sin], axis=1).reshape(2, P, 2, HD).transpose(1, 0, 2, 3)
    attn = np.concatenate([att.reshape(P, -1), rope.reshape(P, -1)], axis=1).astype(f)
    return np.ascontiguousarray(rec), np.ascontiguousarray(attn)


class Chain:

    def __init__(self, eng, sem):
        self.eng, self.sem, self.base, self.n = eng, sem, 0, 0

    def link(self, ins):
        ins.then_inc(self.sem, 1)
        self.n += 1
        self.eng.wait_ge(self.sem, self.base + self.n)

    def enter(self, i, per):
        self.outer, self.per, self.n0 = self.base, per, self.n
        self.base = self.outer + self.n + i * per
        self.n = 0

    def leave(self, turns):
        assert self.n == self.per, (self.n, self.per)
        self.base, self.n = self.outer + self.n0 + turns * self.per, 0


def build_program(nc, x, c, ctx_tok, c_ctx, w_ada, b_ada, g_pre_mix, g_post_mix, g_pre_mlp, g_post_mlp,
                  w_in, attn_sink, mu_prev, mu_next, w0, w2, a0, a2, g2, k_k, k_a, r_k, ln_w, ln_b,
                  w_out, w_mlp_in, w_mlp_out, rec_const, att_const, out):
    stack = ExitStack()
    with stack:
        sem = lambda name: stack.enter_context(nc.semaphore(name))
        PS = [stack.enter_context(nc.psum_tensor(f"bank{b}", [P, 512], F32)) for b in range(8)]

        end = [16512]

        def place(name, shape, dtype=F32, offset=None):
            size = 4 * int(np.prod(shape[1:]))
            size = (size + 31) // 32 * 32
            if offset is None:
                offset = end[0]
                end[0] += size
            assert offset + size <= nc.sbuf_usable_end, (name, offset, size)
            return nc.alloc_sbuf_tensor_at(name, shape, dtype, offset=offset)

        class Region:

            def __init__(self, offset, size):
                self.at, self.end = offset, offset + size

            def place(self, name, shape, dtype=F32):
                size = (4 * int(np.prod(shape[1:])) + 31) // 32 * 32
                assert self.at + size <= self.end, (name, self.at, size, self.end)
                t = nc.alloc_sbuf_tensor_at(name, shape, dtype, offset=self.at)
                self.at += size
                return t

        rec = place("rec", [P, rec_const.shape[1]])
        at = [0]

        def cols(n):
            at[0] += n
            return rec[:, at[0] - n:at[0]]

        ident, ones_bd = cols(P), cols(P)
        strict = [cols(P) for _ in range(2)]
        incl = [cols(L) for _ in range(2)]
        lv1 = [cols(P) for _ in range(2)]
        lvt = [[cols(P) for _ in range(LEVELS)] for _ in range(2)]
        rst = [cols(TOK) for _ in range(2)]
        prm = place("prm", [P, N_PRM])
        mu0 = place("mu0", [P, SLAB])
        vec = place("vec", [P, 64])
        bada = place("bada", [P, N_ADA])
        modc = place("modc", [P, N_ADA, 2])
        silc = place("silc", [P, KT, 2])
        amod = place("amod", [P, 2, KT])
        amod2 = place("amod2", [P, KT])
        stat = place("stat", [P, 32])
        sink = place("sink", [P, NQ])
        raw = [place(f"raw{s}", [P, SLOT]) for s in range(2)]
        ring_hl = end[0]
        whi = [place(f"whi{s}", [P, SLOT], F32R) for s in range(2)]
        wlo = [place(f"wlo{s}", [P, SLOT], F32R) for s in range(2)]
        reg_a = end[0]
        SZ_A, SZ_B = 64 * 1024, 45 * 1024 + 64
        reg_b = reg_a + SZ_A
        reg_c = reg_b + SZ_B
        SZ_C = nc.sbuf_usable_end - reg_c
        ra = Region(reg_a, SZ_A)
        hth = ra.place("hth", [P, KT, TOK], F32R)
        htl = ra.place("htl", [P, KT, TOK], F32R)
        rb = Region(reg_b, SZ_B)
        s_r = rb.place("s_r", [P, FT, SEQ])
        s_kv = rb.place("s_kv", [P, 2 * FT, TOK])
        s_w = rb.place("s_w", [P, TOK])
        s_a = rb.place("s_a", [P, TOK])
        s_g = rb.place("s_g", [P, SEQ])
        rc = Region(reg_c, SZ_C)
        qtk = rc.place("qtk", [P, 2, NQ * HD])
        ktk = rc.place("ktk", [P, 4, NKV * HD])
        vtk = rc.place("vtk", [P, 4, NKV * HD])
        ktr = rc.place("ktr", [P, NKV, TOK])
        att_c = rc.place("att_c", [P, 2 * TOK + 2 * 2 * HD])
        amask = att_c[:, 0:2 * TOK].rearrange("p (a n) -> p a n", a=2)
        rope = att_c[:, 2 * TOK:].rearrange("p (t a n) -> p t a n", t=2, a=2)
        xa = Region(reg_b, SZ_B)
        xs = xa.place("xs", [P, 4, D])
        prow = xa.place("prow", [P, 3, P])
        xb = Region(reg_a, SZ_A)
        modrow = xb.place("modrow", [2, 4096])
        junk = xb.place("junk", [P, D])
        xc = Region(reg_c, SZ_C)
        hmod = xc.place("hmod", [P, 2, TOK])
        rr = Region(reg_b, SZ_B)
        rot1 = rr.place("rot1", [P, 512])
        rot2 = rr.place("rot2", [P, 512])
        mixt = nc.alloc_sbuf_tensor_at("mixt", [P, KT, SEQ], F32, offset=reg_a)
        ta = Region(reg_a + 16 * 1024, SZ_A - 16 * 1024)
        qh = ta.place("qh", [P, 2, HD])
        qT = ta.place("qT", [P, 2, P])
        sc = ta.place("sc", [P, 2, TOK])
        pT = ta.place("pT", [P, 2, TOK])
        ast = ta.place("ast", [P, 16])
        ga = Region(reg_a + 16 * 1024, SZ_A - 16 * 1024)
        gc = Region(reg_c, SZ_C)
        gh = Region(ring_hl, 32 * 1024)
        bda = [ga.place(f"bda{d}", [P, NCH, P]) for d in range(2)]
        bdk = [ga.place(f"bdk{d}", [P, NCH, P]) for d in range(2)]
        bdb = [ga.place(f"bdb{d}", [P, NCH, P]) for d in range(2)]
        dd = [ga.place(f"dd{d}", [P, NCH, P]) for d in range(2)]
        zz = [ga.place(f"zz{d}", [P, NCH, P]) for d in range(2)]
        aak = [ga.place(f"aak{d}", [P, NCH, P]) for d in range(2)]
        bkt = [gh.place(f"bkt{d}", [P, NCH, P]) for d in range(2)]
        bbt = [gh.place(f"bbt{d}", [P, NCH, P]) for d in range(2)]
        vbd = gh.place("vbd", [P, NCH, P])
        vt = gh.place("vt", [P, NCH, P])
        ar = [gh.place("ar0", [P, NCH, P]), None]
        ar[1] = gc.place("ar1", [P, NCH, P])
        arb = [gc.place(f"arb{d}", [P, HC, L]) for d in range(2)]
        ark = [gc.place(f"ark{d}", [P, HC, L]) for d in range(2)]
        ep = [gc.place(f"ep{d}", [P, NCH, L + 1]) for d in range(2)]
        kk = gc.place("kk", [P, TOK])
        sgt = gc.place("sgt", [P, TOK])
        sat = gc.place("sat", [P, TOK])
        en = gc.place("en", [P, TOK])
        cum = gc.place("cum", [P, TOK])
        kd = gc.place("kd", [P, TOK])
        gg = gc.place("gg", [P, SEQ])
        kb = gc.place("kb", [P, SEQ])
        S_ = [gc.place(f"S{d}", [P, P]) for d in range(2)]
        U_ = [gc.place(f"U{d}", [P, P]) for d in range(2)]
        P_ = [gh.place(f"P{d}", [P, P]) for d in range(2)]
        yb = gc.place("yb", [P, 2, SEQ])
        pc = gc.place("pc", [P, 10])
        wsl = gc.place("wsl", [P, 3, P])
        ffh = nc.alloc_sbuf_tensor_at("ffh", [P, F_FF, SEQ], F32, offset=reg_a)
        mm_ = nc.alloc_sbuf_tensor_at("mm_", [P, 2, D], F32, offset=reg_a + 16 * 1024)
        gpost = nc.alloc_sbuf_tensor_at("gpost", [P, 2, D], F32, offset=reg_a + 32 * 1024)
        diag = nc.alloc_sbuf_tensor_at("diag", [P, 2, P], F32, offset=reg_a + 48 * 1024)
        ones = nc.alloc_sbuf_tensor_at("ones", [P, P], F32, offset=reg_a + 50 * 1024)
        hm2 = nc.alloc_sbuf_tensor_at("hm2", [P, 2, SEQ], F32, offset=reg_a + 52 * 1024)
        er = Region(reg_b, nc.sbuf_usable_end - reg_b)
        h2h = er.place("h2h", [P, KT, SEQ], F32R)
        h2l = er.place("h2l", [P, KT, SEQ], F32R)
        gates = er.place("gates", [P, 2, D])
        x1 = er.place("x1", [P, 2, D])
        relu = er.place("relu", [P, 2, SEQ])
        fsh = [er.place(f"fsh{s}", [P, SEQ], F32R) for s in range(2)]
        fsl = [er.place(f"fsl{s}", [P, SEQ], F32R) for s in range(2)]
        junk2 = nc.alloc_sbuf_tensor_at("junk2", [P, D], F32, offset=reg_a + 54 * 1024)
        ffo = nc.alloc_sbuf_tensor_at("ffo", [P, 2, D], F32, offset=reg_a)
        junk3 = nc.alloc_sbuf_tensor_at("junk3", [P, D], F32, offset=reg_a + 16 * 1024)
        fin = nc.alloc_sbuf_tensor_at("fin", [P, 2, D], F32, offset=reg_b)

        s_const, s_rows, s_x = sem("constants_landed"), sem("param_rows_landed"), sem("tokens_landed")
        s_attc, s_sink = sem("att_constants_landed"), sem("sink_landed")
        raw_landed = [sem(f"raw{s}_landed") for s in range(2)]
        ada_used = sem("ada_slot_used")
        prm_T, prm_done = sem("params_transposed"), sem("params_in_columns")
        silu_sig, silu_done = sem("silu_sigmoid"), sem("silu_ready")
        row_out, row_T, mod_done = sem("mod_row_out"), sem("mod_transposed"), sem("mod_in_columns")
        ss_done, sq_done, xhat_done = sem("squares_summed"), sem("root_done"), sem("tokens_normed")
        xT_done, hm_done, hh_done, hl_done = sem("tokens_transposed"), sem("modulated"), sem("h_high"), sem("h_low")
        whi_ready, wlo_ready, w_used = sem("weights_high"), sem("weights_low"), sem("weights_used")
        ctx_out, rot_out = sem("context_kv_out"), sem("latent_qkv_out")
        kT_done, kT_out = sem("k_transposed"), sem("kT_out")
        slab_base, slab_done = sem("slab_base"), sem("slab_shifted")
        dve_s, act_s, pool_s = sem("vector_chain"), sem("scalar_chain"), sem("gpsimd_chain")
        a_qh, a_qT, a_qTo, a_sc, a_lg = sem("q_head_copied"), sem("q_transposed"), sem("qT_out"), sem("scores_done"), sem("negmax_ready")
        a_ex, a_pr, a_pT, a_pTo, a_o, a_oo = sem("exps_done"), sem("probs_ready"), sem("probs_transposed"), sem("pT_out"), sem("att_product"), sem("att_out")
        g_w, g_pc, g_kq, g_nr, g_rt, g_kk = sem("lora_landed"), sem("tile_params"), sem("k_squares"), sem("k_norms"), sem("k_roots"), sem("kk_ready")
        g_lo, g_sg, g_cum, g_ex, g_bd, g_ba, g_gg = (sem("lora_products"), sem("sigmoids"), sem("decay_sums"), sem("decay_exps"),
                                                     sem("operands_ready"), sem("block_a_ready"), sem("gate_out"))
        g_vb, g_vT, g_vo = sem("v_blocks"), sem("v_transposed"), sem("v_out")
        g_am, g_ae, g_tr, g_to, g_z1 = sem("chunk_products"), sem("chunk_masked"), sem("tilde_transposed"), sem("tilde_out"), sem("z_started")
        g_xt, g_xo, g_tm, g_te, g_zm, g_ze = (sem("x_transposed"), sem("x_out"), sem("t_product"), sem("t_masked"),
                                              sem("z_product"), sem("z_added"))
        c_s0, c_p, c_po, c_u, c_uo, c_s, c_so = (sem("state_zero"), sem("p_product"), sem("p_out"), sem("u_product"),
                                                 sem("u_out"), sem("state_product"), sem("state_out"))
        r_yb, r_mu, r_sq, r_var, r_vt, r_sd, ft_done = (sem("y_and_bonus"), sem("y_means"), sem("y_squares"), sem("y_variances"),
                                                        sem("y_var_eps"), sem("y_roots"), sem("tile_done"))
        ft_init = sem("zero_blocks")
        t_lora = sem("lora_inputs")
        d_mh, d_ml = sem("mix_high"), sem("mix_low")
        d_out, d_ss, d_rt, d_xh = sem("out_evacuated"), sem("out_squares"), sem("out_roots"), sem("x1_normed")
        d_gp, d_dg, d_gm, d_gt, d_x, d_x1 = sem("gpost_landed"), sem("gate_diag"), sem("gate_rows"), sem("gate_ready"), sem("x_again"), sem("x1_ready")
        d_tr, d_hm, d_hh, d_hl = sem("x1_transposed"), sem("x1_modulated"), sem("h2_high"), sem("h2_low")
        e_re, e_ff = sem("mlp_relu"), sem("mlp_squared")
        f_fh, f_fl = sem("ff_high"), sem("ff_low")
        o_out, o_ss, o_rt, o_fin, o_st = (sem("mlp_evacuated"), sem("mlp_squares"), sem("mlp_root"), sem("result_ready"),
                                          sem("result_stored"))
        a_rc = sem("sums_inverted")
        pe_go, pool_go = sem("tensor_goes_on"), sem("gpsimd_goes_on")

        x_var, c_y, r_yc = sem("token_variances"), sem("y_product"), sem("y_centred")

        def chunk(d, n):
            return n if d == 0 else HC * (n // HC) + HC - 1 - n % HC

        DVE_LINKS = 20
        STREAMS = [(d, g) for d in range(2) for g in range(2)]
        halves = [slice(L * h, L * h + L) for h in range(2)]

        block = stack.enter_context(nc.Block())

        M_ATT, M_SLAB, M_OUT, M_IN, M_MO = 0, KT, KT + SLAB, 2 * KT + SLAB, 2 * KT + SLAB + F_FF
        M_END = M_MO + F_FF
        ADA_USES = 3 * KT * 2

        def landed(m0, i):
            return m0 % 2, 16 * (ADA_USES // 2 + m0 // 2 + 1 + i)

        SLAB_ORDER = [T_G, T_W, T_A]
        SLAB_LOOPS = [(3, FT // 2, T_R), (3 + FT, FT, T_K)]

        rk_row = r_k.rearrange("a h n -> a (h n)")
        w_in2 = w_in[0]
        v_slab = w_in2[:, ATT_IN:].rearrange("(k p) f -> p k f", p=P)
        v_mlp = w_mlp_in[0].rearrange("(k p) f -> p k f", p=P)

        @block.sync
        def _(sp):
            with sp.Fori(0, 3) as ps:
                for kt in range(KT):
                    for h in range(2):
                        sp.wait_ge(ada_used, ps * (2 * KT) + (2 * kt + h + 1))
                        sp.dma_start(raw[h][:, :], w_ada[0, kt * P:(kt + 1) * P, bass.ds(ps * 4096 + h * SLOT, SLOT)]
                                     ).then_inc(raw_landed[h], 16)

            def slot_free(m, i=0):
                if isinstance(i, int) and m < 2:
                    sp.wait_ge(ada_used, ADA_USES + 2 - 1 + m)
                else:
                    sp.wait_ge(wlo_ready, 2 * i + (m - 1))

            for kt in range(KT):
                slot_free(kt)
                sp.dma_start(raw[kt % 2][:, 0:ATT_IN], w_in2[kt * P:(kt + 1) * P, 0:ATT_IN]).then_inc(raw_landed[kt % 2], 16)

            def load_tile(m, i, view, col):
                slot_free(m, i)
                sp.dma_start(raw[m % 2][:, :].rearrange("p (k f) -> p k f", k=KT), view[:, :, bass.ds(col, P)]
                             ).then_inc(raw_landed[m % 2], 16)

            for q, tile in enumerate(SLAB_ORDER):
                load_tile(M_SLAB + q, 0, v_slab, tile * P)
            for q, turns, tile in SLAB_LOOPS:
                with sp.Fori(0, turns) as i:
                    for j in range(2):
                        load_tile(M_SLAB + q + j, i, v_slab, i * (2 * P) + (tile + j) * P)

            def load_rows(m0, n, w):
                with sp.Fori(0, n // 2) as i:
                    for j in range(2):
                        slot_free(m0 + j, i)
                        sp.dma_start(raw[(m0 + j) % 2][:, :], w[bass.ds(i * (2 * P) + j * P, P), :]
                                     ).then_inc(raw_landed[(m0 + j) % 2], 16)

            load_rows(M_OUT, KT, w_out[0])
            with sp.Fori(0, F_FF // 2) as i:
                for j in range(2):
                    load_tile(M_IN + j, i, v_mlp, i * (2 * P) + j * P)
            load_rows(M_MO, F_FF, w_mlp_out[0])
            for t in range(2):
                sp.wait_ge(o_fin, t + 1)
                sp.dma_start(out[0, t * P:(t + 1) * P, :], fin[:, t, :]).then_inc(o_st, 16)
            sp.wait_ge(o_st, 32)

        @block.gpsimd
        def _(pool):
            ch = Chain(pool, pool_s)
            pool.wait_ge(rot_out, 1)
            pool.wait_ge(w_used, M_OUT)
            with pool.Fori(0, NQ) as h:
                pool.wait_ge(a_qT, h + 1)
                pool.sem_inc(pool_go, 1)
                pool.tensor_copy(qh[:, :, :], qtk[:, :, bass.ds(h * HD, HD)]).then_inc(a_qh, 1)
            pool.wait_ge(a_oo, NQ + 1)
            for t in (*bda, *bdk, *bdb, vbd):
                pool.memset(t[:, :, :], 0.0).then_inc(ft_init, 1)
            pool.wait_ge(ft_init, 7)
            with pool.Fori(0, FT) as i:
                pool.wait_ge(ft_done, i + 1)
                for k, w in enumerate((w2, a2)):
                    pool.dma_start(wsl[:, k, :], w[0].rearrange("d l r -> (d l) r")[:, bass.ds(i * P, P)]).then_inc(g_w, 16)
                pool.dma_start(wsl[:, 2, :], g2[0][:, bass.ds(i * P, P)]).then_inc(g_w, 16)
                for h in range(2):
                    hs = slice(L * h, L * h + L)
                    pool.tensor_copy(vbd[hs, :, L * h:L * h + L],
                                     s_kv[hs, bass.ds(i + FT, 1), :].rearrange("p a (c t) -> p (a c) t", t=L)).then_inc(g_vb, 1)
                for d in range(2):
                    pool.wait_ge(g_bd, 2 * i + d + 1)
                    pool.sem_inc(pool_go, 1)
                    for h in range(2):
                        hs = slice(L * h, L * h + L)
                        pool.tensor_copy(bda[d][hs, :, L * h:L * h + L], ar[d][hs, :, 0:L]).then_inc(g_ba, 1)
            pool.sem_inc(e_ff, 2)
            with pool.Fori(0, F_FF // 2) as i:
                for j in range(2):
                    pool.wait_ge(e_re, 2 * i + j + 3)
                    pool.tensor_tensor(ffh[:, bass.ds(2 * i + j, 1), :], relu[:, j:j + 1, :], relu[:, j:j + 1, :],
                                       ALU.mult).then_inc(e_ff, 1)

        @block.scalar
        def _(act):
            A = nc.scalar.activation
            act.dma_start(rec[:, :], rec_const).then_inc(s_const, 16)
            rows = [(mu_prev, P_MUP, SLAB), (mu_next, P_MUN, SLAB), (k_k, P_FT, FT), (k_a, P_FT + FT, FT),
                    (rk_row, P_FT + 2 * FT, FT), (ln_w, P_FT + 3 * FT, FT), (ln_b, P_FT + 4 * FT, FT)]
            for w, r, n in rows:
                act.dma_start(prow[r:r + n, 0, :], w[0].rearrange("(k p) -> k p", p=P)).then_inc(s_rows, 16)
            for w, r in ((w0, P_FT + 5 * FT), (a0, P_FT + 7 * FT)):
                act.dma_start(prow[r:r + 2 * FT, 0, :], w[0].rearrange("d (k p) -> (d k) p", p=P)).then_inc(s_rows, 16)
            for w, r in ((c[0], V_C), (c_ctx, V_CC), (g_pre_mix[0], V_GMIX), (g_pre_mlp[0], V_GMLP)):
                act.dma_start(prow[r:r + KT, 1, :], w.rearrange("(k p) -> k p", p=P)).then_inc(s_rows, 16)
            act.dma_start(prow[0:N_ADA, 2, :], b_ada[0].rearrange("(k p) -> k p", p=P)).then_inc(s_rows, 16)
            for t in range(2):
                act.dma_start(xs[:, t, :], ctx_tok[0, t * P:(t + 1) * P, :]).then_inc(s_x, 16)
            for t in range(2):
                act.dma_start(xs[:, 2 + t, :], x[0, t * P:(t + 1) * P, :]).then_inc(s_x, 16)
            act.dma_start(sink[:, :], attn_sink.to_broadcast([P, NQ])).then_inc(s_sink, 16)
            act.sem_inc(row_out, 1)
            act.sem_inc(a_oo, 1)
            act.sem_inc(e_re, 2)
            act.wait_ge(prm_done, 3)
            A(stat[:, 0:32], vec[:, 0:32], ACT.Sigmoid).then_inc(silu_sig, 1)
            act.wait_ge(s_x, 64)
            act.wait_ge(silu_done, 1)
            for t in range(4):
                if t:
                    act.wait_ge(ss_done, t)
                A(junk[:, :], xs[:, t, :], ACT.Square, accum_out=stat[:, t:t + 1]).then_inc(ss_done, 1)
            act.wait_ge(x_var, 1)
            A(stat[:, 8:12], stat[:, 4:8], ACT.Sqrt).then_inc(sq_done, 1)
            with act.Fori(0, 3) as ps:
                act.wait_ge(ada_used, ps * (2 * KT) + (2 * KT + 2))
                act.wait_ge(row_T, ps + 1)
                for b in range(8):
                    A(modrow[:, b * 512:(b + 1) * 512], PS[b][0:2, :], ACT.Copy).then_inc(row_out, 1)
            for kt in range(KT):
                act.wait_ge(hm_done, kt + 1)
                if kt == 0:
                    act.wait_ge(row_T, 4)
                A(hth[:, kt, :], hmod[:, kt % 2, :], ACT.Copy).then_inc(hh_done, 1)

            def high(m, i=0, n=SLOT):
                s, count = landed(m, i)
                act.wait_ge(raw_landed[s], count)
                if not (isinstance(i, int) and m < 2):
                    act.wait_ge(w_used, 2 * i + m - 1)
                A(whi[s][:, 0:n], raw[s][:, 0:n], ACT.Copy).then_inc(whi_ready, 1)

            for m in range(KT):
                high(m, 0, ATT_IN)
            high(M_SLAB)
            act.wait_ge(hl_done, KT)
            act.dma_start(att_c[:, :], att_const).then_inc(s_attc, 16)
            act.wait_ge(w_used, KT)
            for t in range(2):
                A(ktk[:, t, :], PS[t][:, 0:256], ACT.Copy).then_inc(ctx_out, 1)
                A(vtk[:, t, :], PS[t][:, 256:512], ACT.Copy).then_inc(ctx_out, 1)

            def base(q, i, dst, mu, last=False):
                if not last:
                    high(M_SLAB + q + 1, i)
                act.wait_ge(w_used, 2 * i + (M_SLAB + q + 1))
                if q == 0:
                    act.wait_ge(rot_out, 1)
                n = dst.free_size()
                A(dst, PS[q % 2][:, 0:n], ACT.Copy, scale=mu).then_inc(slab_base, 1)

            for q, (tile, dst) in enumerate(zip(SLAB_ORDER, (s_g, s_w, s_a))):
                base(q, 0, dst[:, :], mu0[:, tile:tile + 1])
            q0, turns, _ = SLAB_LOOPS[0]
            with act.Fori(0, turns) as i:
                for j in range(2):
                    base(q0 + j, i, s_r[:, bass.ds(2 * i + j, 1), :].rearrange("p a n -> p (a n)"),
                         mu0[:, bass.ds(2 * i + T_R + j, 1)])
            q0, turns, _ = SLAB_LOOPS[1]
            kv = lambda e: s_kv[:, bass.ds(e, 1), :].rearrange("p a n -> p (a n)")
            with act.Fori(0, turns - 1) as i:
                for j in range(2):
                    base(q0 + j, i, kv(2 * i + j), mu0[:, bass.ds(2 * i + T_K + j, 1)])
            for j in range(2):
                e = 2 * (turns - 1) + j
                base(q0 + j + 2 * (turns - 1), 0, s_kv[:, e, :], mu0[:, T_K + e:T_K + e + 1], last=j == 1)
            for g in range(NKV):
                act.wait_ge(kT_done, g + 1)
                A(ktr[:, g, :], PS[g][:, :], ACT.Copy).then_inc(kT_out, 1)
            act.wait_ge(s_sink, 16)
            with act.Fori(0, NQ) as h:
                act.wait_ge(a_qT, h + 2)
                A(qT[:, :, :].rearrange("p a n -> p (a n)"), PS[2][:, 0:256], ACT.Copy, scale=float(HD) ** -0.5).then_inc(a_qTo, 1)
                act.wait_ge(a_lg, h + 1)
                for t in range(2):
                    A(sc[:, t, :], sc[:, t, :], ACT.Exp, bias=ast[:, 2 + t:3 + t], accum_out=ast[:, 4 + t:5 + t]).then_inc(a_ex, 1)
                    A(ast[:, 6 + t:7 + t], sink[:, bass.ds(h, 1)], ACT.Exp, bias=ast[:, 2 + t:3 + t]).then_inc(a_ex, 1)
                for t in range(2):
                    act.wait_ge(a_pT, 2 * h + t + 1)
                    A(pT[:, t, :], PS[5 + t][:, :], ACT.Copy).then_inc(a_pTo, 1)
                act.wait_ge(a_o, h + 1)
                A(mixt[:, bass.ds(h, 1), :].rearrange("p a n -> p (a n)"), PS[7][:, 0:SEQ], ACT.Copy).then_inc(a_oo, 1)
            act.wait_ge(slab_done, SLAB)
            A(s_w[:, :], s_w[:, :], ACT.Tanh).then_inc(t_lora, 1)
            A(s_g[:, :], s_g[:, :], ACT.Sigmoid).then_inc(t_lora, 1)
            with act.Fori(0, FT) as i:
                act.wait_ge(ft_done, i + 1)
                act.wait_ge(g_pc, i + 1)
                A(en[:, :], s_kv[:, bass.ds(i, 1), :].rearrange("p a n -> p (a n)"), ACT.Square, scale=pc[:, C_KK:C_KK + 1]).then_inc(g_kq, 1)
                act.wait_ge(g_nr, i + 1)
                A(sgt[:, :], PS[0][:, :], ACT.Sqrt).then_inc(g_rt, 1)
                act.wait_ge(g_lo, 5 * i + 5)
                A(gg[:, :], PS[5][:, 0:SEQ], ACT.Copy).then_inc(g_gg, 1)
                for d in range(2):
                    if d == 0:
                        act.wait_ge(g_kk, i + 1)
                    else:
                        act.wait_ge(g_bd, 2 * i + 1)
                    A(sgt[:, :], PS[1 + d][:, :], ACT.Sigmoid, bias=pc[:, C_W0 + d:C_W0 + d + 1]).then_inc(g_sg, 1)
                    A(sat[:, :], PS[3 + d][:, :], ACT.Sigmoid, bias=pc[:, C_A0 + d:C_A0 + d + 1]).then_inc(g_sg, 1)
                    act.wait_ge(g_cum, 2 * i + d + 1)
                    o = 1 - d
                    cum3 = cum[:, :].rearrange("p (c t) -> p c t", t=L)
                    A(ep[d][:, :, o:o + L], cum3, ACT.Exp, scale=-DECAY).then_inc(g_ex, 1)
                    A(en[:, :], cum[:, :], ACT.Exp, scale=DECAY).then_inc(g_ex, 1)
                for g in range(2):
                    act.wait_ge(g_vT, 2 * i + g + 1)
                    A(vt[:, HC * g:HC * g + HC, :], PS[6 + g][:, :], ACT.Copy).then_inc(g_vo, 1)
                for s, (d, g) in enumerate(STREAMS):
                    cs = slice(HC * g, HC * g + HC)
                    for k, (dst, bank) in enumerate(((bkt[d], 4 + s), (bbt[d], s))):
                        act.wait_ge(g_tr, 8 * i + 2 * s + k + 1)
                        A(dst[:, cs, :], PS[bank][:, :], ACT.Copy).then_inc(g_to, 1)
                for l in range(LEVELS):
                    for s, (d, g) in enumerate(STREAMS):
                        act.wait_ge(g_xt, 4 * LEVELS * i + 4 * l + s + 1)
                        A(bdk[d][:, HC * g:HC * g + HC, :], PS[4 + s][:, :], ACT.Copy).then_inc(g_xo, 1)
                for n in range(NCH):
                    for d in range(2):
                        act.wait_ge(c_p, 2 * NCH * i + 2 * n + d + 1)
                        A(P_[d][:, :], PS[3 * d][:, 0:P], ACT.Copy).then_inc(c_po, 1)
                    for d in range(2):
                        if n == NCH - 1:
                            continue
                        last = L if d == 0 else 0
                        ck = chunk(d, n)
                        act.wait_ge(c_s, 2 * (NCH - 1) * i + 2 * n + d + 1)
                        A(S_[d][:, :], PS[3 * d + 2][:, 0:P], ACT.Copy, scale=ep[d][:, ck, last:last + 1]).then_inc(c_so, 1)
                act.wait_ge(r_yc, i + 1)
                A(kd[:, 0:SEQ], yb[:, 0, :], ACT.Square).then_inc(r_sq, 1)
                act.wait_ge(r_vt, i + 1)
                A(kd[:, 0:SEQ], kd[:, SEQ:TOK], ACT.Sqrt).then_inc(r_sd, 1)

            act.wait_ge(ft_done, FT + 1)
            for t in range(2):
                act.dma_start(gpost[:, t, :], (g_post_mix, g_post_mlp)[t].to_broadcast([P, D])).then_inc(d_gp, 16)
            for t in range(2):
                act.dma_start(x1[:, t, :], x[0, t * P:(t + 1) * P, :]).then_inc(d_x, 16)
            for t in range(4):
                A(h2h[:, 4 * t:4 * t + 4, :], mixt[:, 4 * t:4 * t + 4, :], ACT.Copy).then_inc(d_mh, 1)
            with act.Fori(0, KT // 2) as i:
                for j in range(2):
                    high(M_OUT + j, i)
            act.wait_ge(w_used, M_IN)
            for t in range(2):
                for b in range(4):
                    A(mm_[:, t, b * 512:(b + 1) * 512], PS[4 * t + b][:, :], ACT.Copy).then_inc(d_out, 1)
            act.wait_ge(d_out, 8)
            for t in range(2):
                A(junk2[:, :], mm_[:, t, :], ACT.Square, accum_out=stat[:, 12 + t:13 + t]).then_inc(d_ss, 1)
                act.wait_ge(d_ss, t + 1)
            act.wait_ge(d_rt, 1)
            A(stat[:, 16:18], stat[:, 14:16], ACT.Sqrt).then_inc(d_ss, 1)
            for t in range(2):
                act.wait_ge(d_x1, t + 1)
                A(junk2[:, :], x1[:, t, :], ACT.Square, accum_out=stat[:, 20 + t:21 + t]).then_inc(d_ss, 1)
                act.wait_ge(d_ss, 4 + t)
            act.wait_ge(d_rt, 2)
            A(stat[:, 24:26], stat[:, 22:24], ACT.Sqrt).then_inc(d_ss, 1)
            for kt in range(KT):
                act.wait_ge(d_hm, kt + 1)
                A(h2h[:, kt, :], hm2[:, kt % 2, :], ACT.Copy).then_inc(d_hh, 1)
            high(M_IN)
            with act.Fori(0, F_FF // 2) as i:
                for j in range(2):
                    high(M_IN + j + 1, i)
                    act.wait_ge(w_used, 2 * i + (M_IN + j + 1))
                    act.wait_ge(e_ff, 2 * i + j + 1)
                    A(relu[:, j, :], PS[j][:, 0:SEQ], ACT.Relu).then_inc(e_re, 1)
            act.wait_ge(e_ff, F_FF + 2)

            def hidden(i, j):
                act.wait_ge(w_used, 2 * i + (M_MO + j - 1))
                A(fsh[j][:, :], ffh[:, bass.ds(2 * i + j, 1), :].rearrange("p a n -> p (a n)"), ACT.Copy).then_inc(f_fh, 1)

            with act.Fori(0, F_FF // 2 - 1) as i:
                for j in range(2):
                    hidden(i, j)
                    high(M_MO + j + 1, i)
            for j in range(2):
                hidden(F_FF // 2 - 1, j)
                if j == 0:
                    high(M_END - 1)
            act.wait_ge(w_used, M_END)
            for t in range(2):
                for b in range(4):
                    A(ffo[:, t, b * 512:(b + 1) * 512], PS[4 * t + b][:, :], ACT.Copy).then_inc(o_out, 1)
                act.wait_ge(o_out, 4 * t + 4)
                A(junk3[:, :], ffo[:, t, :], ACT.Square, accum_out=stat[:, 26 + t:27 + t]).then_inc(o_ss, 1)
                act.wait_ge(o_ss, t + 1)
            act.wait_ge(o_rt, 1)
            A(stat[:, 30:32], stat[:, 28:30], ACT.Sqrt).then_inc(o_ss, 1)

        @block.vector
        def _(dve):
            ch = Chain(dve, dve_s)
            TT, TS, STT = nc.vector.tensor_tensor, nc.vector.tensor_scalar, nc.vector.scalar_tensor_tensor
            dve.sem_inc(mod_done, 1)
            dve.sem_inc(ft_done, 1)
            dve.wait_ge(prm_T, 1)
            nc.vector.tensor_copy(prm[:, :], PS[0][:, 0:N_PRM]).then_inc(prm_done, 1)
            nc.vector.tensor_copy(vec[:, :], PS[0][:, 128:192]).then_inc(prm_done, 1)
            nc.vector.tensor_copy(bada[:, :], PS[0][:, 192:192 + N_ADA]).then_inc(prm_done, 1)
            dve.wait_ge(prm_done, 3)
            ch.link(STT(out=mu0[:, :], in0=prm[:, P_MUP:P_MUP + SLAB], scalar=-1.0, in1=prm[:, P_MUN:P_MUN + SLAB],
                        op0=ALU.mult, op1=ALU.subtract))
            ch.link(TS(mu0[:, :], mu0[:, :], 1.0, None, ALU.add))
            dve.wait_ge(silu_sig, 1)
            TT(silc[:, :, :].rearrange("p k j -> p j k"), vec[:, 0:32].rearrange("p (j k) -> p j k", j=2),
               stat[:, 0:32].rearrange("p (j k) -> p j k", j=2), ALU.mult).then_inc(silu_done, 1)
            dve.wait_ge(ss_done, 4)
            TS(stat[:, 4:8], stat[:, 0:4], 1.0 / D, EPS, ALU.mult, ALU.add).then_inc(x_var, 1)
            dve.wait_ge(sq_done, 1)
            ch.link(nc.vector.reciprocal(stat[:, 12:16], stat[:, 8:12]))
            for t in range(4):
                TS(xs[:, t, :], xs[:, t, :], stat[:, 12 + t:13 + t], None, ALU.mult).then_inc(xhat_done, 1)
            with dve.Fori(0, 3) as ps:
                dve.wait_ge(row_T, ps + 2)
                for j in range(2):
                    TT(modc[:, bass.ds(ps * 32, 32), j], PS[0][:, j:64:2], bada[:, bass.ds(ps * 32, 32)],
                       ALU.add).then_inc(mod_done, 1)
            dve.wait_ge(mod_done, 7)
            for j in range(2):
                ch.link(STT(out=amod[:, j, :], in0=modc[:, M_SC1:M_SC1 + KT, j], scalar=1.0, in1=vec[:, V_GMIX:V_GMIX + KT],
                            op0=ALU.add, op1=ALU.mult))
            ch.link(STT(out=amod2[:, :], in0=modc[:, M_SC2:M_SC2 + KT, 0], scalar=1.0, in1=vec[:, V_GMLP:V_GMLP + KT],
                        op0=ALU.add, op1=ALU.mult))

            def h_low(kt):
                dve.wait_ge(hh_done, kt + 1)
                TT(htl[:, kt, :], hmod[:, kt % 2, :], hth[:, kt, :].bitcast(F32), ALU.subtract).then_inc(hl_done, 1)

            for kt in range(KT):
                dve.wait_ge(xT_done, kt + 1)
                if kt >= 2:
                    dve.wait_ge(hl_done, kt - 1)
                b = PS[1 + kt % 4]
                TS(hmod[:, kt % 2, 0:CTX], b[:, 0:CTX], amod[:, 1, kt:kt + 1], modc[:, M_SH1 + kt, 1:2], ALU.mult, ALU.add)
                TS(hmod[:, kt % 2, CTX:TOK], b[:, CTX:TOK], amod[:, 0, kt:kt + 1], modc[:, M_SH1 + kt, 0:1],
                   ALU.mult, ALU.add).then_inc(hm_done, 1)
                if kt:
                    h_low(kt - 1)
            h_low(KT - 1)

            def low(m, i=0, n=SLOT):
                s = m % 2
                dve.wait_ge(whi_ready, 2 * i + m + 1)
                TT(wlo[s][:, 0:n], raw[s][:, 0:n], whi[s][:, 0:n].bitcast(F32), ALU.subtract).then_inc(wlo_ready, 1)

            for m in range(KT):
                low(m, 0, ATT_IN)
            low(M_SLAB)

            def rotate(dst, src, t, nh):
                n = nh * HD
                cs = rope[:, t, 0, :].unsqueeze(1).to_broadcast([P, nh, HD])
                ch.link(TT(rot1[:, 0:n].rearrange("p (h n) -> p h n", h=nh), src.rearrange("p (h n) -> p h n", h=nh), cs, ALU.mult))
                src4 = src.rearrange("p (h a j n) -> p h a j n", h=nh, a=2, j=2)
                dst4 = rot2[:, 0:n].rearrange("p (h a j n) -> p h a j n", h=nh, a=2, j=2)
                for j in range(2):
                    sn = rope[:, t, 1, :].rearrange("p (a j n) -> p a j n", a=2, j=2)[:, :, j, :]
                    ch.link(TT(dst4[:, :, :, j, :], src4[:, :, :, 1 - j, :],
                               sn.unsqueeze(1).to_broadcast([P, nh, 2, HD // 4]), ALU.mult))
                ch.link(TT(dst, rot1[:, 0:n], rot2[:, 0:n], ALU.add))

            dve.wait_ge(w_used, KT)
            dve.wait_ge(s_attc, 16)
            for t in range(2):
                rotate(ktk[:, 2 + t, :], PS[2 + t][:, 0:256], t, NKV)
                ch.link(nc.vector.tensor_copy(vtk[:, 2 + t, :], PS[2 + t][:, 256:512]))
                for q in range(2):
                    rotate(qtk[:, t, q * 512:(q + 1) * 512], PS[4 + 2 * t + q][:, :], t, 4)
            dve.sem_inc(rot_out, 1)

            def shift(q, i, dst, tile, last=False):
                if not last:
                    low(M_SLAB + q + 1, i)
                dve.wait_ge(slab_base, 2 * i + q + 1)
                n = dst.free_size() // SEQ if dst.free_size() > SEQ else 1
                src = PS[q % 2][:, 0:n * SEQ].rearrange("p (a n) -> p a n", a=n)
                dst = dst.rearrange("p (a n) -> p a n", a=n)
                col = lambda b: prm[:, bass.ds(tile + b, 1)]
                ch.link(STT(out=dst[:, :, 1:SEQ], in0=src[:, :, 0:SEQ - 1], scalar=col(P_MUP), in1=dst[:, :, 1:SEQ],
                            op0=ALU.mult, op1=ALU.add))
                STT(out=dst[:, :, 0:SEQ - 1], in0=src[:, :, 1:SEQ], scalar=col(P_MUN), in1=dst[:, :, 0:SEQ - 1],
                    op0=ALU.mult, op1=ALU.add).then_inc(slab_done, 1)

            flat = lambda t, e: t[:, bass.ds(e, 1), :].rearrange("p a n -> p (a n)")
            for q, (tile, dst) in enumerate(zip(SLAB_ORDER, (s_g, s_w, s_a))):
                shift(q, 0, dst[:, :], tile)
            q0, turns, _ = SLAB_LOOPS[0]
            with dve.Fori(0, turns) as i:
                ch.enter(i, 2)
                for j in range(2):
                    shift(q0 + j, i, flat(s_r, 2 * i + j), 2 * i + T_R + j)
            ch.leave(turns)
            q0, turns, _ = SLAB_LOOPS[1]
            with dve.Fori(0, turns - 1) as i:
                ch.enter(i, 2)
                for j in range(2):
                    shift(q0 + j, i, flat(s_kv, 2 * i + j), 2 * i + T_K + j)
            ch.leave(turns - 1)
            for j in range(2):
                e = 2 * (turns - 1) + j
                shift(q0 + e, 0, s_kv[:, e, :], T_K + e, last=j == 1)

            dve.wait_ge(s_sink, 16)
            with dve.Fori(0, NQ) as h:
                ch.enter(h, 4)
                for t in range(2):
                    dve.wait_ge(a_sc, 2 * h + t + 1)
                    ins = TT(sc[:, t, :], PS[3 + t][:, :], amask[:, t, :], ALU.add)
                ch.link(ins)
                ch.link(nc.vector.tensor_reduce(ast[:, 0:2], sc[:, :, :], AX.X, ALU.max))
                ch.link(TT(ast[:, 12:14], ast[:, 0:2], sink[:, bass.ds(h, 1)].to_broadcast([P, 2]), ALU.max))
                TS(ast[:, 2:4], ast[:, 12:14], -1.0, None, ALU.mult).then_inc(a_lg, 1)
                dve.wait_ge(a_ex, 4 * h + 4)
                ch.link(TT(ast[:, 8:10], ast[:, 4:6], ast[:, 6:8], ALU.add))
                nc.vector.reciprocal(ast[:, 10:12], ast[:, 8:10]).then_inc(a_rc, 1)
                dve.wait_ge(a_rc, h + 1)
                for t in range(2):
                    TS(sc[:, t, :], sc[:, t, :], ast[:, 10 + t:11 + t], None, ALU.mult).then_inc(a_pr, 1)
            ch.leave(NQ)

            dve.wait_ge(a_oo, NQ + 1)
            dve.wait_ge(slab_done, SLAB)
            for d in range(2):
                ch.link(nc.vector.memset(ep[d][:, :, d * L:d * L + 1], 1.0))
            with dve.Fori(0, FT) as i:
                ch.enter(i, DVE_LINKS)
                dve.wait_ge(ft_done, i + 1)
                nc.vector.tensor_copy(pc[:, 0:9], prm[:, P_FT:P_FT + 9 * FT].rearrange("p (v f) -> p v f", f=FT)[:, :, bass.ds(i, 1)]
                                      .rearrange("p v a -> p (v a)")).then_inc(g_pc, 1)
                dve.wait_ge(g_pc, i + 1)
                ch.link(TS(pc[:, 9:10], pc[:, C_KA:C_KA + 1], -1.0, 1.0, ALU.mult, ALU.add))
                for d in range(2):
                    nc.vector.memset(S_[d][:, :], 0.0).then_inc(c_s0, 1)
                keys, values, reads = flat(s_kv, i), flat(s_kv, i + FT), flat(s_r, i)
                dve.wait_ge(g_rt, i + 1)
                ch.link(TS(sgt[:, :], sgt[:, :], 1e-12, None, ALU.max))
                ch.link(nc.vector.reciprocal(sgt[:, :], sgt[:, :]))
                STT(out=kk[:, :], in0=keys, scalar=pc[:, C_KK:C_KK + 1], in1=sgt[:, :], op0=ALU.mult, op1=ALU.mult).then_inc(g_kk, 1)
                dve.wait_ge(g_kk, i + 1)
                c3 = lambda t: t.rearrange("p (c t) -> p c t", t=L)
                for d in range(2):
                    dve.wait_ge(g_sg, 4 * i + 2 * d + 1)
                    step = 1 if d == 0 else -1
                    nc.vector.tensor_tensor_scan(cum[:, ::step], rst[d][:, ::step], sgt[:, ::step], 0.0, ALU.mult, ALU.add
                                                 ).then_inc(g_cum, 1)
                    dve.wait_ge(g_sg, 4 * i + 2 * d + 2)
                    ch.link(TS(kd[:, :], sat[:, :], pc[:, C_KA:C_KA + 1], pc[:, 9:10], ALU.mult, ALU.add))
                    ch.link(TT(kd[:, :], kd[:, :], keys, ALU.mult))
                    if d == 0:
                        ch.link(nc.vector.tensor_copy(kb[:, :], kd[:, CTX:TOK]))
                    else:
                        ch.link(TT(kb[:, :], kb[:, :], kd[:, CTX:TOK], ALU.add))
                    ch.link(TT(sat[:, :], sat[:, :], kk[:, :], ALU.mult))
                    dve.wait_ge(g_ex, 4 * i + 2 * d + 2)
                    for h, hs in enumerate(halves):
                        TT(bdk[d][hs, :, hs], c3(kd[hs, :]), c3(en[hs, :]), ALU.mult)
                    for h, hs in enumerate(halves):
                        TT(bdb[d][hs, :, hs], c3(sat[hs, :]), c3(en[hs, :]), ALU.mult)
                    TT(ar[d][:, HC:NCH, L:P], c3(reads), ep[d][:, HC:NCH, 1 - d:1 - d + L], ALU.mult)
                    STT(out=ar[d][:, :, 0:L], in0=c3(kk[:, :]), scalar=-1.0, in1=ep[d][:, :, d:d + L],
                        op0=ALU.mult, op1=ALU.mult).then_inc(g_bd, 1)
                    dve.wait_ge(g_bd, 2 * i + d + 1)

                def bd(dst, bank, d, cs):
                    src = bank[:, :].rearrange("p (c n) -> p c n", n=P)[:, :, 0:L].unsqueeze(2).to_broadcast([P, HC, 2, L])
                    m = strict[d].rearrange("p (h t) -> p h t", h=2).unsqueeze(1).to_broadcast([P, HC, 2, L])
                    return TT(dst[d][:, cs, :].rearrange("p c (h t) -> p c h t", h=2), src, m, ALU.mult)

                def incmask(dst, bank, d):
                    src = bank[:, :].rearrange("p (c n) -> p c n", n=P)[:, :, L:P]
                    return TT(dst[d][:, :, :], src, incl[d].unsqueeze(1).to_broadcast([P, HC, L]), ALU.mult)

                for s, (d, g) in enumerate(STREAMS):
                    cs = slice(HC * g, HC * g + HC)
                    for k, (dst, dst2, bank) in enumerate(((dd, arb, PS[s]), (aak, ark, PS[4 + s]))):
                        dve.wait_ge(g_am, 8 * i + 2 * s + k + 1)
                        if g == 1:
                            incmask(dst2, bank, d)
                        bd(dst, bank, d, cs).then_inc(g_ae, 1)
                dve.wait_ge(g_ae, 8 * i + 8)
                for s, (d, g) in enumerate(STREAMS):
                    cs = slice(HC * g, HC * g + HC)
                    per = lambda m: m.unsqueeze(1).to_broadcast([P, HC, P])
                    ch.link(TT(zz[d][:, cs, :], dd[d][:, cs, :], per(lv1[d]), ALU.mult))
                    TT(zz[d][:, cs, :], zz[d][:, cs, :], per(ident), ALU.add).then_inc(g_z1, 1)
                for l in range(LEVELS):
                    for s, (d, g) in enumerate(STREAMS):
                        cs = slice(HC * g, HC * g + HC)
                        dve.wait_ge(g_tm, 4 * LEVELS * i + 4 * l + s + 1)
                        TT(bdb[d][:, cs, :], PS[4 + s][:, :].rearrange("p (c n) -> p c n", n=P), per(lvt[d][l]), ALU.mult
                           ).then_inc(g_te, 1)
                    for s, (d, g) in enumerate(STREAMS):
                        cs = slice(HC * g, HC * g + HC)
                        dve.wait_ge(g_zm, 4 * LEVELS * i + 4 * l + s + 1)
                        TT(zz[d][:, cs, :], zz[d][:, cs, :], PS[s][:, :].rearrange("p (c n) -> p c n", n=P), ALU.add
                           ).then_inc(g_ze, 1)
                for n in range(NCH):
                    for d in range(2):
                        dve.wait_ge(c_u, 2 * NCH * i + 2 * n + d + 1)
                        nc.vector.tensor_copy(U_[d][:, :], PS[3 * d + 1][:, 0:P]).then_inc(c_uo, 1)
                dve.wait_ge(c_y, 2 * i + 2)
                ch.link(nc.vector.tensor_copy(yb[:, 0, :], PS[6][:, 0:SEQ]))
                TT(yb[:, 0, :], yb[:, 0, :], PS[7][:, 0:SEQ], ALU.add)
                STT(out=yb[:, 1, :], in0=reads, scalar=pc[:, C_RK:C_RK + 1], in1=kb[:, :], op0=ALU.mult, op1=ALU.mult).then_inc(r_yb, 1)
                dve.wait_ge(r_yb, i + 1)
                dve.wait_ge(r_mu, i + 1)
                STT(out=yb[:, 0, :], in0=PS[0][:, 0:SEQ], scalar=-1.0 / L, in1=yb[:, 0, :], op0=ALU.mult, op1=ALU.add).then_inc(r_yc, 1)
                STT(out=yb[:, 1, :], in0=PS[0][:, SEQ:TOK], scalar=0.5, in1=values[:, CTX:TOK], op0=ALU.mult, op1=ALU.mult)
                dve.wait_ge(r_var, i + 1)
                TS(kd[:, SEQ:TOK], PS[1][:, 0:SEQ], 1.0 / L, GN_EPS, ALU.mult, ALU.add).then_inc(r_vt, 1)
                dve.wait_ge(r_sd, i + 1)
                ch.link(nc.vector.reciprocal(kd[:, SEQ:TOK], kd[:, 0:SEQ]))
                ch.link(TT(yb[:, 0, :], yb[:, 0, :], kd[:, SEQ:TOK], ALU.mult))
                ch.link(TS(yb[:, 0, :], yb[:, 0, :], pc[:, C_LNW:C_LNW + 1], pc[:, C_LNB:C_LNB + 1], ALU.mult, ALU.add))
                ch.link(TT(yb[:, 0, :], yb[:, 0, :], yb[:, 1, :], ALU.add))
                dve.wait_ge(g_gg, i + 1)
                TT(flat(mixt, i + NQ), yb[:, 0, :], gg[:, :], ALU.mult).then_inc(ft_done, 1)
            ch.leave(FT)

            dve.wait_ge(ft_done, FT + 1)
            ch.link(nc.vector.memset(ones[:, :], 1.0))
            for t in range(4):
                dve.wait_ge(d_mh, t + 1)
                TT(h2l[:, 4 * t:4 * t + 4, :], mixt[:, 4 * t:4 * t + 4, :], h2h[:, 4 * t:4 * t + 4, :].bitcast(F32),
                   ALU.subtract).then_inc(d_ml, 1)
            for n in range(2 * KT):
                if n >= 2:
                    dve.wait_ge(d_gm, n - 1)
                col = (M_GT1 if n < KT else M_GT2) + n % KT
                TS(diag[:, n % 2, :], ident, modc[:, col, 0:1], None, ALU.mult).then_inc(d_dg, 1)
            dve.wait_ge(d_gp, 32)
            dve.wait_ge(d_gm, 2 * KT)
            for b in range(8):
                part = slice(b % 4 * 512, b % 4 * 512 + 512)
                TT(gates[:, b // 4, part], PS[b][:, :], gpost[:, b // 4, part], ALU.mult).then_inc(d_gt, 1)
            with dve.Fori(0, KT // 2) as i:
                for j in range(2):
                    low(M_OUT + j, i)

            dve.wait_ge(d_ss, 2)
            TS(stat[:, 14:16], stat[:, 12:14], 1.0 / D, EPS, ALU.mult, ALU.add).then_inc(d_rt, 1)
            dve.wait_ge(d_ss, 3)
            ch.link(nc.vector.reciprocal(stat[:, 18:20], stat[:, 16:18]))
            dve.wait_ge(d_x, 32)
            for t in range(2):
                ch.link(STT(out=mm_[:, t, :], in0=mm_[:, t, :], scalar=stat[:, 18 + t:19 + t], in1=gates[:, 0, :],
                            op0=ALU.mult, op1=ALU.mult))
                TT(x1[:, t, :], x1[:, t, :], mm_[:, t, :], ALU.add).then_inc(d_x1, 1)
            dve.wait_ge(d_ss, 5)
            TS(stat[:, 22:24], stat[:, 20:22], 1.0 / D, EPS, ALU.mult, ALU.add).then_inc(d_rt, 1)
            dve.wait_ge(d_ss, 6)
            ch.link(nc.vector.reciprocal(stat[:, 18:20], stat[:, 24:26]))
            for t in range(2):
                TS(mm_[:, t, :], x1[:, t, :], stat[:, 18 + t:19 + t], None, ALU.mult).then_inc(d_xh, 1)

            def h2_low(kt):
                dve.wait_ge(d_hh, kt + 1)
                TT(h2l[:, kt, :], hm2[:, kt % 2, :], h2h[:, kt, :].bitcast(F32), ALU.subtract).then_inc(d_hl, 1)

            for kt in range(KT):
                dve.wait_ge(d_tr, kt + 1)
                if kt >= 2:
                    dve.wait_ge(d_hl, kt - 1)
                TS(hm2[:, kt % 2, :], PS[kt % 4][:, 0:SEQ], amod2[:, kt:kt + 1], modc[:, M_SH2 + kt, 0:1], ALU.mult, ALU.add
                   ).then_inc(d_hm, 1)
                if kt:
                    h2_low(kt - 1)
            h2_low(KT - 1)
            low(M_IN)
            with dve.Fori(0, F_FF // 2) as i:
                for j in range(2):
                    low(M_IN + j + 1, i)

            def hidden_low(i, j):
                dve.wait_ge(f_fh, 2 * i + j + 1)
                TT(fsl[j][:, :], flat(ffh, 2 * i + j), fsh[j][:, :].bitcast(F32), ALU.subtract).then_inc(f_fl, 1)

            with dve.Fori(0, F_FF // 2 - 1) as i:
                for j in range(2):
                    hidden_low(i, j)
                    low(M_MO + j + 1, i)
            for j in range(2):
                hidden_low(F_FF // 2 - 1, j)
                if j == 0:
                    low(M_END - 1)
            dve.wait_ge(o_ss, 2)
            TS(stat[:, 28:30], stat[:, 26:28], 1.0 / D, EPS, ALU.mult, ALU.add).then_inc(o_rt, 1)
            dve.wait_ge(o_ss, 3)
            ch.link(nc.vector.reciprocal(stat[:, 18:20], stat[:, 30:32]))
            for t in range(2):
                ch.link(STT(out=ffo[:, t, :], in0=ffo[:, t, :], scalar=stat[:, 18 + t:19 + t], in1=gates[:, 1, :],
                            op0=ALU.mult, op1=ALU.mult))
                TT(fin[:, t, :], ffo[:, t, :], x1[:, t, :], ALU.add).then_inc(o_fin, 1)

        @block.tensor
        def _(pe):
            mm, tr = nc.tensor.matmul, nc.tensor.transpose
            pe.sem_inc(ada_used, 2)
            pe.sem_inc(row_T, 1)
            pe.sem_inc(a_qT, 1)
            pe.wait_ge(s_const, 16)
            pe.wait_ge(s_rows, 16 * 14)
            tr(PS[0][:, 0:N_PRM], prow[0:N_PRM, 0, :], ident[0:N_PRM, 0:N_PRM])
            tr(PS[0][:, 128:192], prow[0:64, 1, :], ident[0:64, 0:64])
            tr(PS[0][:, 192:192 + N_ADA], prow[0:N_ADA, 2, :], ident[0:N_ADA, 0:N_ADA]).then_inc(prm_T, 1)
            pe.wait_ge(silu_done, 1)
            pe.wait_ge(prm_done, 3)
            with pe.Fori(0, 3) as ps:
                pe.wait_ge(row_out, 8 * ps + 1)
                pe.wait_ge(mod_done, 2 * ps + 1)
                for kt in range(KT):
                    for h in range(2):
                        pe.wait_ge(raw_landed[h], ps * (16 * KT) + 16 * (kt + 1))
                        for b in range(4):
                            last = mm(PS[4 * h + b][0:2, :], silc[:, kt, :], raw[h][:, b * 512:(b + 1) * 512],
                                      start=kt == 0, stop=kt == KT - 1)
                        last.then_inc(ada_used, 1)
                pe.wait_ge(row_out, 8 * ps + 9)
                pe.sem_inc(pe_go, 1)
                for k in range(32):
                    t_ = tr(PS[0][:, 2 * k:2 * k + 2], modrow[:, k * P:(k + 1) * P], ident[0:2, 0:2])
                t_.then_inc(row_T, 1)
            pe.wait_ge(xhat_done, 4)
            for kt in range(KT):
                if kt >= 4:
                    pe.wait_ge(hm_done, kt - 3)
                for t in range(4):
                    t_ = tr(PS[1 + kt % 4][:, t * P:(t + 1) * P], xs[:, t, kt * P:(kt + 1) * P], ident)
                t_.then_inc(xT_done, 1)

            def parts(hi, lo, s, w):
                return ((hi, whi[s][:, w]), (lo, whi[s][:, w]), (hi, wlo[s][:, w]))

            pe.wait_ge(hl_done, KT)
            for kt in range(KT):
                s = kt % 2
                pe.wait_ge(wlo_ready, kt + 1)
                groups = [(PS[t], t, slice(1024, 1536)) for t in range(4)]
                groups += [(PS[4 + 2 * t + q], 2 + t, slice(q * 512, (q + 1) * 512)) for t in range(2) for q in range(2)]
                for bank, t, w in groups:
                    ts = slice(t * P, (t + 1) * P)
                    for n, (a_, b_) in enumerate(parts(hth[:, kt, ts], htl[:, kt, ts], s, w)):
                        last = mm(bank[:, :], a_, b_, start=kt == 0 and n == 0, stop=kt == KT - 1 and n == 2)
                last.then_inc(w_used, 1)

            def slab_tile(q, i, tok):
                m = M_SLAB + q
                s = m % 2
                n = tok.stop - tok.start
                pe.wait_ge(wlo_ready, 2 * i + m + 1)
                if q >= 2:
                    pe.wait_ge(slab_done, 2 * i + q - 1)
                else:
                    pe.wait_ge(ctx_out, 2 * q + 2)
                for kt in range(KT):
                    w = slice(kt * P, (kt + 1) * P)
                    for k, (a_, b_) in enumerate(parts(hth[:, kt, tok], htl[:, kt, tok], s, w)):
                        last = mm(PS[q % 2][:, 0:n], b_, a_, start=kt == 0 and k == 0, stop=kt == KT - 1 and k == 2)
                last.then_inc(w_used, 1)

            lat, both = slice(CTX, TOK), slice(0, TOK)
            for q, tok in enumerate((lat, both, both)):
                slab_tile(q, 0, tok)
            for (q0, turns, _), tok in zip(SLAB_LOOPS, (lat, both)):
                with pe.Fori(0, turns) as i:
                    for j in range(2):
                        slab_tile(q0 + j, i, tok)

            pe.wait_ge(rot_out, 1)
            pe.wait_ge(slab_done, SLAB)
            for g in range(NKV):
                for t in range(4):
                    t_ = tr(PS[g][:, t * P:(t + 1) * P], ktk[:, t, g * HD:(g + 1) * HD], ident)
                t_.then_inc(kT_done, 1)
            pe.wait_ge(kT_out, 2)
            for g in range(NKV):
                with pe.Fori(0, GQ) as hh:
                    h = hh + g * GQ
                    pe.wait_ge(a_qh, h + 1)
                    for t in range(2):
                        t_ = tr(PS[2][:, t * P:(t + 1) * P], qh[:, t, :], ident)
                    t_.then_inc(a_qT, 1)
                    pe.wait_ge(a_qTo, h + 1)
                    for t in range(2):
                        mm(PS[3 + t][:, :], qT[:, t, :], ktr[:, g, :], start=True, stop=True).then_inc(a_sc, 1)
                    for t in range(2):
                        pe.wait_ge(a_pr, 2 * h + t + 1)
                        for k in range(4):
                            t_ = tr(PS[5 + t][:, k * P:(k + 1) * P], sc[:, t, k * P:(k + 1) * P], ident)
                        t_.then_inc(a_pT, 1)
                    pe.wait_ge(a_oo, h + 1)
                    for t in range(2):
                        pe.wait_ge(a_pTo, 2 * h + t + 1)
                        for k in range(4):
                            last = mm(PS[7][:, t * P:(t + 1) * P], vtk[:, k, g * HD:(g + 1) * HD], pT[:, t, k * P:(k + 1) * P],
                                      start=k == 0, stop=k == 3)
                    last.then_inc(a_o, 1)

            pe.wait_ge(t_lora, 2)
            pe.wait_ge(a_oo, NQ + 1)
            bank3 = lambda b: PS[b][:, :].rearrange("p (c n) -> p c n", n=P)
            with pe.Fori(0, FT) as i:
                pe.wait_ge(g_kq, i + 1)
                mm(PS[0][:, :], ones_bd, en[:, :], start=True, stop=True).then_inc(g_nr, 1)
                pe.wait_ge(g_w, 48 * i + 48)
                for k, src in enumerate((s_w, s_a)):
                    for d, ds_ in enumerate(halves):
                        mm(PS[1 + 2 * k + d][:, :], wsl[ds_, k, :], src[ds_, :], start=True, stop=True).then_inc(g_lo, 1)
                mm(PS[5][:, 0:SEQ], wsl[:, 2, :], s_g[:, :], start=True, stop=True).then_inc(g_lo, 1)
                pe.wait_ge(g_vb, 2 * i + 2)
                for g in range(2):
                    for k in range(HC):
                        t_ = tr(PS[6 + g][:, k * P:(k + 1) * P], vbd[:, HC * g + k, :], ident)
                    t_.then_inc(g_vT, 1)
                pe.wait_ge(g_bd, 2 * i + 2)
                pe.wait_ge(g_gg, i + 1)
                for s, (d, g) in enumerate(STREAMS):
                    n = L if g == 0 else P
                    for lhs, b in ((bdb[d], s), (bdk[d], 4 + s)):
                        if b >= 6:
                            pe.wait_ge(g_vo, 2 * i + 2)
                        for k in range(HC):
                            ck = HC * g + k
                            last = mm(PS[b][:, k * P:k * P + n], lhs[:, ck, :], ar[d][:, ck, 0:n], start=True, stop=True)
                        last.then_inc(g_am, 1)
                for s, (d, g) in enumerate(STREAMS):
                    for k2, (src, b) in enumerate(((bdk[d], 4 + s), (bdb[d], s))):
                        pe.wait_ge(g_ae, 8 * i + 2 * s + 2 - k2)
                        if k2 == 0:
                            pe.wait_ge(g_ae, 8 * i + 2 * s + 2)
                        for k in range(HC):
                            t_ = tr(PS[b][:, k * P:(k + 1) * P], src[:, HC * g + k, :], ident)
                        t_.then_inc(g_tr, 1)

                def turn_x(s, d, g):
                    for k in range(HC):
                        t_ = tr(PS[4 + s][:, k * P:(k + 1) * P], zz[d][:, HC * g + k, :], ident)
                    t_.then_inc(g_xt, 1)

                for s, (d, g) in enumerate(STREAMS):
                    pe.wait_ge(g_z1, 4 * i + s + 1)
                    pe.wait_ge(g_to, 8 * i + 2 * s + 2)
                    turn_x(s, d, g)
                for l in range(LEVELS):
                    for s, (d, g) in enumerate(STREAMS):
                        pe.wait_ge(g_xo, 4 * LEVELS * i + 4 * l + s + 1)
                        for k in range(HC):
                            ck = HC * g + k
                            last = mm(PS[4 + s][:, k * P:(k + 1) * P], dd[d][:, ck, :], bdk[d][:, ck, :], start=True, stop=True)
                        last.then_inc(g_tm, 1)
                    for s, (d, g) in enumerate(STREAMS):
                        pe.wait_ge(g_te, 4 * LEVELS * i + 4 * l + s + 1)
                        for k in range(HC):
                            ck = HC * g + k
                            last = mm(PS[s][:, k * P:(k + 1) * P], bdb[d][:, ck, :], zz[d][:, ck, :], start=True, stop=True)
                        last.then_inc(g_zm, 1)
                    for s, (d, g) in enumerate(STREAMS):
                        pe.wait_ge(g_ze, 4 * LEVELS * i + 4 * l + s + 1)
                        if l < LEVELS - 1:
                            turn_x(s, d, g)
                pe.wait_ge(g_ba, 4 * i + 4)
                pe.wait_ge(c_s0, 2 * i + 2)
                for n in range(NCH):
                    for d in range(2):
                        ck = chunk(d, n)
                        mm(PS[3 * d][:, 0:P], aak[d][:, ck, :], vt[:, ck, :], start=True, stop=False)
                        if n:
                            pe.wait_ge(c_so, 2 * (NCH - 1) * i + 2 * n + d - 1)
                        mm(PS[3 * d][:, 0:P], bda[d][:, ck, :], S_[d][:, :], start=False, stop=True).then_inc(c_p, 1)
                    for d in range(2):
                        ck = chunk(d, n)
                        pe.wait_ge(c_po, 2 * NCH * i + 2 * n + d + 1)
                        mm(PS[3 * d + 1][:, 0:P], zz[d][:, ck, :], P_[d][:, :], start=True, stop=True).then_inc(c_u, 1)
                    for d in range(2):
                        ck = chunk(d, n)
                        if n < NCH - 1:
                            mm(PS[3 * d + 2][:, 0:P], ident, S_[d][:, :], start=True, stop=False)
                            mm(PS[3 * d + 2][:, 0:P], bkt[d][:, ck, :], vt[:, ck, :], start=False, stop=False)
                        if n >= HC:
                            y = PS[6 + d][:, (ck - HC) * L:(ck - HC + 1) * L]
                            mm(y, S_[d][:, :], ar[d][:, ck, L:P], start=True, stop=False)
                            mm(y, vt[:, ck, :], ark[d][:, ck - HC, :], start=False, stop=False)
                        pe.wait_ge(c_uo, 2 * NCH * i + 2 * n + d + 1)
                        if n >= HC:
                            last = mm(y, U_[d][:, :], arb[d][:, ck - HC, :], start=False, stop=True)
                            if n == NCH - 1:
                                last.then_inc(c_y, 1)
                        if n < NCH - 1:
                            mm(PS[3 * d + 2][:, 0:P], bbt[d][:, ck, :], U_[d][:, :], start=False, stop=True).then_inc(c_s, 1)
                pe.wait_ge(r_yb, i + 1)
                mm(PS[0][:, :], ones_bd, yb[:, :, :].rearrange("p a n -> p (a n)"), start=True, stop=True).then_inc(r_mu, 1)
                pe.wait_ge(r_sq, i + 1)
                mm(PS[1][:, 0:SEQ], ones_bd, kd[:, 0:SEQ], start=True, stop=True).then_inc(r_var, 1)

            pe.wait_ge(d_ml, 4)
            for n in range(2 * KT):
                pe.wait_ge(d_dg, n + 1)
                mm(PS[n // 4][:, n % 4 * P:(n % 4 + 1) * P], ones[:, :], diag[:, n % 2, :], start=True, stop=True).then_inc(d_gm, 1)
            pe.wait_ge(d_gt, 8)
            for kt in range(KT):
                m = M_OUT + kt
                s = m % 2
                pe.wait_ge(wlo_ready, m + 1)
                for b in range(8):
                    ts = slice(b // 4 * P, (b // 4 + 1) * P)
                    w = slice(b % 4 * 512, b % 4 * 512 + 512)
                    for n, (a_, b_) in enumerate(parts(h2h[:, kt, ts], h2l[:, kt, ts], s, w)):
                        last = mm(PS[b][:, :], a_, b_, start=kt == 0 and n == 0, stop=kt == KT - 1 and n == 2)
                last.then_inc(w_used, 1)
            pe.wait_ge(d_out, 8)
            pe.wait_ge(d_xh, 2)
            for kt in range(KT):
                if kt >= 4:
                    pe.wait_ge(d_hm, kt - 3)
                for t in range(2):
                    t_ = tr(PS[kt % 4][:, t * P:(t + 1) * P], mm_[:, t, kt * P:(kt + 1) * P], ident)
                t_.then_inc(d_tr, 1)
            pe.wait_ge(d_hl, KT)
            with pe.Fori(0, F_FF // 2) as i:
                for j in range(2):
                    m = M_IN + j
                    s = m % 2
                    pe.wait_ge(wlo_ready, 2 * i + m + 1)
                    pe.wait_ge(e_re, 2 * i + j + 1)
                    for kt in range(KT):
                        for k, (a_, b_) in enumerate(parts(h2h[:, kt, :], h2l[:, kt, :], s, slice(kt * P, (kt + 1) * P))):
                            last = mm(PS[j][:, 0:SEQ], b_, a_, start=kt == 0 and k == 0, stop=kt == KT - 1 and k == 2)
                    last.then_inc(w_used, 1)
            pe.wait_ge(e_re, F_FF + 2)

            def mlp_out(i, j, first=False, final=False):
                m = M_MO + j
                s = m % 2
                pe.wait_ge(f_fl, 2 * i + j + 1)
                pe.wait_ge(wlo_ready, 2 * i + m + 1)
                for b in range(8):
                    ts = slice(b // 4 * P, (b // 4 + 1) * P)
                    w = slice(b % 4 * 512, b % 4 * 512 + 512)
                    for n, (a_, b_) in enumerate(parts(fsh[j][:, ts], fsl[j][:, ts], s, w)):
                        last = mm(PS[b][:, :], a_, b_, start=first and n == 0, stop=final and n == 2)
                last.then_inc(w_used, 1)

            for j in range(2):
                mlp_out(0, j, first=j == 0)
            with pe.Fori(1, F_FF // 2 - 1) as i:
                for j in range(2):
                    mlp_out(i, j)
            for j in range(2):
                mlp_out(F_FF // 2 - 1, j, final=j == 1)


_INS = ["x", "c", "ctx", "c_ctx", "w_ada", "b_ada", "g_pre_mix", "g_post_mix", "g_pre_mlp", "g_post_mlp",
        "w_in", "attn_sink", "rwkv_mu_prev", "rwkv_mu_next", "rwkv_w0", "rwkv_w2", "rwkv_a0", "rwkv_a2",
        "rwkv_g2", "rwkv_k_k", "rwkv_k_a", "rwkv_r_k", "rwkv_ln_w", "rwkv_ln_b", "w_out", "w_mlp_in", "w_mlp_out"]


def kernel(**inputs):
    import numpy as _np
    import concourse.bacc as _bacc
    from concourse import mybir as _mybir
    from concourse.bass_utils import run_bass_kernel_spmd as _run

    nc = _bacc.Bacc("TRN2", target_bir_lowering=False, num_devices=1)
    arrays, args = {}, []
    named = [(name, inputs[name]) for name in _INS] + list(zip(("rec_const", "att_const"), shape_constants()))
    for name, a in named:
        a = _np.ascontiguousarray(a)
        arrays[f"in_{name}_dram"] = a
        args.append(nc.dram_tensor(f"in_{name}_dram", a.shape, _mybir.dt.from_np(a.dtype), kind="ExternalInput").ap())
    args.append(nc.dram_tensor("out_0_dram", (1, SEQ, D), F32, kind="ExternalOutput").ap())
    build_program(nc, *args)
    r = _run(nc, [arrays], core_ids=[0])
    return r.results[0]["out_0_dram"]
```

```python
from contextlib import ExitStack

import numpy as np

import concourse.bass as bass
from concourse import mybir

F32 = mybir.dt.float32
F32R = mybir.dt.float32r
ALU = mybir.AluOpType
ACT = mybir.ActivationFunctionType
AX = mybir.AxisListType

P = 128
D = 2048
KT = D // P
SEQ, CTX = 256, 256
TOK = CTX + SEQ
NQ, NKV, HD = 8, 2, 128
GQ = NQ // NKV
ATT_IN = NQ * HD + 2 * NKV * HD
N_ADA = 6 * D // P
SLAB = 27
T_R, T_K, T_V, T_W, T_A, T_G = 0, 8, 16, 24, 25, 26
FT = 8
L = 64
NCH = TOK // L
HC = NCH // 2
LEVELS = 5
F_FF = 4 * D // P
SLOT = 2048
EPS, GN_EPS = 1e-6, 64e-5
DECAY = float(np.exp(-0.5))
NEG = -1e30

P_MUP, P_MUN, P_FT = 0, 27, 54
N_PRM = P_FT + 9 * FT
C_KK, C_KA, C_RK, C_LNW, C_LNB, C_W0, C_A0 = 0, 1, 2, 3, 4, 5, 7
V_C, V_CC, V_GMIX, V_GMLP = 0, 16, 32, 48
M_SH1, M_SC1, M_GT1, M_SH2, M_SC2, M_GT2 = (16 * k for k in range(6))


def shape_constants():
    f = np.float32
    row = np.arange(P)
    head, t = row // L, row % L
    same = head[:, None] == head[None, :]
    ident = np.eye(P, dtype=f)
    ones_bd = same.astype(f)
    strict, incl, lv1, lvt, rst = [], [], [], [], []
    for d in range(2):
        s = t if d == 0 else L - 1 - t
        strict.append((same & (s[:, None] < s[None, :])).astype(f))
        s64 = s[:L]
        incl.append((s[:, None] <= s64[None, :]).astype(f))
        early, late = s[:, None], s[None, :]
        lv1.append((same & (early // 2 == late // 2) & (early < late)).astype(f))
        for level in range(LEVELS):
            b = 2 ** (level + 1)
            later, earlier = s[:, None], s[None, :]
            lvt.append((same & (later // (2 * b) == earlier // (2 * b))
                        & (later // b > earlier // b)).astype(f))
        r = np.ones(TOK, f)
        r[(0 if d == 0 else L - 1)::L] = 0
        rst.append(np.broadcast_to(r, (P, TOK)))
    rec = np.concatenate([ident, ones_bd, *strict, *incl, *lv1, *lvt, *rst], axis=1).astype(f)
    q, k = np.arange(P)[:, None], np.arange(SEQ)[None, :]
    att = np.zeros((P, 2, TOK), f)
    for qt in range(2):
        att[:, qt, CTX:] = np.where(np.abs(k - (q + qt * P)) <= 128, 0.0, NEG)
    n = HD // 4
    inv = (f(10000.0) ** (-np.arange(n, dtype=f) / f(n))).astype(f)
    pos = np.arange(SEQ)
    ar = (pos // 64).astype(f)[:, None] * inv[None]
    ac = (pos % 64).astype(f)[:, None] * inv[None]
    cos = np.concatenate([np.cos(ar), np.cos(ar), np.cos(ac), np.cos(ac)], axis=1)
    sin = np.concatenate([-np.sin(ar), np.sin(ar), -np.sin(ac), np.sin(ac)], axis=1)
    rope = np.stack([cos, sin], axis=1).reshape(2, P, 2, HD).transpose(1, 0, 2, 3)
    attn = np.concatenate([att.reshape(P, -1), rope.reshape(P, -1)], axis=1).astype(f)
    return np.ascontiguousarray(rec), np.ascontiguousarray(attn)


class Chain:

    def __init__(self, eng, sem):
        self.eng, self.sem, self.base, self.n = eng, sem, 0, 0

    def link(self, ins):
        ins.then_inc(self.sem, 1)
        self.n += 1
        self.eng.wait_ge(self.sem, self.base + self.n)

    def enter(self, i, per, first=0):
        self.outer, self.per, self.n0 = self.base, per, self.n
        self.base = i * per + (self.outer + self.n - first * per)
        self.n = 0

    def leave(self, turns):
        assert self.n == self.per, (self.n, self.per)
        self.base, self.n = self.outer + self.n0 + turns * self.per, 0


def build_program(nc, x, c, ctx_tok, c_ctx, w_ada, b_ada, g_pre_mix, g_post_mix, g_pre_mlp, g_post_mlp,
                  w_in, attn_sink, mu_prev, mu_next, w0, w2, a0, a2, g2, k_k, k_a, r_k, ln_w, ln_b,
                  w_out, w_mlp_in, w_mlp_out, rec_const, att_const, out):
    stack = ExitStack()
    with stack:
        sem = lambda name: stack.enter_context(nc.semaphore(name))
        PS = [stack.enter_context(nc.psum_tensor(f"bank{b}", [P, 512], F32)) for b in range(8)]

        end = [16512]

        def place(name, shape, dtype=F32, offset=None):
            size = 4 * int(np.prod(shape[1:]))
            size = (size + 31) // 32 * 32
            if offset is None:
                offset = end[0]
                end[0] += size
            assert offset + size <= nc.sbuf_usable_end, (name, offset, size)
            return nc.alloc_sbuf_tensor_at(name, shape, dtype, offset=offset)

        class Region:

            def __init__(self, offset, size):
                self.at, self.end = offset, offset + size

            def place(self, name, shape, dtype=F32):
                size = (4 * int(np.prod(shape[1:])) + 31) // 32 * 32
                assert self.at + size <= self.end, (name, self.at, size, self.end)
                t = nc.alloc_sbuf_tensor_at(name, shape, dtype, offset=self.at)
                self.at += size
                return t

        at_rec = end[0]
        rec = place("rec", [P, rec_const.shape[1]])
        at = [0]

        def cols(n):
            at[0] += n
            return rec[:, at[0] - n:at[0]]

        ident, ones_bd = cols(P), cols(P)
        strict = [cols(P) for _ in range(2)]
        incl = [cols(L) for _ in range(2)]
        lv1 = [cols(P) for _ in range(2)]
        lvt = [[cols(P) for _ in range(LEVELS)] for _ in range(2)]
        rst = [cols(TOK) for _ in range(2)]
        prm = place("prm", [P, N_PRM])
        mu0 = place("mu0", [P, SLAB])
        vec = place("vec", [P, 64])
        bada = place("bada", [P, N_ADA])
        modc = place("modc", [P, N_ADA, 2])
        silc = place("silc", [P, KT, 2])
        amod = place("amod", [P, 2, KT])
        amod2 = place("amod2", [P, KT])
        stat = place("stat", [P, 32])
        onec = place("onec", [P, 1])
        sink = place("sink", [P, NQ])
        ring_raw = end[0]
        raw = [place(f"raw{s}", [P, SLOT]) for s in range(2)]
        ring_hl = end[0]
        ada = [nc.alloc_sbuf_tensor_at(f"ada{s}", [P, SLOT], F32, offset=ring_hl + s * 4 * SLOT) for s in range(4)]
        whi = [place(f"whi{s}", [P, SLOT], F32R) for s in range(2)]
        wlo = [place(f"wlo{s}", [P, SLOT], F32R) for s in range(2)]
        reg_a = end[0]
        SZ_A, SZ_B = 64 * 1024, 45 * 1024 + 64
        reg_b = reg_a + SZ_A
        reg_c = reg_b + SZ_B
        SZ_C = nc.sbuf_usable_end - reg_c
        ra = Region(reg_a, SZ_A)
        hth = ra.place("hth", [P, KT, TOK], F32R)
        htl = ra.place("htl", [P, KT, TOK], F32R)
        rb = Region(reg_b, SZ_B)
        s_r = rb.place("s_r", [P, FT, SEQ])
        s_kv = rb.place("s_kv", [P, 2 * FT, TOK])
        s_w = rb.place("s_w", [P, TOK])
        s_a = rb.place("s_a", [P, TOK])
        s_g = rb.place("s_g", [P, SEQ])
        rc = Region(reg_c, SZ_C)
        qtk = rc.place("qtk", [P, 2, NQ * HD])
        ktk = rc.place("ktk", [P, 4, NKV * HD])
        vtk = rc.place("vtk", [P, 4, NKV * HD])
        at_ktr = rc.at
        ktr = rc.place("ktr", [P, NKV, TOK])
        att_c = rc.place("att_c", [P, 2 * TOK + 2 * 2 * HD])
        mb = [nc.alloc_sbuf_tensor_at("mb0", [P, 2, 512], F32, offset=at_ktr), rc.place("mb1", [P, 2, 512])]
        macc = [nc.alloc_sbuf_tensor_at(f"macc{g}", [P, 512], F32, offset=reg_b + 12 * 1024 + g * 2048) for g in range(3)]
        macc.append(rc.place("macc3", [P, 512]))
        amask = att_c[:, 0:2 * TOK].rearrange("p (a n) -> p a n", a=2)
        rope = att_c[:, 2 * TOK:].rearrange("p (t a n) -> p t a n", t=2, a=2)
        xa = Region(reg_b, SZ_B)
        xs = xa.place("xs", [P, 4, D])
        prow = xa.place("prow", [P, 3, P])
        xb = Region(reg_a, SZ_A)
        modrow = xb.place("modrow", [2, 4096])
        junk = xb.place("junk", [P, D])
        aacc = xb.place("aacc", [P, 2, 2, 512])
        pick = xb.place("pick", [P, 2, 2])
        xc = Region(reg_c, SZ_C)
        hmod = xc.place("hmod", [P, 2, TOK])
        rr = Region(reg_b, SZ_B)
        rot1 = rr.place("rot1", [P, 512])
        rot2 = rr.place("rot2", [P, 512])
        mixt = nc.alloc_sbuf_tensor_at("mixt", [P, KT, SEQ], F32, offset=reg_a)
        ta = Region(reg_a + 16 * 1024, SZ_A - 16 * 1024)
        qh = ta.place("qh", [P, 2, HD])
        qT = ta.place("qT", [P, 2, P])
        sc = ta.place("sc", [P, 2, TOK])
        pT = ta.place("pT", [P, 2, TOK])
        ast = ta.place("ast", [P, 16])
        ga = Region(reg_a + 16 * 1024, SZ_A - 16 * 1024)
        gc = Region(reg_c, SZ_C)
        gh = Region(ring_raw, 48 * 1024)
        bda = [ga.place(f"bda{d}", [P, NCH, P]) for d in range(2)]
        bdk = [ga.place(f"bdk{d}", [P, NCH, P]) for d in range(2)]
        bdb = [ga.place(f"bdb{d}", [P, NCH, P]) for d in range(2)]
        dd = [ga.place(f"dd{d}", [P, NCH, P]) for d in range(2)]
        zz = [ga.place(f"zz{d}", [P, NCH, P]) for d in range(2)]
        aak = [ga.place(f"aak{d}", [P, NCH, P]) for d in range(2)]
        bkt = [gh.place(f"bkt{d}", [P, NCH, P]) for d in range(2)]
        bbt = [gh.place(f"bbt{d}", [P, NCH, P]) for d in range(2)]
        ar = [gh.place(f"ar{d}", [P, NCH, P]) for d in range(2)]
        vbd = gh.place("vbd", [P, NCH, P])
        vt = gh.place("vt", [P, NCH, P])
        zn = [gh.place(f"zn{d}", [P, NCH, P]) for d in range(2)]
        Se = [gh.place(f"Se{d}", [P, P]) for d in range(2)]
        ep = [gc.place(f"ep{d}", [P, NCH, L + 1]) for d in range(2)]
        sgt = [gc.place(f"sgt{d}", [P, TOK]) for d in range(2)]
        sat = [gc.place(f"sat{d}", [P, TOK]) for d in range(2)]
        cum = [gc.place(f"cum{d}", [P, TOK]) for d in range(2)]
        kk = gc.place("kk", [P, TOK])
        kd = [gc.place(f"kd{d}", [P, TOK]) for d in range(2)]
        arb = [gc.place(f"arb{d}", [P, HC, L]) for d in range(2)]
        ark = [gc.place(f"ark{d}", [P, HC, L]) for d in range(2)]
        rch = [gc.place(f"rch{d}", [P, HC, L]) for d in range(2)]
        gg, ggn, ggh = gc.place("gg", [P, SEQ]), gh.place("ggn", [P, SEQ]), gc.place("ggh", [P, SEQ])
        bonus = gc.place("bonus", [P, SEQ])
        kb = gh.place("kb", [P, SEQ])
        elast = [gh.place(f"elast{d}", [P, NCH]) for d in range(2)]
        S_ = [gh.place(f"S{d}", [P, P]) for d in range(2)]
        U_ = [gh.place(f"U{d}", [P, P]) for d in range(2)]
        P_ = [gh.place(f"P{d}", [P, P]) for d in range(2)]
        yb = gc.place("yb", [P, 2, SEQ])
        yq = gc.place("yq", [P, 2, SEQ])
        pc, pcr = gc.place("pc", [P, 10]), gc.place("pcr", [P, 2])
        wsl = gh.place("wsl", [P, 3, P])
        ffh = nc.alloc_sbuf_tensor_at("ffh", [P, F_FF, SEQ], F32, offset=reg_a)
        mm_ = nc.alloc_sbuf_tensor_at("mm_", [P, 2, D], F32, offset=reg_a + 16 * 1024)
        gpost = nc.alloc_sbuf_tensor_at("gpost", [P, D], F32, offset=reg_a + 32 * 1024)
        diag = nc.alloc_sbuf_tensor_at("diag", [P, 2, P], F32, offset=reg_a + 48 * 1024)
        masks = Region(at_rec + 2 * P * 4, 4 * (rec_const.shape[1] - 2 * P))
        eb = [masks.place(f"eb{s}", [P, 2, 512]) for s in range(2)]
        ones = masks.place("ones", [P, P])
        hm2 = nc.alloc_sbuf_tensor_at("hm2", [P, 2, SEQ], F32, offset=reg_a + 52 * 1024)
        er = Region(reg_b, nc.sbuf_usable_end - reg_b)
        h2h = er.place("h2h", [P, KT, SEQ], F32R)
        h2l = er.place("h2l", [P, KT, SEQ], F32R)
        gates = er.place("gates", [P, 2, D])
        x1 = er.place("x1", [P, 2, D])
        gpost2 = er.place("gpost2", [P, D])
        relu = er.place("relu", [P, 2, SEQ])
        fsh = [er.place(f"fsh{s}", [P, SEQ], F32R) for s in range(2)]
        fsl = [er.place(f"fsl{s}", [P, SEQ], F32R) for s in range(2)]
        junk2 = nc.alloc_sbuf_tensor_at("junk2", [P, D], F32, offset=reg_a + 54 * 1024)
        ffo = nc.alloc_sbuf_tensor_at("ffo", [P, 2, D], F32, offset=reg_a)
        junk3 = nc.alloc_sbuf_tensor_at("junk3", [P, D], F32, offset=reg_a + 16 * 1024)
        fin = nc.alloc_sbuf_tensor_at("fin", [P, 2, D], F32, offset=reg_b)

        s_const, s_rows, s_x = sem("constants_landed"), sem("param_rows_landed"), sem("tokens_landed")
        s_attc, s_sink = sem("att_constants_landed"), sem("sink_landed")
        raw_landed = [sem(f"raw{s}_landed") for s in range(2)]
        ada_landed = [sem(f"ada{s}_landed") for s in range(4)]
        ada_used, ada_dve, ada_sum, ada_pick = sem("ada_slot_used"), sem("ada_block_summed"), sem("ada_sums_ready"), sem("pick_ready")
        mb_landed = [sem(f"mod_blocks{s}_landed") for s in range(2)]
        m_acc, m_red, m_out = sem("mod_block_added"), sem("mod_partitions_summed"), sem("mod_group_out")
        eb_landed = [sem(f"gate_blocks{s}_landed") for s in range(2)]
        e_zero, e_bias, e_acc, e_red, e_gt = (sem("gate_zeroed"), sem("gate_bias_landed"), sem("gate_block_added"),
                                              sem("gate_partitions_summed"), sem("gate2_ready"))
        prm_T, prm_done = sem("params_transposed"), sem("params_in_columns")
        silu_sig, silu_done = sem("silu_sigmoid"), sem("silu_ready")
        row_out, row_T, mod_done = sem("mod_row_out"), sem("mod_transposed"), sem("mod_in_columns")
        ss_done, sq_done, xhat_done = sem("squares_summed"), sem("root_done"), sem("tokens_normed")
        xT_done, hm_done, hh_done, hl_done = sem("tokens_transposed"), sem("modulated"), sem("h_high"), sem("h_low")
        whi_ready, wlo_ready, w_used = sem("weights_high"), sem("weights_low"), sem("weights_used")
        ctx_out, rot_out = sem("context_kv_out"), sem("latent_qkv_out")
        kT_done, kT_out = sem("k_transposed"), sem("kT_out")
        slab_base, slab_done = sem("slab_base"), sem("slab_shifted")
        dve_s, act_s, pool_s = sem("vector_chain"), sem("scalar_chain"), sem("gpsimd_chain")
        a_qh, a_qT, a_qTo, a_sc, a_lg = sem("q_head_copied"), sem("q_transposed"), sem("qT_out"), sem("scores_done"), sem("negmax_ready")
        a_ex, a_pr, a_pT, a_pTo, a_o, a_oo = sem("exps_done"), sem("probs_ready"), sem("probs_transposed"), sem("pT_out"), sem("att_product"), sem("att_out")
        g_w, g_pc, g_kq, g_nr, g_rt, g_kk = sem("lora_landed"), sem("tile_params"), sem("k_squares"), sem("k_norms"), sem("k_roots"), sem("kk_ready")
        g_lo, g_sg, g_cum, g_ex, g_gg = sem("lora_products"), sem("sigmoids"), sem("decay_sums"), sem("decay_exps"), sem("gate_out")
        g_sa, g_bb, g_bd, g_ba = sem("rates_by_k"), sem("block_b_ready"), sem("operands_ready"), sem("block_a_ready")
        g_vb, g_am, g_ae, g_tr, g_to = sem("v_blocks"), sem("chunk_products"), sem("chunk_masked"), sem("tilde_transposed"), sem("tilde_out")
        g_z1, g_xt, g_xo, g_tm, g_te, g_zm, g_ze = (sem("z_started"), sem("x_transposed"), sem("x_out"), sem("t_product"),
                                                    sem("t_masked"), sem("z_product"), sem("z_added"))
        c_se = sem("state_decayed")
        g_kb, r_mv = sem("key_blocks_ready"), sem("bonus_and_gate_moved")
        g_el, c_p, c_po, c_u, c_uo, c_s, c_so = (sem("last_decays"), sem("p_product"), sem("p_out"), sem("u_product"),
                                                 sem("u_out"), sem("state_product"), sem("state_out"))
        c_yd = sem("y_added")
        r_yb, r_bo, r_gg, r_mu, r_sq, r_bm, r_var, r_vt, r_sd, ft_done = (
            sem("y_out"), sem("bonus_ready"), sem("gate_kept"), sem("y_means"), sem("y_squares"), sem("means_read"),
            sem("y_variances"), sem("y_var_eps"), sem("y_roots"), sem("tile_done"))
        ft_init = sem("zero_blocks")
        t_lora = sem("lora_inputs")
        d_mh, d_ml = sem("mix_high"), sem("mix_low")
        d_out, d_ss, d_rt, d_xh = sem("out_evacuated"), sem("out_squares"), sem("out_roots"), sem("x1_normed")
        d_gp, d_dg, d_gm, d_gt, d_x, d_x1 = sem("gpost_landed"), sem("gate_diag"), sem("gate_rows"), sem("gate_ready"), sem("x_again"), sem("x1_ready")
        d_tr, d_hm, d_hh, d_hl = sem("x1_transposed"), sem("x1_modulated"), sem("h2_high"), sem("h2_low")
        e_re, e_ff = sem("mlp_relu"), sem("mlp_squared")
        f_fh, f_fl = sem("ff_high"), sem("ff_low")
        o_out, o_ss, o_rt, o_fin, o_st = (sem("mlp_evacuated"), sem("mlp_squares"), sem("mlp_root"), sem("result_ready"),
                                          sem("result_stored"))
        a_rc = sem("sums_inverted")
        pe_go, pool_go = sem("tensor_goes_on"), sem("gpsimd_goes_on")

        x_var, r_yc = sem("token_variances"), sem("y_centred")

        def chunk(d, n):
            return n if d == 0 else HC * (n // HC) + HC - 1 - n % HC

        DVE_LINKS = 21
        LBANK = (4, 6, 0, 1)
        STREAMS = [(d, g) for d in range(2) for g in range(2)]
        TURNED = [(d, k, g) for d in range(2) for k in range(2) for g in range(2)]
        fresh = lambda i: isinstance(i, int) and i == 0
        halves = [slice(L * h, L * h + L) for h in range(2)]

        block = stack.enter_context(nc.Block())

        M_ATT, M_SLAB, M_OUT, M_IN, M_MO = 0, KT, KT + SLAB, 2 * KT + SLAB, 2 * KT + SLAB + F_FF
        M_END = M_MO + F_FF
        M_GROUPS, M_EARLY = 12, 3

        def landed(m0, i):
            return m0 % 2, 16 * (m0 // 2 + 1 + i)

        SLAB_ORDER = [T_G, T_W, T_A]
        SLAB_LOOPS = [(3, FT // 2, T_R), (3 + FT, FT, T_K)]

        rk_row = r_k.rearrange("a h n -> a (h n)")
        w_in2 = w_in[0]
        v_slab = w_in2[:, ATT_IN:].rearrange("(k p) f -> p k f", p=P)
        v_mlp = w_mlp_in[0].rearrange("(k p) f -> p k f", p=P)

        @block.sync
        def _(sp):
            with sp.Fori(0, KT // 2) as i:
                for k in range(4):
                    sp.wait_ge(ada_used, 4 * i + k + 1)
                    sp.wait_ge(ada_dve, 4 * i + k + 1)
                    sp.dma_start(ada[k][:, :], w_ada[0, bass.ds(i * (2 * P) + k // 2 * P, P), k % 2 * SLOT:(k % 2 + 1) * SLOT]
                                 ).then_inc(ada_landed[k], 16)

            def slot_free(m, i=0):
                if not (isinstance(i, int) and m < 2):
                    sp.wait_ge(wlo_ready, 2 * i + (m - 1))

            for kt in range(KT):
                slot_free(kt)
                sp.dma_start(raw[kt % 2][:, 0:ATT_IN], w_in2[kt * P:(kt + 1) * P, 0:ATT_IN]).then_inc(raw_landed[kt % 2], 16)

            def load_tile(m, i, view, col):
                slot_free(m, i)
                sp.dma_start(raw[m % 2][:, :].rearrange("p (k f) -> p k f", k=KT), view[:, :, bass.ds(col, P)]
                             ).then_inc(raw_landed[m % 2], 16)

            for q, tile in enumerate(SLAB_ORDER):
                load_tile(M_SLAB + q, 0, v_slab, tile * P)
            for q, turns, tile in SLAB_LOOPS:
                with sp.Fori(0, turns) as i:
                    for j in range(2):
                        load_tile(M_SLAB + q + j, i, v_slab, i * (2 * P) + (tile + j) * P)

            def load_rows(m0, n, w):
                with sp.Fori(0, n // 2) as i:
                    for j in range(2):
                        slot_free(m0 + j, i)
                        sp.dma_start(raw[(m0 + j) % 2][:, :], w[bass.ds(i * (2 * P) + j * P, P), :]
                                     ).then_inc(raw_landed[(m0 + j) % 2], 16)

            sp.wait_ge(ft_done, FT)
            load_rows(M_OUT, KT, w_out[0])
            for cb in range(4):
                with sp.Fori(0, KT // 4) as i:
                    for j in range(4):
                        load_tile(M_IN + KT * cb + j, 2 * i, v_mlp, i * (4 * P) + (KT * cb + j) * P)
                        if j % 2 == 0:
                            sp.wait_ge(e_acc, 4 * i + (KT * cb + j + 2))
                            sp.dma_start(eb[j // 2][:, :, :], w_ada[0, bass.ds(i * (4 * P) + j * P, 2 * P), M_GT2 * P + cb * 512:
                                                                    M_GT2 * P + (cb + 1) * 512]
                                         .rearrange("(k p) f -> p k f", p=P)).then_inc(eb_landed[j // 2], 16)
            load_rows(M_MO, F_FF, w_mlp_out[0])
            for t in range(2):
                sp.wait_ge(o_fin, t + 1)
                sp.dma_start(out[0, t * P:(t + 1) * P, :], fin[:, t, :]).then_inc(o_st, 16)
            sp.wait_ge(o_st, 32)

        @block.gpsimd
        def _(pool):
            ch = Chain(pool, pool_s)
            def mod_load(g, r, free, col):
                if free is not None:
                    pool.wait_ge(m_acc, free)
                pool.dma_start(mb[r % 2][:, :, :], w_ada[0, 2 * r * P:2 * (r + 1) * P, col].rearrange("(k p) f -> p k f", p=P)
                               ).then_inc(mb_landed[r % 2], 16)

            pool.wait_ge(ada_used, 2 * KT + 4)
            pool.wait_ge(hm_done, 1)
            for g in range(M_EARLY + 1):
                for r in range(KT // 2):
                    q = g * (KT // 2) + r
                    mod_load(g, r, 2 * (q - 1) if q >= 2 else None, slice(M_GT1 * P + g * 512, M_GT1 * P + (g + 1) * 512))
            with pool.Fori(0, M_GROUPS - M_EARLY - 1) as i:
                for r in range(KT // 2):
                    mod_load(0, r, i * KT + ((M_EARLY + 1) * KT + 2 * (r - 1)), bass.ds(i * 512 + (M_GT1 * P + (M_EARLY + 1) * 512), 512))
            pool.wait_ge(rot_out, 1)
            pool.wait_ge(w_used, M_OUT)
            with pool.Fori(0, NQ) as h:
                pool.wait_ge(a_qT, h + 1)
                pool.sem_inc(pool_go, 1)
                pool.tensor_copy(qh[:, :, :], qtk[:, :, bass.ds(h * HD, HD)]).then_inc(a_qh, 1)
            pool.wait_ge(a_oo, NQ + 1)
            for t in (*bda, *bdk, *bdb, vbd):
                pool.memset(t[:, :, :], 0.0).then_inc(ft_init, 1)
            pool.wait_ge(ft_init, 7)

            def prep_weights(t):
                if not fresh(t):
                    pool.wait_ge(g_lo, 5 * t)
                for k, w in enumerate((w2, a2)):
                    pool.dma_start(wsl[:, k, :], w[0].rearrange("d l r -> (d l) r")[:, bass.ds(t * P, P)]).then_inc(g_w, 16)
                pool.dma_start(wsl[:, 2, :], g2[0][:, bass.ds(t * P, P)]).then_inc(g_w, 16)

            def prep_b(t, d):
                pool.wait_ge(g_sa, 2 * t + d + 1)
                pool.wait_ge(g_ex, 4 * t + 2 * d + 2)
                if not fresh(t):
                    pool.wait_ge(g_zm, 4 * LEVELS * t)
                for h, hs in enumerate(halves):
                    pool.tensor_tensor(bdb[d][hs, :, hs], sat[d][hs, :].rearrange("p (c t) -> p c t", t=L),
                                       cum[d][hs, :].rearrange("p (c t) -> p c t", t=L), ALU.mult).then_inc(g_bb, 1)
                    pool.wait_ge(g_bb, 4 * t + 2 * d + h + 1)

            def copy(dst, src, done, count):
                pool.sem_inc(pool_go, 1)
                pool.tensor_copy(dst, src).then_inc(done, 1)
                pool.wait_ge(done, count)

            def turn(i, prep):
                if prep:
                    prep_weights(i + 1)
                if not fresh(i):
                    pool.wait_ge(c_yd, 8 * i)
                for d in range(2):
                    pool.wait_ge(g_bd, 2 * i + d + 1)
                    for h, hs in enumerate(halves):
                        copy(bda[d][hs, :, hs], ar[d][hs, :, 0:L], g_ba, 6 * i + 3 * d + h + 1)
                    copy(rch[d][:, :, :], ar[d][:, HC:NCH, L:P], g_ba, 6 * i + 3 * d + 3)
                if prep:
                    prep_values(i + 1)
                    for d in range(2):
                        prep_b(i + 1, d)

            def prep_values(t):
                if not fresh(t):
                    pool.wait_ge(g_tr, 10 * t)
                for h, hs in enumerate(halves):
                    copy(vbd[hs, :, hs], s_kv[hs, bass.ds(t + FT, 1), :].rearrange("p a (c t) -> p (a c) t", t=L), g_vb, 2 * t + h + 1)

            prep_values(0)
            prep_weights(0)
            for d in range(2):
                prep_b(0, d)
            turn(0, True)
            with pool.Fori(1, FT - 1) as i:
                turn(i, True)
            turn(FT - 1, False)
            pool.sem_inc(e_ff, 2)
            with pool.Fori(0, F_FF // 2) as i:
                for j in range(2):
                    pool.wait_ge(e_re, 2 * i + j + 3)
                    pool.tensor_tensor(ffh[:, bass.ds(2 * i + j, 1), :], relu[:, j:j + 1, :], relu[:, j:j + 1, :],
                                       ALU.mult).then_inc(e_ff, 1)

        @block.scalar
        def _(act):
            A = nc.scalar.activation
            act.dma_start(rec[:, :], rec_const).then_inc(s_const, 16)
            rows = [(mu_prev, P_MUP, SLAB), (mu_next, P_MUN, SLAB), (k_k, P_FT, FT), (k_a, P_FT + FT, FT),
                    (rk_row, P_FT + 2 * FT, FT), (ln_w, P_FT + 3 * FT, FT), (ln_b, P_FT + 4 * FT, FT)]
            for w, r, n in rows:
                act.dma_start(prow[r:r + n, 0, :], w[0].rearrange("(k p) -> k p", p=P)).then_inc(s_rows, 16)
            for w, r in ((w0, P_FT + 5 * FT), (a0, P_FT + 7 * FT)):
                act.dma_start(prow[r:r + 2 * FT, 0, :], w[0].rearrange("d (k p) -> (d k) p", p=P)).then_inc(s_rows, 16)
            for w, r in ((c[0], V_C), (c_ctx, V_CC), (g_pre_mix[0], V_GMIX), (g_pre_mlp[0], V_GMLP)):
                act.dma_start(prow[r:r + KT, 1, :], w.rearrange("(k p) -> k p", p=P)).then_inc(s_rows, 16)
            act.dma_start(prow[0:N_ADA, 2, :], b_ada[0].rearrange("(k p) -> k p", p=P)).then_inc(s_rows, 16)
            for t in range(2):
                act.dma_start(xs[:, t, :], ctx_tok[0, t * P:(t + 1) * P, :]).then_inc(s_x, 16)
            for t in range(2):
                act.dma_start(xs[:, 2 + t, :], x[0, t * P:(t + 1) * P, :]).then_inc(s_x, 16)
            act.dma_start(sink[:, :], attn_sink.to_broadcast([P, NQ])).then_inc(s_sink, 16)
            act.sem_inc(a_oo, 1)
            act.sem_inc(e_re, 2)
            act.wait_ge(prm_done, 3)
            A(stat[:, 0:32], vec[:, 0:32], ACT.Sigmoid).then_inc(silu_sig, 1)
            act.wait_ge(s_x, 64)
            act.wait_ge(silu_done, 1)
            for t in range(4):
                if t:
                    act.wait_ge(ss_done, t)
                A(junk[:, :], xs[:, t, :], ACT.Square, accum_out=stat[:, t:t + 1]).then_inc(ss_done, 1)
            act.wait_ge(x_var, 1)
            A(stat[:, 8:12], stat[:, 4:8], ACT.Sqrt).then_inc(sq_done, 1)
            act.wait_ge(ada_used, 2 * KT + 4)
            act.wait_ge(ada_sum, 2)
            for b in range(8):
                A(modrow[:, b * 512:(b + 1) * 512], PS[b][0:2, :], ACT.Copy).then_inc(row_out, 1)
            for kt in range(KT):
                act.wait_ge(hm_done, kt + 1)
                if kt == 0:
                    act.wait_ge(row_T, 1)
                A(hth[:, kt, :], hmod[:, kt % 2, :], ACT.Copy).then_inc(hh_done, 1)

            def high(m, i=0, n=SLOT):
                s, count = landed(m, i)
                act.wait_ge(raw_landed[s], count)
                if isinstance(i, int) and m < 2:
                    act.wait_ge(ada_used, 2 * KT + 4)
                    act.wait_ge(ada_dve, 2 * KT + 4)
                if not (isinstance(i, int) and m < 2):
                    act.wait_ge(w_used, 2 * i + m - 1)
                A(whi[s][:, 0:n], raw[s][:, 0:n], ACT.Copy).then_inc(whi_ready, 1)

            for m in range(KT):
                high(m, 0, ATT_IN)
            high(M_SLAB)
            act.wait_ge(hl_done, KT)
            act.dma_start(att_c[:, :], att_const).then_inc(s_attc, 16)
            act.wait_ge(w_used, KT)
            for t in range(2):
                A(ktk[:, t, :], PS[t][:, 0:256], ACT.Copy).then_inc(ctx_out, 1)
                A(vtk[:, t, :], PS[t][:, 256:512], ACT.Copy).then_inc(ctx_out, 1)

            def base(q, i, dst, mu, last=False):
                if not last:
                    high(M_SLAB + q + 1, i)
                act.wait_ge(w_used, 2 * i + (M_SLAB + q + 1))
                if q == 0:
                    act.wait_ge(rot_out, 1)
                n = dst.free_size()
                A(dst, PS[q % 2][:, 0:n], ACT.Copy, scale=mu).then_inc(slab_base, 1)

            for q, (tile, dst) in enumerate(zip(SLAB_ORDER, (s_g, s_w, s_a))):
                base(q, 0, dst[:, :], mu0[:, tile:tile + 1])
            q0, turns, _ = SLAB_LOOPS[0]
            with act.Fori(0, turns) as i:
                for j in range(2):
                    base(q0 + j, i, s_r[:, bass.ds(2 * i + j, 1), :].rearrange("p a n -> p (a n)"),
                         mu0[:, bass.ds(2 * i + T_R + j, 1)])
            q0, turns, _ = SLAB_LOOPS[1]
            kv = lambda e: s_kv[:, bass.ds(e, 1), :].rearrange("p a n -> p (a n)")
            with act.Fori(0, turns - 1) as i:
                for j in range(2):
                    base(q0 + j, i, kv(2 * i + j), mu0[:, bass.ds(2 * i + T_K + j, 1)])
            for j in range(2):
                e = 2 * (turns - 1) + j
                base(q0 + j + 2 * (turns - 1), 0, s_kv[:, e, :], mu0[:, T_K + e:T_K + e + 1], last=j == 1)
            act.wait_ge(m_acc, M_GROUPS * KT)
            for g in range(NKV):
                act.wait_ge(kT_done, g + 1)
                A(ktr[:, g, :], PS[g][:, :], ACT.Copy).then_inc(kT_out, 1)
            act.wait_ge(s_sink, 16)
            with act.Fori(0, NQ) as h:
                act.wait_ge(a_qT, h + 2)
                A(qT[:, :, :].rearrange("p a n -> p (a n)"), PS[2][:, 0:256], ACT.Copy, scale=float(HD) ** -0.5).then_inc(a_qTo, 1)
                act.wait_ge(a_lg, h + 1)
                for t in range(2):
                    A(sc[:, t, :], sc[:, t, :], ACT.Exp, bias=ast[:, 2 + t:3 + t], accum_out=ast[:, 4 + t:5 + t]).then_inc(a_ex, 1)
                    A(ast[:, 6 + t:7 + t], sink[:, bass.ds(h, 1)], ACT.Exp, bias=ast[:, 2 + t:3 + t]).then_inc(a_ex, 1)
                for t in range(2):
                    act.wait_ge(a_pT, 2 * h + t + 1)
                    A(pT[:, t, :], PS[5 + t][:, :], ACT.Copy).then_inc(a_pTo, 1)
                act.wait_ge(a_o, h + 1)
                A(mixt[:, bass.ds(h, 1), :].rearrange("p a n -> p (a n)"), PS[7][:, 0:SEQ], ACT.Copy).then_inc(a_oo, 1)
            act.wait_ge(slab_done, SLAB)
            A(s_w[:, :], s_w[:, :], ACT.Tanh).then_inc(t_lora, 1)
            A(s_g[:, :], s_g[:, :], ACT.Sigmoid).then_inc(t_lora, 1)

            def prep_square(t):
                act.wait_ge(g_pc, t + 1)
                if not fresh(t):
                    act.wait_ge(g_cum, 2 * t)
                A(sgt[0][:, :], s_kv[:, bass.ds(t, 1), :].rearrange("p a n -> p (a n)"), ACT.Square, scale=pc[:, C_KK:C_KK + 1]).then_inc(g_kq, 1)

            def prep_root(t):
                act.wait_ge(g_nr, t + 1)
                if not fresh(t):
                    act.wait_ge(g_kb, 2 * t)
                A(kd[0][:, :], PS[2][:, :], ACT.Sqrt).then_inc(g_rt, 1)

            def prep_sigmoid(t, k):
                act.wait_ge(g_lo, 5 * t + k + 1)
                if k == 2 and not fresh(t):
                    act.wait_ge(g_bb, 4 * t)
                A((sgt, sat)[k // 2][k % 2][:, :], PS[(5, 7, 2, 5)[k]][:, :], ACT.Sigmoid, bias=pc[:, C_W0 + k:C_W0 + k + 1]).then_inc(g_sg, 1)

            def prep_exp(t, d):
                act.wait_ge(g_cum, 2 * t + d + 1)
                if not fresh(t):
                    act.wait_ge(g_el, 2 * t)
                o = 1 - d
                A(ep[d][:, :, o:o + L], cum[d][:, :].rearrange("p (c t) -> p c t", t=L), ACT.Exp, scale=-DECAY).then_inc(g_ex, 1)
                act.wait_ge(g_ex, 4 * t + 2 * d + 1)
                A(cum[d][:, :], cum[d][:, :], ACT.Exp, scale=DECAY).then_inc(g_ex, 1)

            def prep_gate(t):
                act.wait_ge(g_lo, 5 * t + 5)
                if not fresh(t):
                    act.wait_ge(r_gg, t)
                A(ggn[:, :], PS[7][:, 0:SEQ], ACT.Copy).then_inc(g_gg, 1)

            PREP = {0: [prep_root, lambda t: prep_sigmoid(t, 0)], 1: [lambda t: prep_sigmoid(t, 1), lambda t: prep_sigmoid(t, 2)],
                    2: [lambda t: prep_sigmoid(t, 3), lambda t: prep_exp(t, 0)], 3: [lambda t: prep_exp(t, 1), prep_gate]}

            def turn(i, read, prep):
                if not fresh(i):
                    act.wait_ge(c_yd, 8 * i)
                    act.wait_ge(c_so, 2 * (NCH - 1) * i)
                act.wait_ge(g_ex, 4 * i + 4)
                for d in range(2):
                    A(elast[d][:, :], ep[d][:, :, L if d == 0 else 0], ACT.Copy).then_inc(g_el, 1)
                for q, (d, k, g) in enumerate(TURNED):
                    act.wait_ge(g_tr, 10 * i + q + 1)
                    A((bkt, bbt)[k][d][:, HC * g:HC * g + HC, :], PS[4 + q % 2 * 2][:, :], ACT.Copy).then_inc(g_to, 1)
                for g in range(2):
                    act.wait_ge(g_tr, 10 * i + 9 + g)
                    A(vt[:, HC * g:HC * g + HC, :], PS[4 + 2 * g][:, :], ACT.Copy).then_inc(g_to, 1)
                if prep:
                    prep_square(i + 1)
                for l in range(LEVELS):
                    for s, (d, g) in enumerate(STREAMS):
                        act.wait_ge(g_xt, 4 * LEVELS * i + 4 * l + s + 1)
                        A(bdk[d][:, HC * g:HC * g + HC, :], PS[LBANK[s]][:, :], ACT.Copy).then_inc(g_xo, 1)
                    if prep:
                        for step in PREP.get(l, ()):
                            step(i + 1)
                act.wait_ge(g_el, 2 * i + 2)
                for n in range(NCH):
                    for d in range(2):
                        act.wait_ge(c_p, 2 * NCH * i + 2 * n + d + 1)
                        if n:
                            act.wait_ge(c_so, 2 * (NCH - 1) * i + 2 * n + d - 1)
                        A(P_[d][:, :], PS[3 * d][:, 0:P], ACT.Copy).then_inc(c_po, 1)
                    if 0 < n < NCH - 1:
                        for d in range(2):
                            ck = chunk(d, n)
                            A(Se[d][:, :], S_[d][:, :], ACT.Copy, scale=elast[d][:, ck:ck + 1]).then_inc(c_se, 1)
                    if read and n == 1:
                        read_square(i - 1)
                    if read and n == 3:
                        read_root(i - 1)
                    if n == 5:
                        move(i)

            def move(i):
                if not fresh(i):
                    act.wait_ge(ft_done, i)
                act.wait_ge(r_bo, i + 1)
                act.wait_ge(r_gg, i + 1)
                A(yb[:, 1, :], bonus[:, :], ACT.Copy).then_inc(r_mv, 1)
                A(gg[:, :], ggh[:, :], ACT.Copy).then_inc(r_mv, 1)

            def read_square(r):
                act.wait_ge(r_yc, r + 1)
                A(yq[:, 0, :], yb[:, 0, :], ACT.Square).then_inc(r_sq, 1)

            def read_root(r):
                act.wait_ge(r_vt, r + 1)
                A(yq[:, 0, :], yq[:, 1, :], ACT.Sqrt).then_inc(r_sd, 1)

            prep_square(0)
            for n in range(NCH):
                for step in PREP.get(n, ()):
                    step(0)
            turn(0, False, True)
            with act.Fori(1, FT - 1) as i:
                turn(i, True, True)
            turn(FT - 1, True, False)
            read_square(FT - 1)
            read_root(FT - 1)

            act.wait_ge(ft_done, FT)
            for t, g_post in ((gpost, g_post_mix), (gpost2, g_post_mlp)):
                act.dma_start(t[:, :], g_post[0:1, :].to_broadcast([P, D])).then_inc(d_gp, 16)
            act.wait_ge(e_zero, 1)
            act.dma_start(gates[0:1, 1, :], b_ada[0:1, M_GT2 * P:6 * D]).then_inc(e_bias, 16)
            for t in range(2):
                act.dma_start(x1[:, t, :], x[0, t * P:(t + 1) * P, :]).then_inc(d_x, 16)
            for t in range(4):
                A(h2h[:, 4 * t:4 * t + 4, :], mixt[:, 4 * t:4 * t + 4, :], ACT.Copy).then_inc(d_mh, 1)
            with act.Fori(0, KT // 2) as i:
                for j in range(2):
                    high(M_OUT + j, i)
            act.wait_ge(w_used, M_IN)
            for t in range(2):
                for b in range(4):
                    A(mm_[:, t, b * 512:(b + 1) * 512], PS[4 * t + b][:, :], ACT.Copy).then_inc(d_out, 1)
            act.wait_ge(d_out, 8)
            for t in range(2):
                A(junk2[:, :], mm_[:, t, :], ACT.Square, accum_out=stat[:, 12 + t:13 + t]).then_inc(d_ss, 1)
                act.wait_ge(d_ss, t + 1)
            act.wait_ge(d_rt, 1)
            A(stat[:, 16:18], stat[:, 14:16], ACT.Sqrt).then_inc(d_ss, 1)
            for t in range(2):
                act.wait_ge(d_x1, t + 1)
                A(junk2[:, :], x1[:, t, :], ACT.Square, accum_out=stat[:, 20 + t:21 + t]).then_inc(d_ss, 1)
                act.wait_ge(d_ss, 4 + t)
            act.wait_ge(d_rt, 2)
            A(stat[:, 24:26], stat[:, 22:24], ACT.Sqrt).then_inc(d_ss, 1)
            for kt in range(KT):
                act.wait_ge(d_hm, kt + 1)
                A(h2h[:, kt, :], hm2[:, kt % 2, :], ACT.Copy).then_inc(d_hh, 1)
            high(M_IN)
            with act.Fori(0, F_FF // 2) as i:
                for j in range(2):
                    high(M_IN + j + 1, i)
                    act.wait_ge(w_used, 2 * i + (M_IN + j + 1))
                    act.wait_ge(e_ff, 2 * i + j + 1)
                    A(relu[:, j, :], PS[j][:, 0:SEQ], ACT.Relu).then_inc(e_re, 1)
            act.wait_ge(e_ff, F_FF + 2)

            def hidden(i, j):
                act.wait_ge(w_used, 2 * i + (M_MO + j - 1))
                A(fsh[j][:, :], ffh[:, bass.ds(2 * i + j, 1), :].rearrange("p a n -> p (a n)"), ACT.Copy).then_inc(f_fh, 1)

            with act.Fori(0, F_FF // 2 - 1) as i:
                for j in range(2):
                    hidden(i, j)
                    high(M_MO + j + 1, i)
            for j in range(2):
                hidden(F_FF // 2 - 1, j)
                if j == 0:
                    high(M_END - 1)
            act.wait_ge(w_used, M_END)
            for t in range(2):
                for b in range(4):
                    A(ffo[:, t, b * 512:(b + 1) * 512], PS[4 * t + b][:, :], ACT.Copy).then_inc(o_out, 1)
                act.wait_ge(o_out, 4 * t + 4)
                A(junk3[:, :], ffo[:, t, :], ACT.Square, accum_out=stat[:, 26 + t:27 + t]).then_inc(o_ss, 1)
                act.wait_ge(o_ss, t + 1)
            act.wait_ge(o_rt, 1)
            A(stat[:, 30:32], stat[:, 28:30], ACT.Sqrt).then_inc(o_ss, 1)

        @block.vector
        def _(dve):
            ch = Chain(dve, dve_s)
            TT, TS, STT = nc.vector.tensor_tensor, nc.vector.tensor_scalar, nc.vector.scalar_tensor_tensor
            dve.sem_inc(ada_dve, 4)
            dve.sem_inc(e_acc, 4)
            dve.wait_ge(prm_T, 1)
            nc.vector.tensor_copy(prm[:, :], PS[0][:, 0:N_PRM]).then_inc(prm_done, 1)
            nc.vector.tensor_copy(vec[:, :], PS[0][:, 128:192]).then_inc(prm_done, 1)
            nc.vector.tensor_copy(bada[:, :], PS[0][:, 192:192 + N_ADA]).then_inc(prm_done, 1)
            dve.wait_ge(prm_done, 3)
            ch.link(STT(out=mu0[:, :], in0=prm[:, P_MUP:P_MUP + SLAB], scalar=-1.0, in1=prm[:, P_MUN:P_MUN + SLAB],
                        op0=ALU.mult, op1=ALU.subtract))
            ch.link(TS(mu0[:, :], mu0[:, :], 1.0, None, ALU.add))
            dve.wait_ge(silu_sig, 1)
            TT(silc[:, :, :].rearrange("p k j -> p j k"), vec[:, 0:32].rearrange("p (j k) -> p j k", j=2),
               stat[:, 0:32].rearrange("p (j k) -> p j k", j=2), ALU.mult).then_inc(silu_done, 1)
            ch.link(nc.vector.memset(pick[:, :, :], 0.0))
            for j in range(2):
                nc.vector.memset(pick[:, j, j:j + 1], 1.0).then_inc(ada_pick, 1)
            ch.link(nc.vector.memset(aacc[:, :, :, :], 0.0))
            dve.wait_ge(silu_done, 1)
            with dve.Fori(0, KT // 2) as i:
                ch.enter(i, 4)
                for k in range(4):
                    dve.wait_ge(ada_landed[k], 16 * i + 16)
                    dve.wait_ge(ada_dve, 4 * i + (4 + k - 1))
                    for j in range(2):
                        ins = STT(out=aacc[:, k % 2, j, :], in0=ada[k][:, 3 * 512:SLOT], scalar=silc[:, bass.ds(2 * i + k // 2, 1), j],
                                  in1=aacc[:, k % 2, j, :], op0=ALU.mult, op1=ALU.add)
                        if j == 0:
                            ch.link(ins)
                        else:
                            ins.then_inc(ada_dve, 1)
            ch.leave(KT // 2)
            dve.wait_ge(ss_done, 4)
            TS(stat[:, 4:8], stat[:, 0:4], 1.0 / D, EPS, ALU.mult, ALU.add).then_inc(x_var, 1)
            dve.wait_ge(sq_done, 1)
            ch.link(nc.vector.reciprocal(stat[:, 12:16], stat[:, 8:12]))
            for t in range(4):
                TS(xs[:, t, :], xs[:, t, :], stat[:, 12 + t:13 + t], None, ALU.mult).then_inc(xhat_done, 1)
            dve.wait_ge(row_T, 1)
            for j in range(2):
                TT(modc[:, 0:2 * KT, j], PS[0][:, j:64:2], bada[:, 0:2 * KT], ALU.add).then_inc(mod_done, 1)
            dve.wait_ge(mod_done, 2)
            ch.link(nc.vector.memset(onec[:, :], 1.0))
            for j in range(2):
                ch.link(STT(out=amod[:, j, :], in0=modc[:, M_SC1:M_SC1 + KT, j], scalar=1.0, in1=vec[:, V_GMIX:V_GMIX + KT],
                            op0=ALU.add, op1=ALU.mult))

            def h_low(kt):
                dve.wait_ge(hh_done, kt + 1)
                TT(htl[:, kt, :], hmod[:, kt % 2, :], hth[:, kt, :].bitcast(F32), ALU.subtract).then_inc(hl_done, 1)

            for kt in range(KT):
                dve.wait_ge(xT_done, kt + 1)
                if kt >= 2:
                    dve.wait_ge(hl_done, kt - 1)
                b = PS[1 + kt % 4]
                TS(hmod[:, kt % 2, 0:CTX], b[:, 0:CTX], amod[:, 1, kt:kt + 1], modc[:, M_SH1 + kt, 1:2], ALU.mult, ALU.add)
                TS(hmod[:, kt % 2, CTX:TOK], b[:, CTX:TOK], amod[:, 0, kt:kt + 1], modc[:, M_SH1 + kt, 0:1],
                   ALU.mult, ALU.add).then_inc(hm_done, 1)
                if kt:
                    h_low(kt - 1)
            h_low(KT - 1)

            def low(m, i=0, n=SLOT):
                s = m % 2
                dve.wait_ge(whi_ready, 2 * i + m + 1)
                TT(wlo[s][:, 0:n], raw[s][:, 0:n], whi[s][:, 0:n].bitcast(F32), ALU.subtract).then_inc(wlo_ready, 1)

            def mod_step(g, i, k):
                if k % 2 == 0:
                    dve.wait_ge(mb_landed[k // 2 % 2], 16 * (KT // 4) * i + 16 * (KT // 4 * g + k // 4 + 1))
                acc = macc[g] if g < M_EARLY else macc[M_EARLY]
                src, s_c = mb[k // 2 % 2][:, k % 2, :], silc[:, k, 0:1]
                if k == 0:
                    TS(acc[:, :], src, s_c, None, ALU.mult).then_inc(m_acc, 1)
                else:
                    dve.wait_ge(m_acc, KT * i + (KT * g + k))
                    STT(out=acc[:, :], in0=src, scalar=s_c, in1=acc[:, :], op0=ALU.mult, op1=ALU.add).then_inc(m_acc, 1)

            def mod_out(i, n, at, reds):
                dve.wait_ge(m_red, i + reds)
                TT(modc[:, bass.ds(4 * i + at, n), 0], PS[2][:, 0:n], bada[:, bass.ds(4 * i + at, n)], ALU.add).then_inc(m_out, 1)

            for m in range(KT):
                low(m, 0, ATT_IN)
                for k in range(4):
                    mod_step(m // 4, 0, 4 * (m % 4) + k)
            low(M_SLAB)

            def rotate(dst, src, t, nh):
                n = nh * HD
                cs = rope[:, t, 0, :].unsqueeze(1).to_broadcast([P, nh, HD])
                ch.link(TT(rot1[:, 0:n].rearrange("p (h n) -> p h n", h=nh), src.rearrange("p (h n) -> p h n", h=nh), cs, ALU.mult))
                src4 = src.rearrange("p (h a j n) -> p h a j n", h=nh, a=2, j=2)
                dst4 = rot2[:, 0:n].rearrange("p (h a j n) -> p h a j n", h=nh, a=2, j=2)
                for j in range(2):
                    sn = rope[:, t, 1, :].rearrange("p (a j n) -> p a j n", a=2, j=2)[:, :, j, :]
                    ch.link(TT(dst4[:, :, :, j, :], src4[:, :, :, 1 - j, :],
                               sn.unsqueeze(1).to_broadcast([P, nh, 2, HD // 4]), ALU.mult))
                ch.link(TT(dst, rot1[:, 0:n], rot2[:, 0:n], ALU.add))

            dve.wait_ge(w_used, KT)
            dve.wait_ge(s_attc, 16)
            for t in range(2):
                rotate(ktk[:, 2 + t, :], PS[2 + t][:, 0:256], t, NKV)
                ch.link(nc.vector.tensor_copy(vtk[:, 2 + t, :], PS[2 + t][:, 256:512]))
                for q in range(2):
                    rotate(qtk[:, t, q * 512:(q + 1) * 512], PS[4 + 2 * t + q][:, :], t, 4)
            dve.sem_inc(rot_out, 1)

            def shift(q, i, dst, tile, last=False, between=lambda: None):
                if not last:
                    low(M_SLAB + q + 1, i)
                between()
                dve.wait_ge(slab_base, 2 * i + q + 1)
                n = dst.free_size() // SEQ if dst.free_size() > SEQ else 1
                src = PS[q % 2][:, 0:n * SEQ].rearrange("p (a n) -> p a n", a=n)
                dst = dst.rearrange("p (a n) -> p a n", a=n)
                col = lambda b: prm[:, bass.ds(tile + b, 1)]
                ch.link(STT(out=dst[:, :, 1:SEQ], in0=src[:, :, 0:SEQ - 1], scalar=col(P_MUP), in1=dst[:, :, 1:SEQ],
                            op0=ALU.mult, op1=ALU.add))
                STT(out=dst[:, :, 0:SEQ - 1], in0=src[:, :, 1:SEQ], scalar=col(P_MUN), in1=dst[:, :, 0:SEQ - 1],
                    op0=ALU.mult, op1=ALU.add).then_inc(slab_done, 1)

            flat = lambda t, e: t[:, bass.ds(e, 1), :].rearrange("p a n -> p (a n)")
            for q, (tile, dst) in enumerate(zip(SLAB_ORDER, (s_g, s_w, s_a))):
                shift(q, 0, dst[:, :], tile)
            q0, turns, _ = SLAB_LOOPS[0]
            with dve.Fori(0, turns) as i:
                ch.enter(i, 2)
                for j in range(2):
                    shift(q0 + j, i, flat(s_r, 2 * i + j), 2 * i + T_R + j)
            ch.leave(turns)
            mod_out(0, 4 * M_EARLY, M_GT1, 1)
            q0, turns, _ = SLAB_LOOPS[1]
            assert turns == M_GROUPS - M_EARLY - 1

            def mods(i, j):
                if j == 0:
                    mod_out(i, 4, M_GT1 + 4 * M_EARLY, 2)
                for k in range(KT // 2):
                    mod_step(M_EARLY + 1, i, KT // 2 * j + k)

            with dve.Fori(0, turns - 1) as i:
                ch.enter(i, 2)
                for j in range(2):
                    shift(q0 + j, i, flat(s_kv, 2 * i + j), 2 * i + T_K + j, between=lambda: mods(i, j))
            ch.leave(turns - 1)
            for j in range(2):
                e = 2 * (turns - 1) + j
                shift(q0 + e, 0, s_kv[:, e, :], T_K + e, last=j == 1, between=lambda: mods(turns - 1, j))
            mod_out(turns, 4, M_GT1 + 4 * M_EARLY, 2)
            dve.wait_ge(m_out, turns + 2)
            ch.link(STT(out=amod2[:, :], in0=modc[:, M_SC2:M_SC2 + KT, 0], scalar=1.0, in1=vec[:, V_GMLP:V_GMLP + KT],
                        op0=ALU.add, op1=ALU.mult))

            dve.wait_ge(s_sink, 16)
            with dve.Fori(0, NQ) as h:
                ch.enter(h, 4)
                for t in range(2):
                    dve.wait_ge(a_sc, 2 * h + t + 1)
                    ins = TT(sc[:, t, :], PS[3 + t][:, :], amask[:, t, :], ALU.add)
                ch.link(ins)
                ch.link(nc.vector.tensor_reduce(ast[:, 0:2], sc[:, :, :], AX.X, ALU.max))
                ch.link(TT(ast[:, 12:14], ast[:, 0:2], sink[:, bass.ds(h, 1)].to_broadcast([P, 2]), ALU.max))
                TS(ast[:, 2:4], ast[:, 12:14], -1.0, None, ALU.mult).then_inc(a_lg, 1)
                dve.wait_ge(a_ex, 4 * h + 4)
                ch.link(TT(ast[:, 8:10], ast[:, 4:6], ast[:, 6:8], ALU.add))
                nc.vector.reciprocal(ast[:, 10:12], ast[:, 8:10]).then_inc(a_rc, 1)
                dve.wait_ge(a_rc, h + 1)
                for t in range(2):
                    TS(sc[:, t, :], sc[:, t, :], ast[:, 10 + t:11 + t], None, ALU.mult).then_inc(a_pr, 1)
            ch.leave(NQ)

            dve.wait_ge(a_oo, NQ + 1)
            dve.wait_ge(slab_done, SLAB)
            for d in range(2):
                ch.link(nc.vector.memset(ep[d][:, :, d * L:d * L + 1], 1.0))
            keys_of = lambda t: flat(s_kv, t)
            c3 = lambda t: t.rearrange("p (c t) -> p c t", t=L)

            def prep_params(t):
                if not fresh(t):
                    dve.wait_ge(g_sg, 4 * t)
                nc.vector.tensor_copy(pc[:, 0:9], prm[:, P_FT:P_FT + 9 * FT].rearrange("p (v f) -> p v f", f=FT)[:, :, bass.ds(t, 1)]
                                      .rearrange("p v a -> p (v a)")).then_inc(g_pc, 1)
                dve.wait_ge(g_pc, t + 1)
                ch.link(TS(pc[:, 9:10], pc[:, C_KA:C_KA + 1], -1.0, 1.0, ALU.mult, ALU.add))

            def prep_inverse_norms(t):
                dve.wait_ge(g_rt, t + 1)
                ch.link(TS(kd[0][:, :], kd[0][:, :], 1e-12, None, ALU.max))
                ch.link(nc.vector.reciprocal(kd[0][:, :], kd[0][:, :]))

            def prep_unit_keys(t):
                STT(out=kk[:, :], in0=keys_of(t), scalar=pc[:, C_KK:C_KK + 1], in1=kd[0][:, :], op0=ALU.mult, op1=ALU.mult).then_inc(g_kk, 1)
                dve.wait_ge(g_kk, t + 1)

            def prep_sums(t, d):
                dve.wait_ge(g_sg, 4 * t + d + 1)
                if not fresh(t):
                    dve.wait_ge(g_bb, 4 * t)
                step = 1 if d == 0 else -1
                nc.vector.tensor_tensor_scan(cum[d][:, ::step], rst[d][:, ::step], sgt[d][:, ::step], 0.0, ALU.mult, ALU.add
                                             ).then_inc(g_cum, 1)

            def prep_rates(t, d):
                dve.wait_ge(g_sg, 4 * t + d + 3)
                ch.link(TS(kd[d][:, :], sat[d][:, :], pc[:, C_KA:C_KA + 1], pc[:, 9:10], ALU.mult, ALU.add))
                TT(sat[d][:, :], sat[d][:, :], kk[:, :], ALU.mult).then_inc(g_sa, 1)
                ch.link(TT(kd[d][:, :], kd[d][:, :], keys_of(t), ALU.mult))

            def prep_key_blocks(t, d):
                dve.wait_ge(g_ex, 4 * t + 2 * d + 2)
                if not fresh(t):
                    dve.wait_ge(g_tm, 4 * LEVELS * t)
                for hs in halves:
                    last = TT(bdk[d][hs, :, hs], c3(kd[d][hs, :]), c3(cum[d][hs, :]), ALU.mult)
                last.then_inc(g_kb, 1)
                if d == 1:
                    ch.link(TT(kb[:, :], kd[0][:, CTX:TOK], kd[1][:, CTX:TOK], ALU.add))

            def prep_reads(t, d):
                dve.wait_ge(g_ex, 4 * t + 2 * d + 1)
                if not fresh(t):
                    dve.wait_ge(g_ba, 6 * t)
                TT(ar[d][:, HC:NCH, L:P], c3(flat(s_r, t)), ep[d][:, HC:NCH, 1 - d:1 - d + L], ALU.mult)
                STT(out=ar[d][:, :, 0:L], in0=c3(kk[:, :]), scalar=-1.0, in1=ep[d][:, :, d:d + L],
                    op0=ALU.mult, op1=ALU.mult).then_inc(g_bd, 1)
                dve.wait_ge(g_bd, 2 * t + d + 1)

            PREP = {0: [prep_inverse_norms], 1: [prep_unit_keys, lambda t: prep_sums(t, 0)],
                    2: [lambda t: prep_sums(t, 1), lambda t: prep_rates(t, 0)],
                    3: [lambda t: prep_rates(t, 1), lambda t: prep_reads(t, 0)], 4: [lambda t: prep_reads(t, 1)]}

            PAIR = [(2, 5, 7), (0, 1, 3)]
            low_, high_ = slice(0, HC), slice(HC, NCH)
            per = lambda m: m.unsqueeze(1).to_broadcast([P, HC, m.free_size()])
            wide = lambda b: PS[b][:, :].rearrange("p (c n) -> p c n", n=P)

            def bd(dst, src, d, cs):
                m = strict[d].rearrange("p (h t) -> p h t", h=2).unsqueeze(1).to_broadcast([P, HC, 2, L])
                return TT(dst[d][:, cs, :].rearrange("p c (h t) -> p c h t", h=2),
                          src.unsqueeze(2).to_broadcast([P, HC, 2, L]), m, ALU.mult)

            context = lambda d, k: PS[PAIR[d][0]][:, k * SEQ:(k + 1) * SEQ].rearrange("p (c n) -> p c n", n=L)

            def masked_start(t, d):
                if not fresh(t):
                    dve.wait_ge(g_tm, 4 * LEVELS * t)
                    dve.wait_ge(g_ze, 4 * LEVELS * t)
                for cs, src, k in ((low_, context(d, 0), 1), (high_, wide(PAIR[d][1])[:, :, 0:L], 2)):
                    dve.wait_ge(g_am, 6 * t + 3 * d + k)
                    ch.link(bd(dd, src, d, cs))
                    ch.link(TT(zn[d][:, cs, :], dd[d][:, cs, :], per(lv1[d]), ALU.mult))
                    TT(zn[d][:, cs, :], zn[d][:, cs, :], per(ident), ALU.add).then_inc(g_z1, 1)

            def masked_rest(t, d):
                TT(arb[d][:, :, :], wide(PAIR[d][1])[:, :, L:P], per(incl[d]), ALU.mult)
                bd(aak, context(d, 1), d, low_)
                dve.wait_ge(g_am, 6 * t + 3 * d + 3)
                bd(aak, wide(PAIR[d][2])[:, :, 0:L], d, high_)
                TT(ark[d][:, :, :], wide(PAIR[d][2])[:, :, L:P], per(incl[d]), ALU.mult).then_inc(g_ae, 1)

            def read_y(r):
                dve.wait_ge(c_yd, 8 * r + 8)
                nc.vector.tensor_copy(yb[:, 0, :], PS[6][:, 0:SEQ]).then_inc(r_yb, 1)
                ch.link(nc.vector.tensor_copy(pcr[:, :], prm[:, P_FT:P_FT + 9 * FT].rearrange("p (v f) -> p v f", f=FT)
                                              [:, C_LNW:C_LNB + 1, bass.ds(r, 1)].rearrange("p v a -> p (v a)")))

            def read_centre(r):
                dve.wait_ge(r_mu, r + 1)
                STT(out=yb[:, 0, :], in0=PS[5][:, 0:SEQ], scalar=-1.0 / L, in1=yb[:, 0, :], op0=ALU.mult, op1=ALU.add).then_inc(r_yc, 1)
                STT(out=yb[:, 1, :], in0=PS[5][:, SEQ:TOK], scalar=0.5, in1=flat(s_kv, r + FT)[:, CTX:TOK], op0=ALU.mult, op1=ALU.mult
                    ).then_inc(r_bm, 1)

            def read_variance(r):
                dve.wait_ge(r_var, r + 1)
                TS(yq[:, 1, :], PS[2][:, 0:SEQ], 1.0 / L, GN_EPS, ALU.mult, ALU.add).then_inc(r_vt, 1)

            def read_mix(r):
                dve.wait_ge(r_sd, r + 1)
                ch.link(nc.vector.reciprocal(yq[:, 1, :], yq[:, 0, :]))
                ch.link(TT(yb[:, 0, :], yb[:, 0, :], yq[:, 1, :], ALU.mult))
                ch.link(TS(yb[:, 0, :], yb[:, 0, :], pcr[:, 0:1], pcr[:, 1:2], ALU.mult, ALU.add))
                ch.link(TT(yb[:, 0, :], yb[:, 0, :], yb[:, 1, :], ALU.add))
                TT(flat(mixt, r + NQ), yb[:, 0, :], gg[:, :], ALU.mult).then_inc(ft_done, 1)
                dve.wait_ge(ft_done, r + 1)

            def keep_bonus(i):
                dve.wait_ge(g_gg, i + 1)
                if not fresh(i):
                    dve.wait_ge(r_mv, 2 * i)
                STT(out=bonus[:, :], in0=flat(s_r, i), scalar=pc[:, C_RK:C_RK + 1], in1=kb[:, :], op0=ALU.mult, op1=ALU.mult).then_inc(r_bo, 1)
                nc.vector.tensor_copy(ggh[:, :], ggn[:, :]).then_inc(r_gg, 1)
                dve.wait_ge(r_gg, i + 1)
                dve.wait_ge(r_bo, i + 1)

            def turn(i, read, prep):
                if read:
                    read_y(i - 1)
                masked_start(i, 1)
                for d in range(2):
                    masked_rest(i, d)
                keep_bonus(i)
                if prep:
                    prep_params(i + 1)
                for l in range(LEVELS):
                    for s, (d, g) in enumerate(STREAMS):
                        dve.wait_ge(g_tm, 4 * LEVELS * i + 4 * l + s + 1)
                        TT(bdb[d][:, HC * g:HC * g + HC, :], PS[LBANK[s]][:, :].rearrange("p (c n) -> p c n", n=P),
                           per(lvt[d][l]), ALU.mult).then_inc(g_te, 1)
                    for s, (d, g) in enumerate(STREAMS):
                        cs = slice(HC * g, HC * g + HC)
                        dve.wait_ge(g_zm, 4 * LEVELS * i + 4 * l + s + 1)
                        TT(zz[d][:, cs, :], (zz if l else zn)[d][:, cs, :], PS[LBANK[s]][:, :].rearrange("p (c n) -> p c n", n=P), ALU.add
                           ).then_inc(g_ze, 1)
                    if prep:
                        for step in PREP.get(l, ()):
                            step(i + 1)
                for n in range(NCH):
                    for d in range(2):
                        dve.wait_ge(c_u, 2 * NCH * i + 2 * n + d + 1)
                        nc.vector.tensor_copy(U_[d][:, :], PS[3 * d + 1][:, 0:P]).then_inc(c_uo, 1)
                    if n < NCH - 1:
                        for d in range(2):
                            ck = chunk(d, n)
                            dve.wait_ge(c_s, 2 * (NCH - 1) * i + 2 * n + d + 1)
                            e = elast[d][:, ck:ck + 1]
                            if n == 0:
                                dve.wait_ge(g_el, 2 * i + d + 1)
                                TS(S_[d][:, :], PS[3 * d][:, 0:P], e, None, ALU.mult).then_inc(c_so, 1)
                            else:
                                dve.wait_ge(c_se, 2 * (NCH - 2) * i + 2 * n + d - 1)
                                STT(out=S_[d][:, :], in0=PS[3 * d][:, 0:P], scalar=e, in1=Se[d][:, :], op0=ALU.mult, op1=ALU.add
                                    ).then_inc(c_so, 1)
                    if prep and n in (0, 3):
                        prep_key_blocks(i + 1, n // 3)
                    if read and n == 1:
                        read_centre(i - 1)
                    if read and n == 2:
                        read_variance(i - 1)
                    if read and n == 4:
                        read_mix(i - 1)
                    if prep and n == NCH - 1:
                        masked_start(i + 1, 0)

            prep_params(0)
            for l in range(LEVELS):
                for step in PREP.get(l, ()):
                    step(0)
            for d in range(2):
                prep_key_blocks(0, d)
            masked_start(0, 0)
            turn(0, False, True)
            with dve.Fori(1, FT - 1) as i:
                ch.enter(i, DVE_LINKS, 1)
                turn(i, True, True)
            ch.leave(FT - 2)
            turn(FT - 1, True, False)
            read_y(FT - 1)
            read_centre(FT - 1)
            read_variance(FT - 1)
            read_mix(FT - 1)

            dve.wait_ge(ft_done, FT)
            ch.link(nc.vector.memset(ones[:, :], 1.0))
            nc.vector.memset(gates[:, 1, :], 0.0).then_inc(e_zero, 1)
            for t in range(4):
                dve.wait_ge(d_mh, t + 1)
                TT(h2l[:, 4 * t:4 * t + 4, :], mixt[:, 4 * t:4 * t + 4, :], h2h[:, 4 * t:4 * t + 4, :].bitcast(F32),
                   ALU.subtract).then_inc(d_ml, 1)
            for n in range(KT):
                if n >= 2:
                    dve.wait_ge(d_gm, n - 1)
                TS(diag[:, n % 2, :], ident, modc[:, M_GT1 + n, 0:1], None, ALU.mult).then_inc(d_dg, 1)
            dve.wait_ge(d_gp, 32)
            dve.wait_ge(d_gm, KT)
            for b in range(4):
                part = slice(b * 512, b * 512 + 512)
                TT(gates[:, 0, part], PS[b][:, :], gpost[:, part], ALU.mult).then_inc(d_gt, 1)
            with dve.Fori(0, KT // 2) as i:
                for j in range(2):
                    low(M_OUT + j, i)

            dve.wait_ge(d_ss, 2)
            TS(stat[:, 14:16], stat[:, 12:14], 1.0 / D, EPS, ALU.mult, ALU.add).then_inc(d_rt, 1)
            dve.wait_ge(d_ss, 3)
            ch.link(nc.vector.reciprocal(stat[:, 18:20], stat[:, 16:18]))
            dve.wait_ge(d_x, 32)
            for t in range(2):
                ch.link(STT(out=mm_[:, t, :], in0=mm_[:, t, :], scalar=stat[:, 18 + t:19 + t], in1=gates[:, 0, :],
                            op0=ALU.mult, op1=ALU.mult))
                TT(x1[:, t, :], x1[:, t, :], mm_[:, t, :], ALU.add).then_inc(d_x1, 1)
            dve.wait_ge(d_ss, 5)
            TS(stat[:, 22:24], stat[:, 20:22], 1.0 / D, EPS, ALU.mult, ALU.add).then_inc(d_rt, 1)
            dve.wait_ge(d_ss, 6)
            ch.link(nc.vector.reciprocal(stat[:, 18:20], stat[:, 24:26]))
            for t in range(2):
                TS(mm_[:, t, :], x1[:, t, :], stat[:, 18 + t:19 + t], None, ALU.mult).then_inc(d_xh, 1)

            def h2_low(kt):
                dve.wait_ge(d_hh, kt + 1)
                TT(h2l[:, kt, :], hm2[:, kt % 2, :], h2h[:, kt, :].bitcast(F32), ALU.subtract).then_inc(d_hl, 1)

            for kt in range(KT):
                dve.wait_ge(d_tr, kt + 1)
                if kt >= 2:
                    dve.wait_ge(d_hl, kt - 1)
                TS(hm2[:, kt % 2, :], PS[kt % 4][:, 0:SEQ], amod2[:, kt:kt + 1], modc[:, M_SH2 + kt, 0:1], ALU.mult, ALU.add
                   ).then_inc(d_hm, 1)
                if kt:
                    h2_low(kt - 1)
            h2_low(KT - 1)
            low(M_IN)
            def gate_out(cb):
                dve.wait_ge(e_red, cb + 1)
                part = slice(cb * 512, (cb + 1) * 512)
                TT(gates[:, 1, part], PS[2 + cb][:, :], gpost2[:, part], ALU.mult).then_inc(e_gt, 1)

            dve.wait_ge(e_bias, 16)
            for cb in range(4):
                with dve.Fori(0, KT // 4) as i:
                    for j in range(4):
                        low(M_IN + KT * cb + j + 1, 2 * i)
                        if j % 2 == 0:
                            dve.wait_ge(eb_landed[j // 2], 16 * i + 16 * (4 * cb + 1))
                        dve.wait_ge(e_acc, 4 * i + (KT * cb + j + 4))
                        acc = gates[:, 1, cb * 512:(cb + 1) * 512]
                        STT(out=acc, in0=eb[j // 2][:, j % 2, :], scalar=silc[:, bass.ds(4 * i + j, 1), 0], in1=acc,
                            op0=ALU.mult, op1=ALU.add).then_inc(e_acc, 1)
                if cb:
                    gate_out(cb - 1)
            gate_out(3)

            def hidden_low(i, j):
                dve.wait_ge(f_fh, 2 * i + j + 1)
                TT(fsl[j][:, :], flat(ffh, 2 * i + j), fsh[j][:, :].bitcast(F32), ALU.subtract).then_inc(f_fl, 1)

            with dve.Fori(0, F_FF // 2 - 1) as i:
                for j in range(2):
                    hidden_low(i, j)
                    low(M_MO + j + 1, i)
            for j in range(2):
                hidden_low(F_FF // 2 - 1, j)
                if j == 0:
                    low(M_END - 1)
            dve.wait_ge(o_ss, 2)
            TS(stat[:, 28:30], stat[:, 26:28], 1.0 / D, EPS, ALU.mult, ALU.add).then_inc(o_rt, 1)
            dve.wait_ge(o_ss, 3)
            ch.link(nc.vector.reciprocal(stat[:, 18:20], stat[:, 30:32]))
            for t in range(2):
                ch.link(STT(out=ffo[:, t, :], in0=ffo[:, t, :], scalar=stat[:, 18 + t:19 + t], in1=gates[:, 1, :],
                            op0=ALU.mult, op1=ALU.mult))
                TT(fin[:, t, :], ffo[:, t, :], x1[:, t, :], ALU.add).then_inc(o_fin, 1)

        @block.tensor
        def _(pe):
            mm, tr = nc.tensor.matmul, nc.tensor.transpose
            pe.sem_inc(ada_used, 4)
            pe.sem_inc(a_qT, 1)
            pe.wait_ge(s_const, 16)
            pe.wait_ge(s_rows, 16 * 14)
            tr(PS[0][:, 0:N_PRM], prow[0:N_PRM, 0, :], ident[0:N_PRM, 0:N_PRM])
            tr(PS[0][:, 128:192], prow[0:64, 1, :], ident[0:64, 0:64])
            tr(PS[0][:, 192:192 + N_ADA], prow[0:N_ADA, 2, :], ident[0:N_ADA, 0:N_ADA]).then_inc(prm_T, 1)
            pe.wait_ge(silu_done, 1)
            pe.wait_ge(prm_done, 3)

            def ada_rows(i, slots, first=False, final=False):
                for k in slots:
                    pe.wait_ge(ada_landed[k], 16 * i + 16)
                    for b in range(3):
                        last = mm(PS[4 * (k % 2) + b][0:2, :], silc[:, 2 * i + k // 2, :], ada[k][:, b * 512:(b + 1) * 512], start=first and k < 2, stop=final and k >= 2)
                    last.then_inc(ada_used, 1)

            for i in range(KT // 2):
                ada_rows(i, range(4), first=i == 0, final=i == KT // 2 - 1)
            pe.wait_ge(ada_pick, 2)
            pe.wait_ge(ada_dve, 2 * KT + 4)
            for h in range(2):
                for j in range(2):
                    last = mm(PS[4 * h + 3][0:2, :], pick[:, j, :], aacc[:, h, j, :], start=j == 0, stop=j == 1)
                last.then_inc(ada_sum, 1)
            pe.wait_ge(row_out, 8)
            pe.sem_inc(pe_go, 1)
            for k in range(32):
                t_ = tr(PS[0][:, 2 * k:2 * k + 2], modrow[:, k * P:(k + 1) * P], ident[0:2, 0:2])
            t_.then_inc(row_T, 1)
            pe.wait_ge(xhat_done, 4)
            for kt in range(KT):
                if kt >= 4:
                    pe.wait_ge(hm_done, kt - 3)
                for t in range(4):
                    t_ = tr(PS[1 + kt % 4][:, t * P:(t + 1) * P], xs[:, t, kt * P:(kt + 1) * P], ident)
                t_.then_inc(xT_done, 1)

            def parts(hi, lo, s, w):
                return ((hi, whi[s][:, w]), (lo, whi[s][:, w]), (hi, wlo[s][:, w]))

            pe.wait_ge(hl_done, KT)
            for kt in range(KT):
                s = kt % 2
                pe.wait_ge(wlo_ready, kt + 1)
                groups = [(PS[t], t, slice(1024, 1536)) for t in range(4)]
                groups += [(PS[4 + 2 * t + q], 2 + t, slice(q * 512, (q + 1) * 512)) for t in range(2) for q in range(2)]
                for bank, t, w in groups:
                    ts = slice(t * P, (t + 1) * P)
                    for n, (a_, b_) in enumerate(parts(hth[:, kt, ts], htl[:, kt, ts], s, w)):
                        last = mm(bank[:, :], a_, b_, start=kt == 0 and n == 0, stop=kt == KT - 1 and n == 2)
                last.then_inc(w_used, 1)

            def slab_tile(q, i, tok):
                m = M_SLAB + q
                s = m % 2
                n = tok.stop - tok.start
                pe.wait_ge(wlo_ready, 2 * i + m + 1)
                if q >= 2:
                    pe.wait_ge(slab_done, 2 * i + q - 1)
                else:
                    pe.wait_ge(ctx_out, 2 * q + 2)
                for kt in range(KT):
                    w = slice(kt * P, (kt + 1) * P)
                    for k, (a_, b_) in enumerate(parts(hth[:, kt, tok], htl[:, kt, tok], s, w)):
                        last = mm(PS[q % 2][:, 0:n], b_, a_, start=kt == 0 and k == 0, stop=kt == KT - 1 and k == 2)
                last.then_inc(w_used, 1)

            lat, both = slice(CTX, TOK), slice(0, TOK)
            for q, tok in enumerate((lat, both, both)):
                slab_tile(q, 0, tok)
            q0, turns, _ = SLAB_LOOPS[0]
            with pe.Fori(0, turns) as i:
                for j in range(2):
                    slab_tile(q0 + j, i, lat)

            def mod_sum(acc, k0):
                for k in range(4):
                    last = mm(PS[2][:, k0 + k:k0 + k + 1], acc[:, k * P:(k + 1) * P], onec[:, :], start=True, stop=True)
                return last

            pe.wait_ge(rot_out, 1)
            pe.wait_ge(m_acc, KT * (M_EARLY + 1))
            for g in range(M_EARLY):
                last = mod_sum(macc[g], 4 * g)
            last.then_inc(m_red, 1)
            q0, turns, _ = SLAB_LOOPS[1]
            with pe.Fori(0, turns) as i:
                pe.wait_ge(m_acc, KT * i + KT * (M_EARLY + 1))
                pe.wait_ge(m_out, i + 1)
                mod_sum(macc[M_EARLY], 0).then_inc(m_red, 1)
                for j in range(2):
                    slab_tile(q0 + j, i, both)
            pe.wait_ge(m_acc, KT * M_GROUPS)
            pe.wait_ge(m_out, turns + 1)
            mod_sum(macc[M_EARLY], 0).then_inc(m_red, 1)

            pe.wait_ge(m_out, turns + 2)
            pe.wait_ge(rot_out, 1)
            pe.wait_ge(slab_done, SLAB)
            for g in range(NKV):
                for t in range(4):
                    t_ = tr(PS[g][:, t * P:(t + 1) * P], ktk[:, t, g * HD:(g + 1) * HD], ident)
                t_.then_inc(kT_done, 1)
            pe.wait_ge(kT_out, 2)
            for g in range(NKV):
                with pe.Fori(0, GQ) as hh:
                    h = hh + g * GQ
                    pe.wait_ge(a_qh, h + 1)
                    for t in range(2):
                        t_ = tr(PS[2][:, t * P:(t + 1) * P], qh[:, t, :], ident)
                    t_.then_inc(a_qT, 1)
                    pe.wait_ge(a_qTo, h + 1)
                    for t in range(2):
                        mm(PS[3 + t][:, :], qT[:, t, :], ktr[:, g, :], start=True, stop=True).then_inc(a_sc, 1)
                    for t in range(2):
                        pe.wait_ge(a_pr, 2 * h + t + 1)
                        for k in range(4):
                            t_ = tr(PS[5 + t][:, k * P:(k + 1) * P], sc[:, t, k * P:(k + 1) * P], ident)
                        t_.then_inc(a_pT, 1)
                    pe.wait_ge(a_oo, h + 1)
                    for t in range(2):
                        pe.wait_ge(a_pTo, 2 * h + t + 1)
                        for k in range(4):
                            last = mm(PS[7][:, t * P:(t + 1) * P], vtk[:, k, g * HD:(g + 1) * HD], pT[:, t, k * P:(k + 1) * P],
                                      start=k == 0, stop=k == 3)
                    last.then_inc(a_o, 1)

            pe.wait_ge(t_lora, 2)
            pe.wait_ge(a_oo, NQ + 1)
            def prep_norms(t):
                pe.wait_ge(g_kq, t + 1)
                mm(PS[2][:, :], ones_bd, sgt[0][:, :], start=True, stop=True).then_inc(g_nr, 1)

            def prep_lora(t, k):
                if k == 0:
                    pe.wait_ge(g_w, 48 * t + 48)
                if k == 2:
                    pe.wait_ge(g_rt, t + 1)
                if k > 2:
                    pe.wait_ge(g_sg, 4 * t + k - 2)
                if k < 4:
                    src, hs = (s_w, s_a)[k // 2], halves[k % 2]
                    ins = mm(PS[(5, 7, 2, 5)[k]][:, :], wsl[hs, k // 2, :], src[hs, :], start=True, stop=True)
                else:
                    ins = mm(PS[7][:, 0:SEQ], wsl[:, 2, :], s_g[:, :], start=True, stop=True)
                ins.then_inc(g_lo, 1)

            PAIR = [(2, 5, 7), (0, 1, 3)]

            def pair_products(t, d):
                pe.wait_ge(g_bb, 4 * t + 2 * d + 2)
                pe.wait_ge(g_kb, 2 * t + d + 1)
                pe.wait_ge(g_bd, 2 * t + d + 1)
                if d == 0:
                    pe.wait_ge(g_sg, 4 * t + 4)
                    pe.wait_ge(g_gg, t + 1)
                for k, lhs in enumerate((bdb[d], bdk[d])):
                    for c_ in range(HC):
                        last = mm(PS[PAIR[d][0]][:, k * SEQ + c_ * L:k * SEQ + (c_ + 1) * L], lhs[:, c_, :], ar[d][:, c_, 0:L],
                                  start=True, stop=True)
                last.then_inc(g_am, 1)
                for k, lhs in enumerate((bdb[d], bdk[d])):
                    for c_ in range(HC):
                        last = mm(PS[PAIR[d][1 + k]][:, c_ * P:(c_ + 1) * P], lhs[:, HC + c_, :], ar[d][:, HC + c_, :],
                                  start=True, stop=True)
                    last.then_inc(g_am, 1)

            PREP = {0: [prep_norms, lambda t: prep_lora(t, 0)], 1: [lambda t: prep_lora(t, 1), lambda t: prep_lora(t, 2)],
                    2: [lambda t: prep_lora(t, 3), lambda t: prep_lora(t, 4)]}

            def read_means(r):
                pe.wait_ge(r_yb, r + 1)
                pe.wait_ge(r_mv, 2 * r + 2)
                mm(PS[5][:, :], ones_bd, yb[:, :, :].rearrange("p a n -> p (a n)"), start=True, stop=True).then_inc(r_mu, 1)

            def read_variances(r):
                pe.wait_ge(r_sq, r + 1)
                pe.wait_ge(r_bm, r + 1)
                mm(PS[2][:, 0:SEQ], ones_bd, yq[:, 0, :], start=True, stop=True).then_inc(r_var, 1)

            def y_known(n, d):
                c_ = chunk(d, n) - HC
                y = PS[6][:, c_ * L:(c_ + 1) * L]
                mm(y, S_[d][:, :], rch[d][:, c_, :], start=n == HC and d == 0, stop=False)
                mm(y, vt[:, HC + c_, :], ark[d][:, c_, :], start=False, stop=False)

            def y_last(n, d):
                c_ = chunk(d, n) - HC
                mm(PS[6][:, c_ * L:(c_ + 1) * L], U_[d][:, :], arb[d][:, c_, :], start=False,
                   stop=n == NCH - 1 and d == 1).then_inc(c_yd, 1)

            def turn(i, read, prep):
                pair_products(i, 1)
                if read:
                    pe.wait_ge(r_yb, i)
                for q, (d, k, g) in enumerate(TURNED):
                    if q >= 2:
                        pe.wait_ge(g_to, 10 * i + q - 1)
                    for c_ in range(HC):
                        t_ = tr(PS[4 + q % 2 * 2][:, c_ * P:(c_ + 1) * P], (bdk, bdb)[k][d][:, HC * g + c_, :], ident)
                    t_.then_inc(g_tr, 1)
                pe.wait_ge(g_vb, 2 * i + 2)
                for g in range(2):
                    pe.wait_ge(g_to, 10 * i + 7 + g)
                    for c_ in range(HC):
                        t_ = tr(PS[4 + 2 * g][:, c_ * P:(c_ + 1) * P], vbd[:, HC * g + c_, :], ident)
                    t_.then_inc(g_tr, 1)

                def turn_x(z, s, d, g):
                    for k in range(HC):
                        t_ = tr(PS[LBANK[s]][:, k * P:(k + 1) * P], z[d][:, HC * g + k, :], ident)
                    t_.then_inc(g_xt, 1)

                for s, (d, g) in enumerate(STREAMS):
                    if s < 2:
                        pe.wait_ge(g_to, 10 * i + 9 + s)
                    if s == 2:
                        pe.wait_ge(g_ae, 2 * i + 2)
                    pe.wait_ge(g_z1, 4 * i + s + 1)
                    turn_x(zn, s, d, g)
                for l in range(LEVELS):
                    n = 4 * LEVELS * i + 4 * l
                    for s, (d, g) in enumerate(STREAMS):
                        pe.wait_ge(g_xo, n + s + 1)
                        for k in range(HC):
                            ck = HC * g + k
                            last = mm(PS[LBANK[s]][:, k * P:(k + 1) * P], dd[d][:, ck, :], bdk[d][:, ck, :], start=True, stop=True)
                        last.then_inc(g_tm, 1)
                    if prep:
                        for step in PREP.get(l, ()):
                            step(i + 1)
                    for s, (d, g) in enumerate(STREAMS):
                        pe.wait_ge(g_te, n + s + 1)
                        for k in range(HC):
                            ck = HC * g + k
                            last = mm(PS[LBANK[s]][:, k * P:(k + 1) * P], bdb[d][:, ck, :], (zz if l else zn)[d][:, ck, :], start=True, stop=True)
                        last.then_inc(g_zm, 1)
                    if l < LEVELS - 1:
                        for s, (d, g) in enumerate(STREAMS):
                            pe.wait_ge(g_ze, n + s + 1)
                            turn_x(zz, s, d, g)
                pe.wait_ge(g_ze, 4 * LEVELS * i + 4 * LEVELS)
                pe.wait_ge(g_ba, 6 * i + 6)
                for n in range(NCH):
                    for d in range(2):
                        ck = chunk(d, n)
                        if n:
                            pe.wait_ge(c_so, 2 * (NCH - 1) * i + 2 * n + d - 1)
                            mm(PS[3 * d][:, 0:P], bda[d][:, ck, :], S_[d][:, :], start=True, stop=False)
                        mm(PS[3 * d][:, 0:P], aak[d][:, ck, :], vt[:, ck, :], start=n == 0, stop=True).then_inc(c_p, 1)
                    if read and n == 0:
                        read_means(i - 1)
                    if read and n == 2:
                        read_variances(i - 1)
                    if prep and n == 5:
                        if read:
                            pe.wait_ge(r_vt, i)
                        pair_products(i + 1, 0)
                    for d in range(2):
                        ck = chunk(d, n)
                        pe.wait_ge(c_po, 2 * NCH * i + 2 * n + d + 1)
                        mm(PS[3 * d + 1][:, 0:P], zz[d][:, ck, :], P_[d][:, :], start=True, stop=True).then_inc(c_u, 1)
                    if n < NCH - 1:
                        for d in range(2):
                            ck = chunk(d, n)
                            mm(PS[3 * d][:, 0:P], bkt[d][:, ck, :], vt[:, ck, :], start=True, stop=False)
                    if n >= HC:
                        for d in range(2):
                            y_known(n, d)
                    for d in range(2):
                        pe.wait_ge(c_uo, 2 * NCH * i + 2 * n + d + 1)
                        if n < NCH - 1:
                            mm(PS[3 * d][:, 0:P], bbt[d][:, chunk(d, n), :], U_[d][:, :], start=False, stop=True).then_inc(c_s, 1)
                    if n >= HC:
                        for d in range(2):
                            y_last(n, d)

            for l in range(LEVELS):
                for step in PREP.get(l, ()):
                    step(0)
            pair_products(0, 0)
            turn(0, False, True)
            with pe.Fori(1, FT - 1) as i:
                turn(i, True, True)
            turn(FT - 1, True, False)
            read_means(FT - 1)
            read_variances(FT - 1)

            pe.wait_ge(d_ml, 4)
            for n in range(KT):
                pe.wait_ge(d_dg, n + 1)
                mm(PS[n // 4][:, n % 4 * P:(n % 4 + 1) * P], ones[:, :], diag[:, n % 2, :], start=True, stop=True).then_inc(d_gm, 1)
            pe.wait_ge(d_gt, 4)
            for kt in range(KT):
                m = M_OUT + kt
                s = m % 2
                pe.wait_ge(wlo_ready, m + 1)
                for b in range(8):
                    ts = slice(b // 4 * P, (b // 4 + 1) * P)
                    w = slice(b % 4 * 512, b % 4 * 512 + 512)
                    for n, (a_, b_) in enumerate(parts(h2h[:, kt, ts], h2l[:, kt, ts], s, w)):
                        last = mm(PS[b][:, :], a_, b_, start=kt == 0 and n == 0, stop=kt == KT - 1 and n == 2)
                last.then_inc(w_used, 1)
            pe.wait_ge(d_out, 8)
            pe.wait_ge(d_xh, 2)
            for kt in range(KT):
                if kt >= 4:
                    pe.wait_ge(d_hm, kt - 3)
                for t in range(2):
                    t_ = tr(PS[kt % 4][:, t * P:(t + 1) * P], mm_[:, t, kt * P:(kt + 1) * P], ident)
                t_.then_inc(d_tr, 1)
            pe.wait_ge(d_hl, KT)
            for cb in range(4):
                with pe.Fori(0, KT // 2) as i:
                    for j in range(2):
                        m = M_IN + KT * cb + j
                        s = m % 2
                        pe.wait_ge(wlo_ready, 2 * i + m + 1)
                        pe.wait_ge(e_re, 2 * i + (KT * cb + j + 1))
                        for kt in range(KT):
                            for k, (a_, b_) in enumerate(parts(h2h[:, kt, :], h2l[:, kt, :], s, slice(kt * P, (kt + 1) * P))):
                                last = mm(PS[j][:, 0:SEQ], b_, a_, start=kt == 0 and k == 0, stop=kt == KT - 1 and k == 2)
                        last.then_inc(w_used, 1)
                pe.wait_ge(e_acc, KT * (cb + 1) + 4)
                mm(PS[2 + cb][:, :], ones[:, :], gates[:, 1, cb * 512:(cb + 1) * 512], start=True, stop=True).then_inc(e_red, 1)
            pe.wait_ge(e_re, F_FF + 2)
            pe.wait_ge(e_gt, 4)

            def mlp_out(i, j, first=False, final=False):
                m = M_MO + j
                s = m % 2
                pe.wait_ge(f_fl, 2 * i + j + 1)
                pe.wait_ge(wlo_ready, 2 * i + m + 1)
                for b in range(8):
                    ts = slice(b // 4 * P, (b // 4 + 1) * P)
                    w = slice(b % 4 * 512, b % 4 * 512 + 512)
                    for n, (a_, b_) in enumerate(parts(fsh[j][:, ts], fsl[j][:, ts], s, w)):
                        last = mm(PS[b][:, :], a_, b_, start=first and n == 0, stop=final and n == 2)
                last.then_inc(w_used, 1)

            for j in range(2):
                mlp_out(0, j, first=j == 0)
            with pe.Fori(1, F_FF // 2 - 1) as i:
                for j in range(2):
                    mlp_out(i, j)
            for j in range(2):
                mlp_out(F_FF // 2 - 1, j, final=j == 1)


_INS = ["x", "c", "ctx", "c_ctx", "w_ada", "b_ada", "g_pre_mix", "g_post_mix", "g_pre_mlp", "g_post_mlp",
        "w_in", "attn_sink", "rwkv_mu_prev", "rwkv_mu_next", "rwkv_w0", "rwkv_w2", "rwkv_a0", "rwkv_a2",
        "rwkv_g2", "rwkv_k_k", "rwkv_k_a", "rwkv_r_k", "rwkv_ln_w", "rwkv_ln_b", "w_out", "w_mlp_in", "w_mlp_out"]


def kernel(**inputs):
    import numpy as _np
    import concourse.bacc as _bacc
    from concourse import mybir as _mybir
    from concourse.bass_utils import run_bass_kernel_spmd as _run

    nc = _bacc.Bacc("TRN2", target_bir_lowering=False, num_devices=1)
    arrays, args = {}, []
    named = [(name, inputs[name]) for name in _INS] + list(zip(("rec_const", "att_const"), shape_constants()))
    for name, a in named:
        a = _np.ascontiguousarray(a)
        arrays[f"in_{name}_dram"] = a
        args.append(nc.dram_tensor(f"in_{name}_dram", a.shape, _mybir.dt.from_np(a.dtype), kind="ExternalInput").ap())
    args.append(nc.dram_tensor("out_0_dram", (1, SEQ, D), F32, kind="ExternalOutput").ap())
    build_program(nc, *args)
    r = _run(nc, [arrays], core_ids=[0])
    return r.results[0]["out_0_dram"]
```

```python
from contextlib import ExitStack

import numpy as np

import concourse.bass as bass
from concourse import mybir

F32 = mybir.dt.float32
F32R = mybir.dt.float32r
ALU = mybir.AluOpType
ACT = mybir.ActivationFunctionType
AX = mybir.AxisListType

P = 128
D = 2048
KT = D // P
SEQ, CTX = 256, 256
TOK = CTX + SEQ
NQ, NKV, HD = 8, 2, 128
GQ = NQ // NKV
ATT_IN = NQ * HD + 2 * NKV * HD
N_ADA = 6 * D // P
SLAB = 27
T_R, T_K, T_V, T_W, T_A, T_G = 0, 8, 16, 24, 25, 26
FT = 8
L = 64
NCH = TOK // L
HC = NCH // 2
LEVELS = 5
F_FF = 4 * D // P
SLOT = 2048
EPS, GN_EPS = 1e-6, 64e-5
DECAY = float(np.exp(-0.5))
NEG = -1e30

P_MUP, P_MUN, P_FT = 0, 27, 54
N_PRM = P_FT + 9 * FT
C_KK, C_KA, C_RK, C_LNW, C_LNB, C_W0, C_A0 = 0, 1, 2, 3, 4, 5, 7
V_C, V_CC, V_GMIX, V_GMLP = 0, 16, 32, 48
M_SH1, M_SC1, M_GT1, M_SH2, M_SC2, M_GT2 = (16 * k for k in range(6))


def shape_constants():
    f = np.float32
    row = np.arange(P)
    head, t = row // L, row % L
    same = head[:, None] == head[None, :]
    ident = np.eye(P, dtype=f)
    ones_bd = same.astype(f)
    strict, incl, lv1, lvt, rst = [], [], [], [], []
    for d in range(2):
        s = t if d == 0 else L - 1 - t
        strict.append((same & (s[:, None] < s[None, :])).astype(f))
        s64 = s[:L]
        incl.append((s[:, None] <= s64[None, :]).astype(f))
        early, late = s[:, None], s[None, :]
        lv1.append((same & (early // 2 == late // 2) & (early < late)).astype(f))
        for level in range(LEVELS):
            b = 2 ** (level + 1)
            later, earlier = s[:, None], s[None, :]
            lvt.append((same & (later // (2 * b) == earlier // (2 * b))
                        & (later // b > earlier // b)).astype(f))
        r = np.ones(TOK, f)
        r[(0 if d == 0 else L - 1)::L] = 0
        rst.append(np.broadcast_to(r, (P, TOK)))
    rec = np.concatenate([ident, ones_bd, *strict, *incl, *lv1, *lvt, *rst], axis=1).astype(f)
    q, k = np.arange(P)[:, None], np.arange(SEQ)[None, :]
    att = np.zeros((P, 2, TOK), f)
    for qt in range(2):
        att[:, qt, CTX:] = np.where(np.abs(k - (q + qt * P)) <= 128, 0.0, NEG)
    n = HD // 4
    inv = (f(10000.0) ** (-np.arange(n, dtype=f) / f(n))).astype(f)
    pos = np.arange(SEQ)
    ar = (pos // 64).astype(f)[:, None] * inv[None]
    ac = (pos % 64).astype(f)[:, None] * inv[None]
    cos = np.concatenate([np.cos(ar), np.cos(ar), np.cos(ac), np.cos(ac)], axis=1)
    sin = np.concatenate([-np.sin(ar), np.sin(ar), -np.sin(ac), np.sin(ac)], axis=1)
    rope = np.stack([cos, sin], axis=1).reshape(2, P, 2, HD).transpose(1, 0, 2, 3)
    attn = np.concatenate([att.reshape(P, -1), rope.reshape(P, -1)], axis=1).astype(f)
    return np.ascontiguousarray(rec), np.ascontiguousarray(attn)


class Chain:

    def __init__(self, eng, sem):
        self.eng, self.sem, self.base, self.n = eng, sem, 0, 0

    def link(self, ins):
        ins.then_inc(self.sem, 1)
        self.n += 1
        self.eng.wait_ge(self.sem, self.base + self.n)

    def enter(self, i, per, first=0):
        self.outer, self.per, self.n0 = self.base, per, self.n
        self.base = i * per + (self.outer + self.n - first * per)
        self.n = 0

    def leave(self, turns):
        assert self.n == self.per, (self.n, self.per)
        self.base, self.n = self.outer + self.n0 + turns * self.per, 0


def build_program(nc, x, c, ctx_tok, c_ctx, w_ada, b_ada, g_pre_mix, g_post_mix, g_pre_mlp, g_post_mlp,
                  w_in, attn_sink, mu_prev, mu_next, w0, w2, a0, a2, g2, k_k, k_a, r_k, ln_w, ln_b,
                  w_out, w_mlp_in, w_mlp_out, rec_const, att_const, out):
    stack = ExitStack()
    with stack:
        sem = lambda name: stack.enter_context(nc.semaphore(name))
        PS = [stack.enter_context(nc.psum_tensor(f"bank{b}", [P, 512], F32)) for b in range(8)]

        end = [16512]

        def place(name, shape, dtype=F32, offset=None):
            size = 4 * int(np.prod(shape[1:]))
            size = (size + 31) // 32 * 32
            if offset is None:
                offset = end[0]
                end[0] += size
            assert offset + size <= nc.sbuf_usable_end, (name, offset, size)
            return nc.alloc_sbuf_tensor_at(name, shape, dtype, offset=offset)

        class Region:

            def __init__(self, offset, size):
                self.at, self.end = offset, offset + size

            def place(self, name, shape, dtype=F32):
                size = (4 * int(np.prod(shape[1:])) + 31) // 32 * 32
                assert self.at + size <= self.end, (name, self.at, size, self.end)
                t = nc.alloc_sbuf_tensor_at(name, shape, dtype, offset=self.at)
                self.at += size
                return t

        at_rec = end[0]
        rec = place("rec", [P, rec_const.shape[1]])
        at = [0]

        def cols(n):
            at[0] += n
            return rec[:, at[0] - n:at[0]]

        ident, ones_bd = cols(P), cols(P)
        strict = [cols(P) for _ in range(2)]
        incl = [cols(L) for _ in range(2)]
        lv1 = [cols(P) for _ in range(2)]
        lvt = [[cols(P) for _ in range(LEVELS)] for _ in range(2)]
        rst = [cols(TOK) for _ in range(2)]
        prm = place("prm", [P, N_PRM])
        mu0 = place("mu0", [P, SLAB])
        vec = place("vec", [P, 64])
        bada = place("bada", [P, N_ADA])
        modc = place("modc", [P, N_ADA, 2])
        silc = place("silc", [P, KT, 2])
        amod = place("amod", [P, 2, KT])
        amod2 = place("amod2", [P, KT])
        stat = place("stat", [P, 32])
        onec = place("onec", [P, 1])
        sqs = place("sqs", [P, 2, 4])
        sink = place("sink", [P, NQ])
        ring_raw = end[0]
        raw = [place(f"raw{s}", [P, SLOT]) for s in range(2)]
        ring_hl = end[0]
        ada = [nc.alloc_sbuf_tensor_at(f"ada{s}", [P, SLOT], F32, offset=ring_hl + s * 4 * SLOT) for s in range(4)]
        whi = [place(f"whi{s}", [P, SLOT], F32R) for s in range(2)]
        wlo = [place(f"wlo{s}", [P, SLOT], F32R) for s in range(2)]
        reg_a = end[0]
        SZ_A, SZ_B = 64 * 1024, 45 * 1024 + 64
        reg_b = reg_a + SZ_A
        reg_c = reg_b + SZ_B
        SZ_C = nc.sbuf_usable_end - reg_c
        ra = Region(reg_a, SZ_A)
        hth = ra.place("hth", [P, KT, TOK], F32R)
        htl = ra.place("htl", [P, KT, TOK], F32R)
        rb = Region(reg_b, SZ_B)
        s_r = rb.place("s_r", [P, FT, SEQ])
        s_kv = rb.place("s_kv", [P, 2 * FT, TOK])
        s_w = rb.place("s_w", [P, TOK])
        s_a = rb.place("s_a", [P, TOK])
        s_g = rb.place("s_g", [P, SEQ])
        rc = Region(reg_c, SZ_C)
        qtk = rc.place("qtk", [P, 2, NQ * HD])
        ktk = rc.place("ktk", [P, 4, NKV * HD])
        vtk = rc.place("vtk", [P, 4, NKV * HD])
        at_ktr = rc.at
        ktr = rc.place("ktr", [P, NKV, TOK])
        att_c = rc.place("att_c", [P, 2 * TOK + 2 * 2 * HD])
        mb = [nc.alloc_sbuf_tensor_at("mb0", [P, 2, 512], F32, offset=at_ktr), rc.place("mb1", [P, 2, 512])]
        mb += [nc.alloc_sbuf_tensor_at(f"mb{2 + k}", [P, 2, 512], F32, offset=at_rec + 2 * P * 4 + 4096 * k) for k in range(2)]
        macc = [nc.alloc_sbuf_tensor_at(f"macc{g}", [P, 512], F32, offset=reg_b + 12 * 1024 + g * 2048) for g in range(3)]
        macc.append(rc.place("macc3", [P, 512]))
        amask = att_c[:, 0:2 * TOK].rearrange("p (a n) -> p a n", a=2)
        rope = att_c[:, 2 * TOK:].rearrange("p (t a n) -> p t a n", t=2, a=2)
        xa = Region(reg_b, SZ_B)
        xs = xa.place("xs", [P, 4, D])
        prow = xa.place("prow", [P, 3, P])
        xb = Region(reg_a, SZ_A)
        modrow = xb.place("modrow", [2, 4096])
        junk = xb.place("junk", [P, D])
        aacc = xb.place("aacc", [P, 2, 2, 512])
        pick = xb.place("pick", [P, 2, 2])
        xc = Region(reg_c, SZ_C)
        hmod = xc.place("hmod", [P, 4, TOK])
        rr = Region(reg_b, SZ_B)
        rot1 = rr.place("rot1", [P, 512])
        rot2 = rr.place("rot2", [P, 512])
        mixt = nc.alloc_sbuf_tensor_at("mixt", [P, KT, SEQ], F32, offset=reg_a)
        ta = Region(reg_a + 16 * 1024, SZ_A - 16 * 1024)
        qh = ta.place("qh", [P, 2, HD])
        qT = ta.place("qT", [P, 2, P])
        sc = ta.place("sc", [P, 2, 2, TOK])
        pT = ta.place("pT", [P, 2, TOK])
        ast = ta.place("ast", [P, 2, 16])
        ga = Region(reg_a + 16 * 1024, SZ_A - 16 * 1024)
        gc = Region(reg_c, SZ_C)
        gh = Region(ring_raw, 48 * 1024)
        dd = [ga.place(f"dd{d}", [P, NCH, P]) for d in range(2)]
        zz = [ga.place(f"zz{d}", [P, NCH, P]) for d in range(2)]
        assert ga.at >= ta.at
        bda = [ga.place(f"bda{d}", [P, NCH, P]) for d in range(2)]
        bdk = [ga.place(f"bdk{d}", [P, NCH, P]) for d in range(2)]
        bdb = [ga.place(f"bdb{d}", [P, NCH, P]) for d in range(2)]
        aak = [ga.place(f"aak{d}", [P, NCH, P]) for d in range(2)]
        bkt = [gh.place(f"bkt{d}", [P, NCH, P]) for d in range(2)]
        bbt = [gh.place(f"bbt{d}", [P, NCH, P]) for d in range(2)]
        ar = [gh.place(f"ar{d}", [P, NCH, P]) for d in range(2)]
        vbd = gh.place("vbd", [P, NCH, P])
        vt = gh.place("vt", [P, NCH, P])
        zn = [gh.place(f"zn{d}", [P, NCH, P]) for d in range(2)]
        Se = [gh.place(f"Se{d}", [P, P]) for d in range(2)]
        ep = [gc.place(f"ep{d}", [P, NCH, L + 1]) for d in range(2)]
        sgt = [gc.place(f"sgt{d}", [P, TOK]) for d in range(2)]
        sat = [gc.place(f"sat{d}", [P, TOK]) for d in range(2)]
        cum = [gc.place(f"cum{d}", [P, TOK]) for d in range(2)]
        kk = gc.place("kk", [P, TOK])
        kd = [gc.place(f"kd{d}", [P, TOK]) for d in range(2)]
        arb = [gc.place(f"arb{d}", [P, HC, L]) for d in range(2)]
        ark = [gc.place(f"ark{d}", [P, HC, L]) for d in range(2)]
        rch = [gc.place(f"rch{d}", [P, HC, L]) for d in range(2)]
        gg, ggn, ggh = gc.place("gg", [P, SEQ]), gh.place("ggn", [P, SEQ]), gc.place("ggh", [P, SEQ])
        bonus = gc.place("bonus", [P, SEQ])
        kb = gh.place("kb", [P, SEQ])
        elast = [gh.place(f"elast{d}", [P, NCH]) for d in range(2)]
        S_ = [gh.place(f"S{d}", [P, P]) for d in range(2)]
        U_ = [gh.place(f"U{d}", [P, P]) for d in range(2)]
        P_ = [gh.place(f"P{d}", [P, P]) for d in range(2)]
        yb = gc.place("yb", [P, 2, SEQ])
        yq = gc.place("yq", [P, 2, SEQ])
        pc, pcr = gc.place("pc", [P, 10]), gc.place("pcr", [P, 2])
        wsl = gh.place("wsl", [P, 3, P])
        ffh = nc.alloc_sbuf_tensor_at("ffh", [P, F_FF, SEQ], F32, offset=reg_a)
        mm_ = nc.alloc_sbuf_tensor_at("mm_", [P, 2, D], F32, offset=reg_a + 16 * 1024)
        gpost = nc.alloc_sbuf_tensor_at("gpost", [P, D], F32, offset=reg_a + 32 * 1024)
        diag = nc.alloc_sbuf_tensor_at("diag", [P, KT, P], F32, offset=reg_a + 40 * 1024)
        masks = Region(at_rec + 2 * P * 4, 4 * (rec_const.shape[1] - 2 * P))
        eb = [masks.place(f"eb{s}", [P, 2, 512]) for s in range(2)]
        ones = masks.place("ones", [P, P])
        hm2 = nc.alloc_sbuf_tensor_at("hm2", [P, 4, SEQ], F32, offset=reg_a + 50 * 1024)
        dg2 = nc.alloc_sbuf_tensor_at("dg2", [P, 2, P], F32, offset=reg_a + 48 * 1024)
        er = Region(reg_b, nc.sbuf_usable_end - reg_b)
        gates = er.place("gates", [P, 2, D])
        h2h = er.place("h2h", [P, KT, SEQ], F32R)
        h2l = er.place("h2l", [P, KT, SEQ], F32R)
        x1 = er.place("x1", [P, 2, D])
        gpost2 = er.place("gpost2", [P, D])
        relu = er.place("relu", [P, 2, SEQ])
        fsh = [er.place(f"fsh{s}", [P, SEQ], F32R) for s in range(2)]
        fsl = [er.place(f"fsl{s}", [P, SEQ], F32R) for s in range(2)]
        junk2 = nc.alloc_sbuf_tensor_at("junk2", [P, D], F32, offset=reg_a + 54 * 1024)
        ffo = nc.alloc_sbuf_tensor_at("ffo", [P, 2, D], F32, offset=reg_a)
        junk3 = nc.alloc_sbuf_tensor_at("junk3", [P, D], F32, offset=reg_a + 16 * 1024)
        fin = nc.alloc_sbuf_tensor_at("fin", [P, 2, D], F32, offset=reg_b + 16 * 1024)

        s_const, s_rows, s_x = sem("constants_landed"), sem("param_rows_landed"), sem("tokens_landed")
        s_attc, s_sink = sem("att_constants_landed"), sem("sink_landed")
        raw_landed = [sem(f"raw{s}_landed") for s in range(2)]
        ada_landed = [sem(f"ada{s}_landed") for s in range(4)]
        ada_used, ada_dve, ada_sum, ada_pick = sem("ada_slot_used"), sem("ada_block_summed"), sem("ada_sums_ready"), sem("pick_ready")
        mb_landed = [sem(f"mod_blocks{s}_landed") for s in range(4)]
        s_masks = sem("masks_landed")
        m_acc, m_red, m_out = sem("mod_block_added"), sem("mod_partitions_summed"), sem("mod_group_out")
        eb_landed = [sem(f"gate_blocks{s}_landed") for s in range(2)]
        e_zero, e_bias, e_acc, e_red, e_gt = (sem("gate_zeroed"), sem("gate_bias_landed"), sem("gate_block_added"),
                                              sem("gate_partitions_summed"), sem("gate2_ready"))
        prm_T, prm_done = sem("params_transposed"), sem("params_in_columns")
        silu_sig, silu_done = sem("silu_sigmoid"), sem("silu_ready")
        row_out, row_T, mod_done = sem("mod_row_out"), sem("mod_transposed"), sem("mod_in_columns")
        ss_done, sq_done, xhat_done = sem("squares_summed"), sem("root_done"), sem("tokens_normed")
        xT_done, hm_done, hh_done, hl_done = sem("tokens_transposed"), sem("modulated"), sem("h_high"), sem("h_low")
        whi_ready, wlo_ready, w_used = sem("weights_high"), sem("weights_low"), sem("weights_used")
        ctx_out, rot_out = sem("context_kv_out"), sem("latent_qkv_out")
        kT_done, kT_out = sem("k_transposed"), sem("kT_out")
        slab_base, slab_done = sem("slab_base"), sem("slab_shifted")
        dve_s, pool_s = sem("vector_chain"), sem("gpsimd_chain")
        a_qh, a_qT, a_qTo, a_sc, a_lg = sem("q_head_copied"), sem("q_transposed"), sem("qT_out"), sem("scores_done"), sem("negmax_ready")
        a_ex, a_pr, a_pT, a_pTo, a_o, a_oo = sem("exps_done"), sem("probs_ready"), sem("probs_transposed"), sem("pT_out"), sem("att_product"), sem("att_out")
        g_w, g_pc, g_kq, g_nr, g_rt, g_kk = sem("lora_landed"), sem("tile_params"), sem("k_squares"), sem("k_norms"), sem("k_roots"), sem("kk_ready")
        g_lo, g_sg, g_cum, g_ex, g_gg = sem("lora_products"), sem("sigmoids"), sem("decay_sums"), sem("decay_exps"), sem("gate_out")
        g_sa, g_bb, g_bd, g_ba = sem("rates_by_k"), sem("block_b_ready"), sem("operands_ready"), sem("block_a_ready")
        g_vb, g_am, g_ae, g_tr, g_to = sem("v_blocks"), sem("chunk_products"), sem("chunk_masked"), sem("tilde_transposed"), sem("tilde_out")
        g_z1, g_xt, g_xo, g_tm, g_te, g_zm, g_ze = (sem("z_started"), sem("x_transposed"), sem("x_out"), sem("t_product"),
                                                    sem("t_masked"), sem("z_product"), sem("z_added"))
        c_se = sem("state_decayed")
        g_kb, r_mv, g_aa = sem("key_blocks_ready"), sem("bonus_and_gate_moved"), sem("level_banks_read")
        g_el, c_p, c_po, c_u, c_uo, c_s, c_so = (sem("last_decays"), sem("p_product"), sem("p_out"), sem("u_product"),
                                                 sem("u_out"), sem("state_product"), sem("state_out"))
        c_yd = sem("y_added")
        r_yb, r_bo, r_gg, r_mu, r_sq, r_bm, r_var, r_vt, r_sd, ft_done = (
            sem("y_out"), sem("bonus_ready"), sem("gate_kept"), sem("y_means"), sem("y_squares"), sem("means_read"),
            sem("y_variances"), sem("y_var_eps"), sem("y_roots"), sem("tile_done"))
        ft_init = sem("zero_blocks")
        t_lora = sem("lora_inputs")
        d_mh, d_ml = sem("mix_high"), sem("mix_low")
        d_pg, o_pg = sem("out_by_gate"), sem("mlp_by_gate")
        hl_pool, hl2_pool = sem("h_low_odd"), sem("h2_low_odd")
        d_out, d_ss, d_rt, d_xh = sem("out_squares_by_bank"), sem("out_squares"), sem("out_roots"), sem("x1_normed")
        d_gp, d_dg, d_gm, d_gt, d_x, d_x1 = sem("gpost_landed"), sem("gate_diag"), sem("gate_rows"), sem("gate_ready"), sem("x_again"), sem("x1_ready")
        d_tr, d_hm, d_hh, d_hl = sem("x1_transposed"), sem("x1_modulated"), sem("h2_high"), sem("h2_low")
        e_re, e_ff = sem("mlp_relu"), sem("mlp_squared")
        f_fh, f_fl = sem("ff_high"), sem("ff_low")
        o_ss, o_rt, o_fin, o_st = (sem("mlp_squares"), sem("mlp_root"), sem("result_ready"),
                                          sem("result_stored"))
        a_rc = sem("sums_inverted")
        pe_go, pool_go = sem("tensor_goes_on"), sem("gpsimd_goes_on")

        x_var, r_yc = sem("token_variances"), sem("y_centred")

        def chunk(d, n):
            return n if d == 0 else HC * (n // HC) + HC - 1 - n % HC

        DVE_LINKS = 21
        LBANK = (4, 6, 0, 1)
        TBANK = (4, 6, 2, 5, 7)
        STREAMS = [(d, g) for d in range(2) for g in range(2)]
        TURNED = [(d, k, g) for d in range(2) for k in range(2) for g in range(2)]
        fresh = lambda i: isinstance(i, int) and i == 0
        halves = [slice(L * h, L * h + L) for h in range(2)]

        block = stack.enter_context(nc.Block())

        M_ATT, M_SLAB, M_OUT, M_IN, M_MO = 0, KT, KT + SLAB, 2 * KT + SLAB, 2 * KT + SLAB + F_FF
        M_END = M_MO + F_FF
        M_GROUPS, M_EARLY = 12, 3

        def landed(m0, i):
            return m0 % 2, 16 * (m0 // 2 + 1 + i)

        SLAB_ORDER = [T_G, T_W, T_A]
        SLAB_LOOPS = [(3, FT // 2, T_R), (3 + FT, FT, T_K)]

        rk_row = r_k.rearrange("a h n -> a (h n)")
        w_in2 = w_in[0]
        v_slab = w_in2[:, ATT_IN:].rearrange("(k p) f -> p k f", p=P)
        v_mlp = w_mlp_in[0].rearrange("(k p) f -> p k f", p=P)

        @block.sync
        def _(sp):
            with sp.Fori(0, KT // 2) as i:
                for k in range(4):
                    sp.wait_ge(ada_used, 4 * i + k + 1)
                    sp.wait_ge(ada_dve, 4 * i + k + 1)
                    sp.dma_start(ada[k][:, :], w_ada[0, bass.ds(i * (2 * P) + k // 2 * P, P), k % 2 * SLOT:(k % 2 + 1) * SLOT]
                                 ).then_inc(ada_landed[k], 16)

            def slot_free(m, i=0):
                if not (isinstance(i, int) and m < 2):
                    sp.wait_ge(wlo_ready, 2 * i + (m - 1))

            for kt in range(KT):
                slot_free(kt)
                sp.dma_start(raw[kt % 2][:, 0:ATT_IN], w_in2[kt * P:(kt + 1) * P, 0:ATT_IN]).then_inc(raw_landed[kt % 2], 16)

            def load_tile(m, i, view, col):
                slot_free(m, i)
                sp.dma_start(raw[m % 2][:, :].rearrange("p (k f) -> p k f", k=KT), view[:, :, bass.ds(col, P)]
                             ).then_inc(raw_landed[m % 2], 16)

            for q, tile in enumerate(SLAB_ORDER):
                load_tile(M_SLAB + q, 0, v_slab, tile * P)
            for q, turns, tile in SLAB_LOOPS:
                with sp.Fori(0, turns) as i:
                    for j in range(2):
                        load_tile(M_SLAB + q + j, i, v_slab, i * (2 * P) + (tile + j) * P)

            def load_rows(m0, n, w):
                with sp.Fori(0, n // 2) as i:
                    for j in range(2):
                        slot_free(m0 + j, i)
                        sp.dma_start(raw[(m0 + j) % 2][:, :], w[bass.ds(i * (2 * P) + j * P, P), :]
                                     ).then_inc(raw_landed[(m0 + j) % 2], 16)

            sp.wait_ge(c_yd, 8 * FT)
            load_rows(M_OUT, KT, w_out[0])
            for cb in range(4):
                with sp.Fori(0, KT // 4) as i:
                    for j in range(4):
                        load_tile(M_IN + KT * cb + j, 2 * i, v_mlp, i * (4 * P) + (KT * cb + j) * P)
                        if j % 2 == 0:
                            sp.wait_ge(e_acc, 4 * i + (KT * cb + j + 2))
                            sp.dma_start(eb[j // 2][:, :, :], w_ada[0, bass.ds(i * (4 * P) + j * P, 2 * P), M_GT2 * P + cb * 512:
                                                                    M_GT2 * P + (cb + 1) * 512]
                                         .rearrange("(k p) f -> p k f", p=P)).then_inc(eb_landed[j // 2], 16)
            load_rows(M_MO, F_FF, w_mlp_out[0])
            for t in range(2):
                sp.wait_ge(o_fin, t + 1)
                sp.dma_start(out[0, t * P:(t + 1) * P, :], fin[:, t, :]).then_inc(o_st, 16)
            sp.wait_ge(o_st, 32)

        @block.gpsimd
        def _(pool):
            ch = Chain(pool, pool_s)
            def mod_load(g, r, free, col):
                if free is not None:
                    pool.wait_ge(m_acc, free)
                pool.dma_start(mb[r % 4][:, :, :], w_ada[0, 2 * r * P:2 * (r + 1) * P, col].rearrange("(k p) f -> p k f", p=P)
                               ).then_inc(mb_landed[r % 4], 16)

            pool.wait_ge(ada_used, 2 * KT + 4)
            pool.wait_ge(hm_done, 1)
            for g in range(M_EARLY + 1):
                for r in range(KT // 2):
                    q = g * (KT // 2) + r
                    if q == 4:
                        for kt in range(1, KT, 2):
                            pool.wait_ge(hh_done, kt + 1)
                            pool.tensor_tensor(htl[:, kt, :], hmod[:, kt % 4, :], hth[:, kt, :].bitcast(F32), ALU.subtract
                                               ).then_inc(hl_pool, 1)
                    mod_load(g, r, 2 * (q - 3) if q >= 4 else None, slice(M_GT1 * P + g * 512, M_GT1 * P + (g + 1) * 512))

            def rotate(x, t, nh):
                n = nh * HD
                cs = rope[:, t, 0, :].unsqueeze(1).to_broadcast([P, nh, HD])
                ch.link(pool.tensor_tensor(rot1[:, 0:n].rearrange("p (h n) -> p h n", h=nh), x.rearrange("p (h n) -> p h n", h=nh),
                                           cs, ALU.mult))
                src4 = x.rearrange("p (h a j n) -> p h a j n", h=nh, a=2, j=2)
                dst4 = rot2[:, 0:n].rearrange("p (h a j n) -> p h a j n", h=nh, a=2, j=2)
                for j in range(2):
                    sn = rope[:, t, 1, :].rearrange("p (a j n) -> p a j n", a=2, j=2)[:, :, j, :]
                    ch.link(pool.tensor_tensor(dst4[:, :, :, j, :], src4[:, :, :, 1 - j, :],
                                               sn.unsqueeze(1).to_broadcast([P, nh, 2, HD // 4]), ALU.mult))
                ch.link(pool.tensor_tensor(x, rot1[:, 0:n], rot2[:, 0:n], ALU.add))

            pool.wait_ge(ctx_out, 12)
            pool.wait_ge(s_attc, 16)
            for t in range(2):
                rotate(ktk[:, 2 + t, :], t, NKV)
                for q in range(2):
                    rotate(qtk[:, t, q * 512:(q + 1) * 512], t, 4)
            pool.sem_inc(rot_out, 1)
            with pool.Fori(0, M_GROUPS - M_EARLY - 1) as i:
                for r in range(KT // 2):
                    mod_load(0, r, i * KT + ((M_EARLY + 1) * KT + 2 * (r - 3)), bass.ds(i * 512 + (M_GT1 * P + (M_EARLY + 1) * 512), 512))
            pool.wait_ge(rot_out, 1)
            pool.wait_ge(w_used, M_OUT)
            with pool.Fori(0, NQ) as h:
                pool.wait_ge(a_qT, h + 1)
                pool.sem_inc(pool_go, 1)
                pool.tensor_copy(qh[:, :, :], qtk[:, :, bass.ds(h * HD, HD)]).then_inc(a_qh, 1)
            for t in (*bda, *bdk, *bdb, vbd):
                pool.memset(t[:, :, :], 0.0).then_inc(ft_init, 1)
            pool.wait_ge(ft_init, 7)

            def prep_weights(t):
                if not fresh(t):
                    pool.wait_ge(g_lo, 5 * t)
                for k, w in enumerate((w2, a2)):
                    pool.dma_start(wsl[:, k, :], w[0].rearrange("d l r -> (d l) r")[:, bass.ds(t * P, P)]).then_inc(g_w, 16)
                pool.dma_start(wsl[:, 2, :], g2[0][:, bass.ds(t * P, P)]).then_inc(g_w, 16)

            def prep_b(t, d):
                pool.wait_ge(g_sa, 2 * t + d + 1)
                pool.wait_ge(g_ex, 4 * t + 2 * d + 2)
                if not fresh(t):
                    pool.wait_ge(g_zm, 4 * LEVELS * t)
                for h, hs in enumerate(halves):
                    pool.tensor_tensor(bdb[d][hs, :, hs], sat[d][hs, :].rearrange("p (c t) -> p c t", t=L),
                                       cum[d][hs, :].rearrange("p (c t) -> p c t", t=L), ALU.mult).then_inc(g_bb, 1)
                    pool.wait_ge(g_bb, 4 * t + 2 * d + h + 1)

            def copy(dst, src, done, count):
                pool.sem_inc(pool_go, 1)
                pool.tensor_copy(dst, src).then_inc(done, 1)
                pool.wait_ge(done, count)

            def turn(i, prep):
                if prep:
                    prep_weights(i + 1)
                if not fresh(i):
                    pool.wait_ge(c_yd, 8 * i)
                for d in range(2):
                    pool.wait_ge(g_bd, 2 * i + d + 1)
                    for h, hs in enumerate(halves):
                        copy(bda[d][hs, :, hs], ar[d][hs, :, 0:L], g_ba, 6 * i + 3 * d + h + 1)
                    copy(rch[d][:, :, :], ar[d][:, HC:NCH, L:P], g_ba, 6 * i + 3 * d + 3)
                if prep:
                    for d in range(2):
                        prep_b(i + 1, d)
                    prep_values(i + 1)

            def prep_values(t):
                if not fresh(t):
                    pool.wait_ge(g_tr, 10 * t)
                for h, hs in enumerate(halves):
                    copy(vbd[hs, :, hs], s_kv[hs, bass.ds(t + FT, 1), :].rearrange("p a (c t) -> p (a c) t", t=L), g_vb, 2 * t + h + 1)

            prep_weights(0)
            for d in range(2):
                prep_b(0, d)
            prep_values(0)
            turn(0, True)
            with pool.Fori(1, FT - 1) as i:
                turn(i, True)
            turn(FT - 1, False)
            pool.sem_inc(e_ff, 2)
            pool.wait_ge(whi_ready, M_IN + 1)
            pool.tensor_tensor(wlo[M_IN % 2][:, :], raw[M_IN % 2][:, :], whi[M_IN % 2][:, :].bitcast(F32), ALU.subtract
                               ).then_inc(wlo_ready, 1)
            for kt in range(1, KT, 2):
                pool.wait_ge(d_hh, kt + 1)
                pool.tensor_tensor(h2l[:, kt, :], hm2[:, kt % 4, :], h2h[:, kt, :].bitcast(F32), ALU.subtract).then_inc(hl2_pool, 1)
            with pool.Fori(0, F_FF // 2) as i:
                for j in range(2):
                    pool.wait_ge(e_re, 2 * i + j + 3)
                    pool.tensor_tensor(ffh[:, bass.ds(2 * i + j, 1), :], relu[:, j:j + 1, :], relu[:, j:j + 1, :],
                                       ALU.mult).then_inc(e_ff, 1)

        @block.scalar
        def _(act):
            A = nc.scalar.activation
            act.dma_start(rec[:, 0:2 * P], rec_const[:, 0:2 * P]).then_inc(s_const, 16)
            rows = [(mu_prev, P_MUP, SLAB), (mu_next, P_MUN, SLAB), (k_k, P_FT, FT), (k_a, P_FT + FT, FT),
                    (rk_row, P_FT + 2 * FT, FT), (ln_w, P_FT + 3 * FT, FT), (ln_b, P_FT + 4 * FT, FT)]
            for w, r, n in rows:
                act.dma_start(prow[r:r + n, 0, :], w[0].rearrange("(k p) -> k p", p=P)).then_inc(s_rows, 16)
            for w, r in ((w0, P_FT + 5 * FT), (a0, P_FT + 7 * FT)):
                act.dma_start(prow[r:r + 2 * FT, 0, :], w[0].rearrange("d (k p) -> (d k) p", p=P)).then_inc(s_rows, 16)
            for w, r in ((c[0], V_C), (c_ctx, V_CC), (g_pre_mix[0], V_GMIX), (g_pre_mlp[0], V_GMLP)):
                act.dma_start(prow[r:r + KT, 1, :], w.rearrange("(k p) -> k p", p=P)).then_inc(s_rows, 16)
            act.dma_start(prow[0:N_ADA, 2, :], b_ada[0].rearrange("(k p) -> k p", p=P)).then_inc(s_rows, 16)
            for t in range(2):
                act.dma_start(xs[:, t, :], ctx_tok[0, t * P:(t + 1) * P, :]).then_inc(s_x, 16)
            for t in range(2):
                act.dma_start(xs[:, 2 + t, :], x[0, t * P:(t + 1) * P, :]).then_inc(s_x, 16)
            act.dma_start(sink[:, :], attn_sink.to_broadcast([P, NQ])).then_inc(s_sink, 16)
            act.sem_inc(a_oo, 1)
            act.sem_inc(e_re, 2)
            act.wait_ge(prm_done, 3)
            A(stat[:, 0:32], vec[:, 0:32], ACT.Sigmoid).then_inc(silu_sig, 1)
            act.wait_ge(s_x, 64)
            act.wait_ge(silu_done, 1)
            for t in range(4):
                if t:
                    act.wait_ge(ss_done, t)
                A(junk[:, :], xs[:, t, :], ACT.Square, accum_out=stat[:, t:t + 1]).then_inc(ss_done, 1)
            act.wait_ge(x_var, 1)
            A(stat[:, 8:12], stat[:, 4:8], ACT.Sqrt).then_inc(sq_done, 1)
            act.wait_ge(ada_used, 2 * KT + 4)
            act.wait_ge(ada_sum, 2)
            for b in range(8):
                A(modrow[:, b * 512:(b + 1) * 512], PS[b][0:2, :], ACT.Copy).then_inc(row_out, 1)
            for kt in range(KT):
                act.wait_ge(hm_done, kt + 1)
                if kt == 0:
                    act.wait_ge(row_T, 1)
                A(hth[:, kt, :], hmod[:, kt % 4, :], ACT.Copy).then_inc(hh_done, 1)

            def high(m, i=0, n=SLOT):
                s, count = landed(m, i)
                act.wait_ge(raw_landed[s], count)
                if isinstance(i, int) and m < 2:
                    act.wait_ge(ada_used, 2 * KT + 4)
                    act.wait_ge(ada_dve, 2 * KT + 4)
                if not (isinstance(i, int) and m < 2):
                    act.wait_ge(w_used, 2 * i + m - 1)
                A(whi[s][:, 0:n], raw[s][:, 0:n], ACT.Copy).then_inc(whi_ready, 1)

            for m in range(KT):
                high(m, 0, ATT_IN)
            high(M_SLAB)
            act.wait_ge(hl_done, KT // 2)
            act.wait_ge(hl_pool, KT // 2)
            act.dma_start(att_c[:, :], att_const).then_inc(s_attc, 16)
            act.wait_ge(w_used, KT)
            for t in range(2):
                A(ktk[:, t, :], PS[t][:, 0:256], ACT.Copy).then_inc(ctx_out, 1)
                A(vtk[:, t, :], PS[t][:, 256:512], ACT.Copy).then_inc(ctx_out, 1)

            for t in range(2):
                A(ktk[:, 2 + t, :], PS[2 + t][:, 0:256], ACT.Copy).then_inc(ctx_out, 1)
                A(vtk[:, 2 + t, :], PS[2 + t][:, 256:512], ACT.Copy).then_inc(ctx_out, 1)
                for q in range(2):
                    A(qtk[:, t, q * 512:(q + 1) * 512], PS[4 + 2 * t + q][:, :], ACT.Copy).then_inc(ctx_out, 1)

            def base(q, i, dst, mu, last=False):
                if not last:
                    high(M_SLAB + q + 1, i)
                act.wait_ge(w_used, 2 * i + (M_SLAB + q + 1))
                n = dst.free_size()
                A(dst, PS[q % 2][:, 0:n], ACT.Copy, scale=mu).then_inc(slab_base, 1)

            for q, (tile, dst) in enumerate(zip(SLAB_ORDER, (s_g, s_w, s_a))):
                base(q, 0, dst[:, :], mu0[:, tile:tile + 1])
            act.wait_ge(rot_out, 1)
            q0, turns, _ = SLAB_LOOPS[0]
            with act.Fori(0, turns) as i:
                for j in range(2):
                    base(q0 + j, i, s_r[:, bass.ds(2 * i + j, 1), :].rearrange("p a n -> p (a n)"),
                         mu0[:, bass.ds(2 * i + T_R + j, 1)])
            q0, turns, _ = SLAB_LOOPS[1]
            kv = lambda e: s_kv[:, bass.ds(e, 1), :].rearrange("p a n -> p (a n)")
            with act.Fori(0, turns - 1) as i:
                for j in range(2):
                    base(q0 + j, i, kv(2 * i + j), mu0[:, bass.ds(2 * i + T_K + j, 1)])
            for j in range(2):
                e = 2 * (turns - 1) + j
                base(q0 + j + 2 * (turns - 1), 0, s_kv[:, e, :], mu0[:, T_K + e:T_K + e + 1], last=j == 1)
            act.wait_ge(m_acc, M_GROUPS * KT)
            act.dma_start(rec[:, 2 * P:], rec_const[:, 2 * P:]).then_inc(s_masks, 16)
            for g in range(NKV):
                act.wait_ge(kT_done, g + 1)
                A(ktr[:, g, :], PS[g][:, :], ACT.Copy).then_inc(kT_out, 1)
            act.wait_ge(s_sink, 16)
            def queries_out(h):
                act.wait_ge(a_qT, h + 2)
                A(qT[:, :, :].rearrange("p a n -> p (a n)"), PS[2][:, 0:256], ACT.Copy, scale=float(HD) ** -0.5).then_inc(a_qTo, 1)

            def exps(h, j):
                act.wait_ge(a_lg, h + 1)
                st = ast[:, j, :]
                for t in range(2):
                    A(sc[:, j, t, :], sc[:, j, t, :], ACT.Exp, bias=st[:, 2 + t:3 + t], accum_out=st[:, 4 + t:5 + t]).then_inc(a_ex, 1)
                    A(st[:, 6 + t:7 + t], sink[:, bass.ds(h, 1)], ACT.Exp, bias=st[:, 2 + t:3 + t]).then_inc(a_ex, 1)

            def head(h, j, ahead=3):
                for t in range(2):
                    act.wait_ge(a_pT, 2 * h + t + 1)
                    A(pT[:, t, :], PS[5 + t][:, :], ACT.Copy).then_inc(a_pTo, 1)
                if ahead == 3:
                    queries_out(h + 3)
                if ahead:
                    exps(h + 1, 1 - j)
                act.wait_ge(a_o, h + 1)
                A(mixt[:, bass.ds(h, 1), :].rearrange("p a n -> p (a n)"), PS[7][:, 0:SEQ], ACT.Copy).then_inc(a_oo, 1)

            for h in range(3):
                queries_out(h)
            exps(0, 0)
            with act.Fori(0, NQ // 2 - 2) as i:
                for j in range(2):
                    head(2 * i + j, j)
            for h in range(NQ - 4, NQ):
                head(h, h % 2, ahead=min(3, NQ - 1 - h))
            act.wait_ge(slab_done, SLAB)
            A(s_w[:, :], s_w[:, :], ACT.Tanh).then_inc(t_lora, 1)
            A(s_g[:, :], s_g[:, :], ACT.Sigmoid).then_inc(t_lora, 1)

            def prep_square(t):
                act.wait_ge(g_pc, t + 1)
                if not fresh(t):
                    act.wait_ge(g_cum, 2 * t)
                A(sgt[0][:, :], s_kv[:, bass.ds(t, 1), :].rearrange("p a n -> p (a n)"), ACT.Square, scale=pc[:, C_KK:C_KK + 1]).then_inc(g_kq, 1)

            def prep_root(t):
                act.wait_ge(g_nr, t + 1)
                if not fresh(t):
                    act.wait_ge(g_kb, 2 * t)
                A(kd[0][:, :], PS[2][:, :], ACT.Sqrt).then_inc(g_rt, 1)

            def prep_sigmoid(t, k):
                act.wait_ge(g_lo, 5 * t + k + 1)
                if k == 2 and not fresh(t):
                    act.wait_ge(g_bb, 4 * t)
                A((sgt, sat)[k // 2][k % 2][:, :], PS[(5, 7, 2, 5)[k]][:, :], ACT.Sigmoid, bias=pc[:, C_W0 + k:C_W0 + k + 1]).then_inc(g_sg, 1)

            def prep_exp(t, d):
                act.wait_ge(g_cum, 2 * t + d + 1)
                if not fresh(t):
                    act.wait_ge(g_el, 2 * t)
                o = 1 - d
                A(ep[d][:, :, o:o + L], cum[d][:, :].rearrange("p (c t) -> p c t", t=L), ACT.Exp, scale=-DECAY).then_inc(g_ex, 1)
                act.wait_ge(g_ex, 4 * t + 2 * d + 1)
                A(cum[d][:, :], cum[d][:, :], ACT.Exp, scale=DECAY).then_inc(g_ex, 1)

            def prep_gate(t):
                act.wait_ge(g_lo, 5 * t + 5)
                if not fresh(t):
                    act.wait_ge(r_gg, t)
                A(ggn[:, :], PS[7][:, 0:SEQ], ACT.Copy).then_inc(g_gg, 1)

            PREP = {0: [prep_root, lambda t: prep_sigmoid(t, 0)], 1: [lambda t: prep_sigmoid(t, 1), lambda t: prep_sigmoid(t, 2)],
                    2: [lambda t: prep_sigmoid(t, 3), lambda t: prep_exp(t, 0)], 3: [lambda t: prep_exp(t, 1), prep_gate]}

            def turn(i, read, prep):
                if not fresh(i):
                    act.wait_ge(c_yd, 8 * i)
                    act.wait_ge(c_so, 2 * (NCH - 1) * i)
                act.wait_ge(g_ex, 4 * i + 4)
                for d in range(2):
                    A(elast[d][:, :], ep[d][:, :, L if d == 0 else 0], ACT.Copy).then_inc(g_el, 1)

                def turned_out(qs):
                    for q in qs:
                        act.wait_ge(g_tr, 10 * i + q + 1)
                        if q < 8:
                            d, k, g = TURNED[q]
                            dst = (bkt, bbt)[k][d]
                        else:
                            dst, g = vt, q - 8
                        A(dst[:, HC * g:HC * g + HC, :], PS[TBANK[q % 5]][:, :], ACT.Copy).then_inc(g_to, 1)

                def x_out(l, streams):
                    for s in streams:
                        d, g = STREAMS[s]
                        act.wait_ge(g_xt, 4 * LEVELS * i + 4 * l + s + 1)
                        A(bdk[d][:, HC * g:HC * g + HC, :], PS[LBANK[s]][:, :], ACT.Copy).then_inc(g_xo, 1)

                turned_out(range(0, 7))
                x_out(0, (0, 1))
                turned_out(range(7, 10))
                x_out(0, (2, 3))
                if prep:
                    prep_square(i + 1)
                for l in range(LEVELS):
                    if l:
                        x_out(l, range(4))
                    if prep:
                        for step in PREP.get(l, ()):
                            step(i + 1)
                act.wait_ge(g_el, 2 * i + 2)
                for n in range(NCH):
                    for d in range(2):
                        act.wait_ge(c_p, 2 * NCH * i + 2 * n + d + 1)
                        if n:
                            act.wait_ge(c_so, 2 * (NCH - 1) * i + 2 * n + d - 1)
                        A(P_[d][:, :], PS[3 * d + 1][:, 0:P], ACT.Copy).then_inc(c_po, 1)
                    if 0 < n < NCH - 1:
                        for d in range(2):
                            ck = chunk(d, n)
                            A(Se[d][:, :], S_[d][:, :], ACT.Copy, scale=elast[d][:, ck:ck + 1]).then_inc(c_se, 1)
                    if read and n == 1:
                        read_square(i - 1)
                    if read and n == 3:
                        read_root(i - 1)
                    if n == 5:
                        move(i)

            def move(i):
                if not fresh(i):
                    act.wait_ge(ft_done, i)
                act.wait_ge(r_bo, i + 1)
                act.wait_ge(r_gg, i + 1)
                A(yb[:, 1, :], bonus[:, :], ACT.Copy).then_inc(r_mv, 1)
                A(gg[:, :], ggh[:, :], ACT.Copy).then_inc(r_mv, 1)

            def read_square(r):
                act.wait_ge(r_yc, r + 1)
                A(yq[:, 0, :], yb[:, 0, :], ACT.Square).then_inc(r_sq, 1)

            def read_root(r):
                act.wait_ge(r_vt, r + 1)
                A(yq[:, 0, :], yq[:, 1, :], ACT.Sqrt).then_inc(r_sd, 1)

            prep_square(0)
            for n in range(NCH):
                for step in PREP.get(n, ()):
                    step(0)
            turn(0, False, True)
            with act.Fori(1, FT - 1) as i:
                turn(i, True, True)
            turn(FT - 1, True, False)
            def mix_high(t):
                A(h2h[:, 4 * t:4 * t + 4, :], mixt[:, 4 * t:4 * t + 4, :], ACT.Copy).then_inc(d_mh, 1)

            act.wait_ge(c_yd, 8 * FT)
            for t, g_post in ((gpost, g_post_mix), (gpost2, g_post_mlp)):
                act.dma_start(t[:, :], g_post[0:1, :].to_broadcast([P, D])).then_inc(d_gp, 16)
            for t in range(2):
                act.dma_start(x1[:, t, :], x[0, t * P:(t + 1) * P, :]).then_inc(d_x, 16)
            act.wait_ge(ft_done, 4)
            read_square(FT - 1)
            for t in range(3):
                mix_high(t)
            read_root(FT - 1)
            for j in range(2):
                high(M_OUT + j)
            act.wait_ge(ft_done, FT)
            mix_high(3)
            act.wait_ge(e_zero, 1)
            act.dma_start(gates[0:1, 1, :], b_ada[0:1, M_GT2 * P:6 * D]).then_inc(e_bias, 16)
            with act.Fori(1, KT // 2) as i:
                for j in range(2):
                    high(M_OUT + j, i)
            act.wait_ge(w_used, M_IN)
            for t in range(2):
                if t:
                    act.wait_ge(d_pg, 4)
                for b in range(4):
                    if t:
                        act.wait_ge(d_out, b + 1)
                    A(junk2[:, b * 512:(b + 1) * 512], PS[4 * t + b][:, :], ACT.Square, accum_out=sqs[:, t, b:b + 1]).then_inc(d_out, 1)
            act.wait_ge(d_rt, 1)
            A(stat[:, 16:18], stat[:, 14:16], ACT.Sqrt).then_inc(d_ss, 1)
            for t in range(2):
                act.wait_ge(d_x1, t + 1)
                A(junk2[:, :], x1[:, t, :], ACT.Square, accum_out=stat[:, 20 + t:21 + t]).then_inc(d_ss, 1)
                act.wait_ge(d_ss, 2 + t)
            act.wait_ge(d_rt, 2)
            A(stat[:, 24:26], stat[:, 22:24], ACT.Sqrt).then_inc(d_ss, 1)
            high(M_IN)
            for kt in range(KT):
                act.wait_ge(d_hm, kt + 1)
                A(h2h[:, kt, :], hm2[:, kt % 4, :], ACT.Copy).then_inc(d_hh, 1)
            with act.Fori(0, F_FF // 2) as i:
                for j in range(2):
                    high(M_IN + j + 1, i)
                    act.wait_ge(w_used, 2 * i + (M_IN + j + 1))
                    act.wait_ge(e_ff, 2 * i + j + 1)
                    A(relu[:, j, :], PS[j][:, 0:SEQ], ACT.Relu).then_inc(e_re, 1)
            act.wait_ge(e_ff, F_FF + 2)

            def hidden(i, j):
                act.wait_ge(w_used, 2 * i + (M_MO + j - 1))
                A(fsh[j][:, :], ffh[:, bass.ds(2 * i + j, 1), :].rearrange("p a n -> p (a n)"), ACT.Copy).then_inc(f_fh, 1)

            with act.Fori(0, F_FF // 2 - 1) as i:
                for j in range(2):
                    hidden(i, j)
                    high(M_MO + j + 1, i)
            for j in range(2):
                hidden(F_FF // 2 - 1, j)
                if j == 0:
                    high(M_END - 1)
            act.wait_ge(w_used, M_END)
            for t in range(2):
                if t:
                    act.wait_ge(o_pg, 4)
                for b in range(4):
                    if t:
                        act.wait_ge(o_ss, b + 1)
                    A(junk3[:, b * 512:(b + 1) * 512], PS[4 * t + b][:, :], ACT.Square, accum_out=sqs[:, t, b:b + 1]).then_inc(o_ss, 1)
            act.wait_ge(o_rt, 1)
            A(stat[:, 30:32], stat[:, 28:30], ACT.Sqrt).then_inc(o_ss, 1)

        @block.vector
        def _(dve):
            ch = Chain(dve, dve_s)
            TT, TS, STT = nc.vector.tensor_tensor, nc.vector.tensor_scalar, nc.vector.scalar_tensor_tensor
            dve.sem_inc(ada_dve, 4)
            dve.sem_inc(e_acc, 4)
            dve.wait_ge(prm_T, 1)
            nc.vector.tensor_copy(prm[:, :], PS[0][:, 0:N_PRM]).then_inc(prm_done, 1)
            nc.vector.tensor_copy(vec[:, :], PS[0][:, 128:192]).then_inc(prm_done, 1)
            nc.vector.tensor_copy(bada[:, :], PS[0][:, 192:192 + N_ADA]).then_inc(prm_done, 1)
            dve.wait_ge(prm_done, 3)
            ch.link(STT(out=mu0[:, :], in0=prm[:, P_MUP:P_MUP + SLAB], scalar=-1.0, in1=prm[:, P_MUN:P_MUN + SLAB],
                        op0=ALU.mult, op1=ALU.subtract))
            ch.link(TS(mu0[:, :], mu0[:, :], 1.0, None, ALU.add))
            dve.wait_ge(silu_sig, 1)
            TT(silc[:, :, :].rearrange("p k j -> p j k"), vec[:, 0:32].rearrange("p (j k) -> p j k", j=2),
               stat[:, 0:32].rearrange("p (j k) -> p j k", j=2), ALU.mult).then_inc(silu_done, 1)
            ch.link(nc.vector.memset(pick[:, :, :], 0.0))
            for j in range(2):
                nc.vector.memset(pick[:, j, j:j + 1], 1.0).then_inc(ada_pick, 1)
            ch.link(nc.vector.memset(aacc[:, :, :, :], 0.0))
            dve.wait_ge(silu_done, 1)
            with dve.Fori(0, KT // 2) as i:
                ch.enter(i, 4)
                for k in range(4):
                    dve.wait_ge(ada_landed[k], 16 * i + 16)
                    dve.wait_ge(ada_dve, 4 * i + (4 + k - 1))
                    for j in range(2):
                        ins = STT(out=aacc[:, k % 2, j, :], in0=ada[k][:, 3 * 512:SLOT], scalar=silc[:, bass.ds(2 * i + k // 2, 1), j],
                                  in1=aacc[:, k % 2, j, :], op0=ALU.mult, op1=ALU.add)
                        if j == 0:
                            ch.link(ins)
                        else:
                            ins.then_inc(ada_dve, 1)
            ch.leave(KT // 2)
            dve.wait_ge(ss_done, 4)
            TS(stat[:, 4:8], stat[:, 0:4], 1.0 / D, EPS, ALU.mult, ALU.add).then_inc(x_var, 1)
            dve.wait_ge(sq_done, 1)
            ch.link(nc.vector.reciprocal(stat[:, 12:16], stat[:, 8:12]))
            for t in range(4):
                TS(xs[:, t, :], xs[:, t, :], stat[:, 12 + t:13 + t], None, ALU.mult).then_inc(xhat_done, 1)
            dve.wait_ge(row_T, 1)
            for j in range(2):
                TT(modc[:, 0:2 * KT, j], PS[0][:, j:64:2], bada[:, 0:2 * KT], ALU.add).then_inc(mod_done, 1)
            dve.wait_ge(mod_done, 2)
            ch.link(nc.vector.memset(onec[:, :], 1.0))
            for j in range(2):
                ch.link(STT(out=amod[:, j, :], in0=modc[:, M_SC1:M_SC1 + KT, j], scalar=1.0, in1=vec[:, V_GMIX:V_GMIX + KT],
                            op0=ALU.add, op1=ALU.mult))

            def h_low(kt):
                dve.wait_ge(hh_done, kt + 1)
                TT(htl[:, kt, :], hmod[:, kt % 4, :], hth[:, kt, :].bitcast(F32), ALU.subtract).then_inc(hl_done, 1)

            for kt in range(KT):
                dve.wait_ge(xT_done, kt + 1)
                if kt >= 4:
                    dve.wait_ge((hl_done, hl_pool)[kt % 2], kt // 2 - 1)
                b = PS[1 + kt % 4]
                TS(hmod[:, kt % 4, 0:CTX], b[:, 0:CTX], amod[:, 1, kt:kt + 1], modc[:, M_SH1 + kt, 1:2], ALU.mult, ALU.add)
                TS(hmod[:, kt % 4, CTX:TOK], b[:, CTX:TOK], amod[:, 0, kt:kt + 1], modc[:, M_SH1 + kt, 0:1],
                   ALU.mult, ALU.add).then_inc(hm_done, 1)
                if kt % 2:
                    h_low(kt - 1)

            def low(m, i=0, n=SLOT):
                s = m % 2
                dve.wait_ge(whi_ready, 2 * i + m + 1)
                TT(wlo[s][:, 0:n], raw[s][:, 0:n], whi[s][:, 0:n].bitcast(F32), ALU.subtract).then_inc(wlo_ready, 1)

            def mod_step(g, i, k):
                if k % 2 == 0:
                    dve.wait_ge(mb_landed[k // 2 % 4], 16 * (KT // 8) * i + 16 * (KT // 8 * g + k // 8 + 1))
                acc = macc[g] if g < M_EARLY else macc[M_EARLY]
                src, s_c = mb[k // 2 % 4][:, k % 2, :], silc[:, k, 0:1]
                if k == 0:
                    TS(acc[:, :], src, s_c, None, ALU.mult).then_inc(m_acc, 1)
                else:
                    dve.wait_ge(m_acc, KT * i + (KT * g + k))
                    STT(out=acc[:, :], in0=src, scalar=s_c, in1=acc[:, :], op0=ALU.mult, op1=ALU.add).then_inc(m_acc, 1)

            def mod_out(i, n, at, reds):
                dve.wait_ge(m_red, i + reds)
                TT(modc[:, bass.ds(4 * i + at, n), 0], PS[2][:, 0:n], bada[:, bass.ds(4 * i + at, n)], ALU.add).then_inc(m_out, 1)

            for m in range(KT):
                low(m, 0, ATT_IN)
                if m == KT - 1:
                    low(M_SLAB)
                for k in range(4):
                    mod_step(m // 4, 0, 4 * (m % 4) + k)

            def shift(q, i, dst, tile, last=False, between=lambda: None):
                if not last:
                    low(M_SLAB + q + 1, i)
                between()
                dve.wait_ge(slab_base, 2 * i + q + 1)
                n = dst.free_size() // SEQ if dst.free_size() > SEQ else 1
                src = PS[q % 2][:, 0:n * SEQ].rearrange("p (a n) -> p a n", a=n)
                dst = dst.rearrange("p (a n) -> p a n", a=n)
                col = lambda b: prm[:, bass.ds(tile + b, 1)]
                ch.link(STT(out=dst[:, :, 1:SEQ], in0=src[:, :, 0:SEQ - 1], scalar=col(P_MUP), in1=dst[:, :, 1:SEQ],
                            op0=ALU.mult, op1=ALU.add))
                STT(out=dst[:, :, 0:SEQ - 1], in0=src[:, :, 1:SEQ], scalar=col(P_MUN), in1=dst[:, :, 0:SEQ - 1],
                    op0=ALU.mult, op1=ALU.add).then_inc(slab_done, 1)

            flat = lambda t, e: t[:, bass.ds(e, 1), :].rearrange("p a n -> p (a n)")
            for q, (tile, dst) in enumerate(zip(SLAB_ORDER, (s_g, s_w, s_a))):
                shift(q, 0, dst[:, :], tile)
            q0, turns, _ = SLAB_LOOPS[0]
            with dve.Fori(0, turns) as i:
                ch.enter(i, 2)
                for j in range(2):
                    shift(q0 + j, i, flat(s_r, 2 * i + j), 2 * i + T_R + j)
            ch.leave(turns)
            mod_out(0, 4 * M_EARLY, M_GT1, 1)
            q0, turns, _ = SLAB_LOOPS[1]
            assert turns == M_GROUPS - M_EARLY - 1

            def mods(i, j):
                if j == 0:
                    mod_out(i, 4, M_GT1 + 4 * M_EARLY, 2)
                for k in range(KT // 2):
                    mod_step(M_EARLY + 1, i, KT // 2 * j + k)

            with dve.Fori(0, turns - 1) as i:
                ch.enter(i, 2)
                for j in range(2):
                    shift(q0 + j, i, flat(s_kv, 2 * i + j), 2 * i + T_K + j, between=lambda: mods(i, j))
            ch.leave(turns - 1)
            for j in range(2):
                e = 2 * (turns - 1) + j
                shift(q0 + e, 0, s_kv[:, e, :], T_K + e, last=j == 1, between=lambda: mods(turns - 1, j))
            mod_out(turns, 4, M_GT1 + 4 * M_EARLY, 2)
            dve.wait_ge(m_out, turns + 2)
            ch.link(STT(out=amod2[:, :], in0=modc[:, M_SC2:M_SC2 + KT, 0], scalar=1.0, in1=vec[:, V_GMLP:V_GMLP + KT],
                        op0=ALU.add, op1=ALU.mult))

            dve.wait_ge(s_sink, 16)
            def scores(h, j):
                st = ast[:, j, :]
                for t in range(2):
                    dve.wait_ge(a_sc, 2 * h + t + 1)
                    ins = TT(sc[:, j, t, :], PS[(3, 0)[j] + t][:, :], amask[:, t, :], ALU.add)
                ch.link(ins)
                ch.link(nc.vector.tensor_reduce(st[:, 0:2], sc[:, j, :, :], AX.X, ALU.max))
                ch.link(TT(st[:, 12:14], st[:, 0:2], sink[:, bass.ds(h, 1)].to_broadcast([P, 2]), ALU.max))
                TS(st[:, 2:4], st[:, 12:14], -1.0, None, ALU.mult).then_inc(a_lg, 1)

            def head(h, j, more=True):
                st = ast[:, j, :]
                dve.wait_ge(a_ex, 4 * h + 4)
                ch.link(TT(st[:, 8:10], st[:, 4:6], st[:, 6:8], ALU.add))
                nc.vector.reciprocal(st[:, 10:12], st[:, 8:10]).then_inc(a_rc, 1)
                dve.wait_ge(a_rc, h + 1)
                for t in range(2):
                    TS(sc[:, j, t, :], sc[:, j, t, :], st[:, 10 + t:11 + t], None, ALU.mult).then_inc(a_pr, 1)
                if more:
                    if not (isinstance(h, int) and h == 0):
                        dve.wait_ge(a_pT, 2 * h)
                    scores(h + 1, 1 - j)

            scores(0, 0)
            for j in range(2):
                head(j, j)
            with dve.Fori(1, NQ // 2 - 1) as i:
                ch.enter(i, 8, 1)
                for j in range(2):
                    head(2 * i + j, j)
            ch.leave(NQ // 2 - 2)
            for j in range(2):
                head(NQ - 2 + j, j, more=j == 0)

            dve.wait_ge(a_oo, NQ + 1)
            dve.wait_ge(slab_done, SLAB)
            dve.wait_ge(s_masks, 16)
            for d in range(2):
                ch.link(nc.vector.memset(ep[d][:, :, d * L:d * L + 1], 1.0))
            keys_of = lambda t: flat(s_kv, t)
            c3 = lambda t: t.rearrange("p (c t) -> p c t", t=L)

            def prep_params(t):
                if not fresh(t):
                    dve.wait_ge(g_sg, 4 * t)
                nc.vector.tensor_copy(pc[:, 0:9], prm[:, P_FT:P_FT + 9 * FT].rearrange("p (v f) -> p v f", f=FT)[:, :, bass.ds(t, 1)]
                                      .rearrange("p v a -> p (v a)")).then_inc(g_pc, 1)
                dve.wait_ge(g_pc, t + 1)
                ch.link(TS(pc[:, 9:10], pc[:, C_KA:C_KA + 1], -1.0, 1.0, ALU.mult, ALU.add))

            def prep_inverse_norms(t):
                dve.wait_ge(g_rt, t + 1)
                ch.link(TS(kd[0][:, :], kd[0][:, :], 1e-12, None, ALU.max))
                ch.link(nc.vector.reciprocal(kd[0][:, :], kd[0][:, :]))

            def prep_unit_keys(t):
                STT(out=kk[:, :], in0=keys_of(t), scalar=pc[:, C_KK:C_KK + 1], in1=kd[0][:, :], op0=ALU.mult, op1=ALU.mult).then_inc(g_kk, 1)
                dve.wait_ge(g_kk, t + 1)

            def prep_sums(t, d):
                dve.wait_ge(g_sg, 4 * t + d + 1)
                if not fresh(t):
                    dve.wait_ge(g_bb, 4 * t)
                step = 1 if d == 0 else -1
                nc.vector.tensor_tensor_scan(cum[d][:, ::step], rst[d][:, ::step], sgt[d][:, ::step], 0.0, ALU.mult, ALU.add
                                             ).then_inc(g_cum, 1)

            def prep_rates(t, d):
                dve.wait_ge(g_sg, 4 * t + d + 3)
                ch.link(TS(kd[d][:, :], sat[d][:, :], pc[:, C_KA:C_KA + 1], pc[:, 9:10], ALU.mult, ALU.add))
                TT(sat[d][:, :], sat[d][:, :], kk[:, :], ALU.mult).then_inc(g_sa, 1)
                ch.link(TT(kd[d][:, :], kd[d][:, :], keys_of(t), ALU.mult))

            def prep_key_blocks(t, d):
                dve.wait_ge(g_ex, 4 * t + 2 * d + 2)
                if not fresh(t):
                    dve.wait_ge(g_tm, 4 * LEVELS * t)
                for hs in halves:
                    last = TT(bdk[d][hs, :, hs], c3(kd[d][hs, :]), c3(cum[d][hs, :]), ALU.mult)
                last.then_inc(g_kb, 1)
                if d == 1:
                    ch.link(TT(kb[:, :], kd[0][:, CTX:TOK], kd[1][:, CTX:TOK], ALU.add))

            def prep_reads(t, d):
                dve.wait_ge(g_ex, 4 * t + 2 * d + 1)
                if not fresh(t):
                    dve.wait_ge(g_ba, 6 * t)
                TT(ar[d][:, HC:NCH, L:P], c3(flat(s_r, t)), ep[d][:, HC:NCH, 1 - d:1 - d + L], ALU.mult)
                STT(out=ar[d][:, :, 0:L], in0=c3(kk[:, :]), scalar=-1.0, in1=ep[d][:, :, d:d + L],
                    op0=ALU.mult, op1=ALU.mult).then_inc(g_bd, 1)
                dve.wait_ge(g_bd, 2 * t + d + 1)

            PREP = {0: [prep_inverse_norms], 1: [prep_unit_keys, lambda t: prep_sums(t, 0)],
                    2: [lambda t: prep_sums(t, 1), lambda t: prep_rates(t, 0)],
                    3: [lambda t: prep_rates(t, 1), lambda t: prep_reads(t, 0)], 4: [lambda t: prep_reads(t, 1)]}

            PAIR = [(2, 5, 7), (0, 1, 3)]
            low_, high_ = slice(0, HC), slice(HC, NCH)
            per = lambda m: m.unsqueeze(1).to_broadcast([P, HC, m.free_size()])
            wide = lambda b: PS[b][:, :].rearrange("p (c n) -> p c n", n=P)

            def bd(dst, src, d, cs):
                m = strict[d].rearrange("p (h t) -> p h t", h=2).unsqueeze(1).to_broadcast([P, HC, 2, L])
                return TT(dst[d][:, cs, :].rearrange("p c (h t) -> p c h t", h=2),
                          src.unsqueeze(2).to_broadcast([P, HC, 2, L]), m, ALU.mult)

            context = lambda d, k: PS[PAIR[d][0]][:, k * SEQ:(k + 1) * SEQ].rearrange("p (c n) -> p c n", n=L)

            def masked_start(t, d):
                if not fresh(t):
                    dve.wait_ge(g_tm, 4 * LEVELS * t)
                    dve.wait_ge(g_ze, 4 * LEVELS * t)
                for cs, src, k in ((low_, context(d, 0), 1), (high_, wide(PAIR[d][1])[:, :, 0:L], 2)):
                    dve.wait_ge(g_am, 6 * t + 3 * d + k)
                    ch.link(bd(dd, src, d, cs))
                    ch.link(TT(zn[d][:, cs, :], dd[d][:, cs, :], per(lv1[d]), ALU.mult))
                    TT(zn[d][:, cs, :], zn[d][:, cs, :], per(ident), ALU.add).then_inc(g_z1, 1)

            def masked_rest(t, d):
                TT(arb[d][:, :, :], wide(PAIR[d][1])[:, :, L:P], per(incl[d]), ALU.mult)
                last = bd(aak, context(d, 1), d, low_)
                if d == 1:
                    last.then_inc(g_aa, 1)
                dve.wait_ge(g_am, 6 * t + 3 * d + 3)
                bd(aak, wide(PAIR[d][2])[:, :, 0:L], d, high_)
                TT(ark[d][:, :, :], wide(PAIR[d][2])[:, :, L:P], per(incl[d]), ALU.mult).then_inc(g_ae, 1)

            def read_y(r):
                dve.wait_ge(c_yd, 8 * r + 8)
                nc.vector.tensor_copy(yb[:, 0, :], PS[6][:, 0:SEQ]).then_inc(r_yb, 1)
                ch.link(nc.vector.tensor_copy(pcr[:, :], prm[:, P_FT:P_FT + 9 * FT].rearrange("p (v f) -> p v f", f=FT)
                                              [:, C_LNW:C_LNB + 1, bass.ds(r, 1)].rearrange("p v a -> p (v a)")))

            def read_centre(r):
                dve.wait_ge(r_mu, r + 1)
                STT(out=yb[:, 0, :], in0=PS[5][:, 0:SEQ], scalar=-1.0 / L, in1=yb[:, 0, :], op0=ALU.mult, op1=ALU.add).then_inc(r_yc, 1)
                STT(out=yb[:, 1, :], in0=PS[5][:, SEQ:TOK], scalar=0.5, in1=flat(s_kv, r + FT)[:, CTX:TOK], op0=ALU.mult, op1=ALU.mult
                    ).then_inc(r_bm, 1)

            def read_variance(r):
                dve.wait_ge(r_var, r + 1)
                TS(yq[:, 1, :], PS[2][:, 0:SEQ], 1.0 / L, GN_EPS, ALU.mult, ALU.add).then_inc(r_vt, 1)

            def read_mix(r):
                dve.wait_ge(r_sd, r + 1)
                ch.link(nc.vector.reciprocal(yq[:, 1, :], yq[:, 0, :]))
                ch.link(TT(yb[:, 0, :], yb[:, 0, :], yq[:, 1, :], ALU.mult))
                ch.link(TS(yb[:, 0, :], yb[:, 0, :], pcr[:, 0:1], pcr[:, 1:2], ALU.mult, ALU.add))
                ch.link(TT(yb[:, 0, :], yb[:, 0, :], yb[:, 1, :], ALU.add))
                TT(flat(mixt, r + NQ), yb[:, 0, :], gg[:, :], ALU.mult).then_inc(ft_done, 1)
                dve.wait_ge(ft_done, r + 1)

            def keep_bonus(i):
                dve.wait_ge(g_gg, i + 1)
                if not fresh(i):
                    dve.wait_ge(r_mv, 2 * i)
                STT(out=bonus[:, :], in0=flat(s_r, i), scalar=pc[:, C_RK:C_RK + 1], in1=kb[:, :], op0=ALU.mult, op1=ALU.mult).then_inc(r_bo, 1)
                nc.vector.tensor_copy(ggh[:, :], ggn[:, :]).then_inc(r_gg, 1)
                dve.wait_ge(r_gg, i + 1)
                dve.wait_ge(r_bo, i + 1)

            def turn(i, read, prep):
                if read:
                    read_y(i - 1)
                masked_rest(i, 0)
                masked_start(i, 1)
                masked_rest(i, 1)
                keep_bonus(i)
                if prep:
                    prep_params(i + 1)
                for l in range(LEVELS):
                    for s, (d, g) in enumerate(STREAMS):
                        dve.wait_ge(g_tm, 4 * LEVELS * i + 4 * l + s + 1)
                        TT(bdb[d][:, HC * g:HC * g + HC, :], PS[LBANK[s]][:, :].rearrange("p (c n) -> p c n", n=P),
                           per(lvt[d][l]), ALU.mult).then_inc(g_te, 1)
                    for s, (d, g) in enumerate(STREAMS):
                        cs = slice(HC * g, HC * g + HC)
                        dve.wait_ge(g_zm, 4 * LEVELS * i + 4 * l + s + 1)
                        TT(zz[d][:, cs, :], (zz if l else zn)[d][:, cs, :], PS[LBANK[s]][:, :].rearrange("p (c n) -> p c n", n=P), ALU.add
                           ).then_inc(g_ze, 1)
                    if prep:
                        for step in PREP.get(l, ()):
                            step(i + 1)
                for n in range(NCH):
                    for d in range(2):
                        dve.wait_ge(c_u, 2 * NCH * i + 2 * n + d + 1)
                        nc.vector.tensor_copy(U_[d][:, :], PS[3 * d + 1][:, P:2 * P]).then_inc(c_uo, 1)
                    if n < NCH - 1:
                        for d in range(2):
                            ck = chunk(d, n)
                            dve.wait_ge(c_s, 2 * (NCH - 1) * i + 2 * n + d + 1)
                            e = elast[d][:, ck:ck + 1]
                            if n == 0:
                                dve.wait_ge(g_el, 2 * i + d + 1)
                                TS(S_[d][:, :], PS[3 * d][:, 0:P], e, None, ALU.mult).then_inc(c_so, 1)
                            else:
                                dve.wait_ge(c_se, 2 * (NCH - 2) * i + 2 * n + d - 1)
                                STT(out=S_[d][:, :], in0=PS[3 * d][:, 0:P], scalar=e, in1=Se[d][:, :], op0=ALU.mult, op1=ALU.add
                                    ).then_inc(c_so, 1)
                    if prep and n in (0, 3):
                        prep_key_blocks(i + 1, n // 3)
                    if read and n == 1:
                        read_centre(i - 1)
                    if read and n == 2:
                        read_variance(i - 1)
                    if read and n == 4:
                        read_mix(i - 1)
                    if prep and n == NCH - 1:
                        masked_start(i + 1, 0)

            prep_params(0)
            for l in range(LEVELS):
                for step in PREP.get(l, ()):
                    step(0)
            for d in range(2):
                prep_key_blocks(0, d)
            masked_start(0, 0)
            turn(0, False, True)
            with dve.Fori(1, FT - 1) as i:
                ch.enter(i, DVE_LINKS, 1)
                turn(i, True, True)
            ch.leave(FT - 2)
            turn(FT - 1, True, False)
            read_y(FT - 1)
            ch.link(nc.vector.memset(ones[:, :], 1.0))
            for b in range(4):
                TT(diag[:, 4 * b:4 * b + 4, :], ident.unsqueeze(1).to_broadcast([P, 4, P]),
                   modc[:, M_GT1 + 4 * b:M_GT1 + 4 * b + 4, 0:1].to_broadcast([P, 4, P]), ALU.mult).then_inc(d_dg, 1)
                if b == 1:
                    read_centre(FT - 1)
            read_variance(FT - 1)

            def mix_low(t):
                dve.wait_ge(d_mh, t + 1)
                TT(h2l[:, 4 * t:4 * t + 4, :], mixt[:, 4 * t:4 * t + 4, :], h2h[:, 4 * t:4 * t + 4, :].bitcast(F32),
                   ALU.subtract).then_inc(d_ml, 1)

            dve.wait_ge(r_bm, FT)
            dve.wait_ge(d_gp, 32)
            for b in range(4):
                dve.wait_ge(d_gm, b + 1)
                part = slice(b * 512, b * 512 + 512)
                TT(gates[:, 0, part], PS[(0, 1, 3, 4)[b]][:, :], gpost[:, part], ALU.mult).then_inc(d_gt, 1)
            mix_low(0)
            for j in range(2):
                low(M_OUT + j)
            mix_low(1)
            mix_low(2)
            read_mix(FT - 1)
            mix_low(3)
            nc.vector.memset(gates[:, 1, :], 0.0).then_inc(e_zero, 1)
            with dve.Fori(1, KT // 2) as i:
                for j in range(2):
                    low(M_OUT + j, i)

            dve.wait_ge(w_used, M_IN)
            for t in (1, 0):
                if t == 0:
                    dve.wait_ge(d_out, 4)
                for b in range(4):
                    part = slice(b * 512, b * 512 + 512)
                    TT(mm_[:, t, part], PS[4 * t + b][:, :], gates[:, 0, part], ALU.mult).then_inc(d_pg, 1)
            dve.wait_ge(d_out, 8)
            dve.wait_ge(d_pg, 8)
            ch.link(nc.vector.tensor_reduce(stat[:, 12:14], sqs[:, :, :], AX.X, ALU.add))
            TS(stat[:, 14:16], stat[:, 12:14], 1.0 / D, EPS, ALU.mult, ALU.add).then_inc(d_rt, 1)
            dve.wait_ge(d_ss, 1)
            ch.link(nc.vector.reciprocal(stat[:, 18:20], stat[:, 16:18]))
            dve.wait_ge(d_x, 32)
            for t in range(2):
                STT(out=x1[:, t, :], in0=mm_[:, t, :], scalar=stat[:, 18 + t:19 + t], in1=x1[:, t, :],
                    op0=ALU.mult, op1=ALU.add).then_inc(d_x1, 1)
            dve.wait_ge(d_ss, 3)
            TS(stat[:, 22:24], stat[:, 20:22], 1.0 / D, EPS, ALU.mult, ALU.add).then_inc(d_rt, 1)
            dve.wait_ge(d_ss, 4)
            ch.link(nc.vector.reciprocal(stat[:, 18:20], stat[:, 24:26]))
            for t in range(2):
                TS(dg2[:, t, :], ident, stat[:, 18 + t:19 + t], None, ALU.mult).then_inc(d_xh, 1)

            def h2_low(kt):
                dve.wait_ge(d_hh, kt + 1)
                TT(h2l[:, kt, :], hm2[:, kt % 4, :], h2h[:, kt, :].bitcast(F32), ALU.subtract).then_inc(d_hl, 1)

            for kt in range(KT):
                dve.wait_ge(d_tr, kt + 1)
                if kt >= 4:
                    dve.wait_ge((d_hl, hl2_pool)[kt % 2], kt // 2 - 1)
                TS(hm2[:, kt % 4, :], PS[kt % 4][:, 0:SEQ], amod2[:, kt:kt + 1], modc[:, M_SH2 + kt, 0:1], ALU.mult, ALU.add
                   ).then_inc(d_hm, 1)
                if kt >= 2 and kt % 2 == 0:
                    h2_low(kt - 2)
            h2_low(KT - 2)
            dve.wait_ge(wlo_ready, M_IN + 1)
            def gate_out(cb):
                dve.wait_ge(e_red, cb + 1)
                part = slice(cb * 512, (cb + 1) * 512)
                TT(gates[:, 1, part], PS[2 + cb][:, :], gpost2[:, part], ALU.mult).then_inc(e_gt, 1)

            dve.wait_ge(e_bias, 16)
            for cb in range(4):
                with dve.Fori(0, KT // 4) as i:
                    for j in range(4):
                        low(M_IN + KT * cb + j + 1, 2 * i)
                        if j % 2 == 0:
                            dve.wait_ge(eb_landed[j // 2], 16 * i + 16 * (4 * cb + 1))
                        dve.wait_ge(e_acc, 4 * i + (KT * cb + j + 4))
                        acc = gates[:, 1, cb * 512:(cb + 1) * 512]
                        STT(out=acc, in0=eb[j // 2][:, j % 2, :], scalar=silc[:, bass.ds(4 * i + j, 1), 0], in1=acc,
                            op0=ALU.mult, op1=ALU.add).then_inc(e_acc, 1)
                if cb:
                    gate_out(cb - 1)
            gate_out(3)

            def hidden_low(i, j):
                dve.wait_ge(f_fh, 2 * i + j + 1)
                TT(fsl[j][:, :], flat(ffh, 2 * i + j), fsh[j][:, :].bitcast(F32), ALU.subtract).then_inc(f_fl, 1)

            with dve.Fori(0, F_FF // 2 - 1) as i:
                for j in range(2):
                    hidden_low(i, j)
                    low(M_MO + j + 1, i)
            for j in range(2):
                hidden_low(F_FF // 2 - 1, j)
                if j == 0:
                    low(M_END - 1)
            dve.wait_ge(w_used, M_END)
            for t in (1, 0):
                if t == 0:
                    dve.wait_ge(o_ss, 4)
                for b in range(4):
                    part = slice(b * 512, b * 512 + 512)
                    TT(ffo[:, t, part], PS[4 * t + b][:, :], gates[:, 1, part], ALU.mult).then_inc(o_pg, 1)
            dve.wait_ge(o_ss, 8)
            dve.wait_ge(o_pg, 8)
            ch.link(nc.vector.tensor_reduce(stat[:, 26:28], sqs[:, :, :], AX.X, ALU.add))
            TS(stat[:, 28:30], stat[:, 26:28], 1.0 / D, EPS, ALU.mult, ALU.add).then_inc(o_rt, 1)
            dve.wait_ge(o_ss, 9)
            ch.link(nc.vector.reciprocal(stat[:, 18:20], stat[:, 30:32]))
            for t in range(2):
                STT(out=fin[:, t, :], in0=ffo[:, t, :], scalar=stat[:, 18 + t:19 + t], in1=x1[:, t, :],
                    op0=ALU.mult, op1=ALU.add).then_inc(o_fin, 1)

        @block.tensor
        def _(pe):
            mm, tr = nc.tensor.matmul, nc.tensor.transpose
            pe.sem_inc(ada_used, 4)
            pe.sem_inc(a_qT, 1)
            pe.wait_ge(s_const, 16)
            pe.wait_ge(s_rows, 16 * 14)
            tr(PS[0][:, 0:N_PRM], prow[0:N_PRM, 0, :], ident[0:N_PRM, 0:N_PRM])
            tr(PS[0][:, 128:192], prow[0:64, 1, :], ident[0:64, 0:64])
            tr(PS[0][:, 192:192 + N_ADA], prow[0:N_ADA, 2, :], ident[0:N_ADA, 0:N_ADA]).then_inc(prm_T, 1)
            pe.wait_ge(silu_done, 1)
            pe.wait_ge(prm_done, 3)

            def ada_rows(i, slots, first=False, final=False):
                for k in slots:
                    pe.wait_ge(ada_landed[k], 16 * i + 16)
                    for b in range(3):
                        last = mm(PS[4 * (k % 2) + b][0:2, :], silc[:, 2 * i + k // 2, :], ada[k][:, b * 512:(b + 1) * 512], start=first and k < 2, stop=final and k >= 2)
                    last.then_inc(ada_used, 1)

            for i in range(KT // 2):
                ada_rows(i, range(4), first=i == 0, final=i == KT // 2 - 1)
            pe.wait_ge(ada_pick, 2)
            pe.wait_ge(ada_dve, 2 * KT + 4)
            for h in range(2):
                for j in range(2):
                    last = mm(PS[4 * h + 3][0:2, :], pick[:, j, :], aacc[:, h, j, :], start=j == 0, stop=j == 1)
                last.then_inc(ada_sum, 1)
            pe.wait_ge(row_out, 8)
            pe.sem_inc(pe_go, 1)
            for k in range(32):
                t_ = tr(PS[0][:, 2 * k:2 * k + 2], modrow[:, k * P:(k + 1) * P], ident[0:2, 0:2])
            t_.then_inc(row_T, 1)
            pe.wait_ge(xhat_done, 4)
            for kt in range(KT):
                if kt >= 4:
                    pe.wait_ge(hm_done, kt - 3)
                for t in range(4):
                    t_ = tr(PS[1 + kt % 4][:, t * P:(t + 1) * P], xs[:, t, kt * P:(kt + 1) * P], ident)
                t_.then_inc(xT_done, 1)

            def parts(hi, lo, s, w):
                return ((hi, whi[s][:, w]), (lo, whi[s][:, w]), (hi, wlo[s][:, w]))

            pe.wait_ge(hl_done, KT // 2)
            pe.wait_ge(hl_pool, KT // 2)
            for kt in range(KT):
                s = kt % 2
                pe.wait_ge(wlo_ready, kt + 1)
                groups = [(PS[t], t, slice(1024, 1536)) for t in range(4)]
                groups += [(PS[4 + 2 * t + q], 2 + t, slice(q * 512, (q + 1) * 512)) for t in range(2) for q in range(2)]
                for bank, t, w in groups:
                    ts = slice(t * P, (t + 1) * P)
                    for n, (a_, b_) in enumerate(parts(hth[:, kt, ts], htl[:, kt, ts], s, w)):
                        last = mm(bank[:, :], a_, b_, start=kt == 0 and n == 0, stop=kt == KT - 1 and n == 2)
                last.then_inc(w_used, 1)

            def slab_tile(q, i, tok):
                m = M_SLAB + q
                s = m % 2
                n = tok.stop - tok.start
                pe.wait_ge(wlo_ready, 2 * i + m + 1)
                if q >= 2:
                    pe.wait_ge(slab_done, 2 * i + q - 1)
                else:
                    pe.wait_ge(ctx_out, 2 * q + 2)
                for kt in range(KT):
                    w = slice(kt * P, (kt + 1) * P)
                    for k, (a_, b_) in enumerate(parts(hth[:, kt, tok], htl[:, kt, tok], s, w)):
                        last = mm(PS[q % 2][:, 0:n], b_, a_, start=kt == 0 and k == 0, stop=kt == KT - 1 and k == 2)
                last.then_inc(w_used, 1)

            lat, both = slice(CTX, TOK), slice(0, TOK)
            for q, tok in enumerate((lat, both, both)):
                slab_tile(q, 0, tok)
            q0, turns, _ = SLAB_LOOPS[0]
            with pe.Fori(0, turns) as i:
                for j in range(2):
                    slab_tile(q0 + j, i, lat)

            def mod_sum(acc, k0):
                for k in range(4):
                    last = mm(PS[2][:, k0 + k:k0 + k + 1], acc[:, k * P:(k + 1) * P], onec[:, :], start=True, stop=True)
                return last

            pe.wait_ge(ctx_out, 12)
            pe.wait_ge(m_acc, KT * (M_EARLY + 1))
            for g in range(M_EARLY):
                last = mod_sum(macc[g], 4 * g)
            last.then_inc(m_red, 1)
            q0, turns, _ = SLAB_LOOPS[1]
            with pe.Fori(0, turns) as i:
                pe.wait_ge(m_acc, KT * i + KT * (M_EARLY + 1))
                pe.wait_ge(m_out, i + 1)
                mod_sum(macc[M_EARLY], 0).then_inc(m_red, 1)
                for j in range(2):
                    slab_tile(q0 + j, i, both)
            pe.wait_ge(m_acc, KT * M_GROUPS)
            pe.wait_ge(m_out, turns + 1)
            mod_sum(macc[M_EARLY], 0).then_inc(m_red, 1)

            pe.wait_ge(m_out, turns + 2)
            pe.wait_ge(rot_out, 1)
            pe.wait_ge(slab_done, SLAB)
            for g in range(NKV):
                for t in range(4):
                    t_ = tr(PS[g][:, t * P:(t + 1) * P], ktk[:, t, g * HD:(g + 1) * HD], ident)
                t_.then_inc(kT_done, 1)
            pe.wait_ge(kT_out, 2)
            def queries(h):
                pe.wait_ge(a_qh, h + 1)
                if h:
                    pe.wait_ge(a_qTo, h)
                for t in range(2):
                    t_ = tr(PS[2][:, t * P:(t + 1) * P], qh[:, t, :], ident)
                t_.then_inc(a_qT, 1)

            def scores(h):
                pe.wait_ge(a_qTo, h + 1)
                if h >= 2:
                    pe.wait_ge(a_lg, h - 1)
                for t in range(2):
                    mm(PS[(3, 0)[h % 2] + t][:, :], qT[:, t, :], ktr[:, h // GQ, :], start=True, stop=True).then_inc(a_sc, 1)

            for h in range(2):
                queries(h)
                scores(h)
            queries(2)
            for h in range(NQ):
                for t in range(2):
                    pe.wait_ge(a_pr, 2 * h + t + 1)
                    for k in range(4):
                        t_ = tr(PS[5 + t][:, k * P:(k + 1) * P], sc[:, h % 2, t, k * P:(k + 1) * P], ident)
                    t_.then_inc(a_pT, 1)
                if h + 2 < NQ:
                    scores(h + 2)
                if h + 3 < NQ:
                    queries(h + 3)
                pe.wait_ge(a_oo, h + 1)
                for t in range(2):
                    pe.wait_ge(a_pTo, 2 * h + t + 1)
                    for k in range(4):
                        last = mm(PS[7][:, t * P:(t + 1) * P], vtk[:, k, h // GQ * HD:(h // GQ + 1) * HD], pT[:, t, k * P:(k + 1) * P],
                                  start=k == 0, stop=k == 3)
                last.then_inc(a_o, 1)

            pe.wait_ge(t_lora, 2)
            pe.wait_ge(a_oo, NQ + 1)
            def prep_norms(t):
                pe.wait_ge(g_kq, t + 1)
                mm(PS[2][:, :], ones_bd, sgt[0][:, :], start=True, stop=True).then_inc(g_nr, 1)

            def prep_lora(t, k):
                if k == 0:
                    pe.wait_ge(g_w, 48 * t + 48)
                if k == 2:
                    pe.wait_ge(g_rt, t + 1)
                if k > 2:
                    pe.wait_ge(g_sg, 4 * t + k - 2)
                if k < 4:
                    src, hs = (s_w, s_a)[k // 2], halves[k % 2]
                    ins = mm(PS[(5, 7, 2, 5)[k]][:, :], wsl[hs, k // 2, :], src[hs, :], start=True, stop=True)
                else:
                    ins = mm(PS[7][:, 0:SEQ], wsl[:, 2, :], s_g[:, :], start=True, stop=True)
                ins.then_inc(g_lo, 1)

            PAIR = [(2, 5, 7), (0, 1, 3)]

            def pair_products(t, d):
                pe.wait_ge(g_bb, 4 * t + 2 * d + 2)
                pe.wait_ge(g_kb, 2 * t + d + 1)
                pe.wait_ge(g_bd, 2 * t + d + 1)
                if d == 0:
                    pe.wait_ge(g_sg, 4 * t + 4)
                    pe.wait_ge(g_gg, t + 1)
                for k, lhs in enumerate((bdb[d], bdk[d])):
                    for c_ in range(HC):
                        last = mm(PS[PAIR[d][0]][:, k * SEQ + c_ * L:k * SEQ + (c_ + 1) * L], lhs[:, c_, :], ar[d][:, c_, 0:L],
                                  start=True, stop=True)
                last.then_inc(g_am, 1)
                for k, lhs in enumerate((bdb[d], bdk[d])):
                    for c_ in range(HC):
                        last = mm(PS[PAIR[d][1 + k]][:, c_ * P:(c_ + 1) * P], lhs[:, HC + c_, :], ar[d][:, HC + c_, :],
                                  start=True, stop=True)
                    last.then_inc(g_am, 1)

            PREP = {0: [prep_norms, lambda t: prep_lora(t, 0)], 1: [lambda t: prep_lora(t, 1), lambda t: prep_lora(t, 2)],
                    2: [lambda t: prep_lora(t, 3), lambda t: prep_lora(t, 4)]}

            def read_means(r):
                pe.wait_ge(r_yb, r + 1)
                pe.wait_ge(r_mv, 2 * r + 2)
                mm(PS[5][:, :], ones_bd, yb[:, :, :].rearrange("p a n -> p (a n)"), start=True, stop=True).then_inc(r_mu, 1)

            def read_variances(r):
                pe.wait_ge(r_sq, r + 1)
                pe.wait_ge(r_bm, r + 1)
                mm(PS[2][:, 0:SEQ], ones_bd, yq[:, 0, :], start=True, stop=True).then_inc(r_var, 1)

            def y_known(n, d):
                c_ = chunk(d, n) - HC
                y = PS[6][:, c_ * L:(c_ + 1) * L]
                mm(y, S_[d][:, :], rch[d][:, c_, :], start=n == HC and d == 0, stop=False)
                mm(y, vt[:, HC + c_, :], ark[d][:, c_, :], start=False, stop=False)

            def y_last(n, d):
                c_ = chunk(d, n) - HC
                mm(PS[6][:, c_ * L:(c_ + 1) * L], U_[d][:, :], arb[d][:, c_, :], start=False,
                   stop=n == NCH - 1 and d == 1).then_inc(c_yd, 1)

            def turn(i, read, prep):
                pair_products(i, 1)
                if read:
                    pe.wait_ge(r_yb, i)
                def turned(qs):
                    for q in qs:
                        if q == 2:
                            pe.wait_ge(g_ae, 2 * i + 1)
                        if q >= 5:
                            pe.wait_ge(g_to, 10 * i + q - 4)
                        if q < 8:
                            d, k, g = TURNED[q]
                            src = (bdk, bdb)[k][d]
                        else:
                            src, g = vbd, q - 8
                            pe.wait_ge(g_vb, 2 * i + 2)
                        for c_ in range(HC):
                            t_ = tr(PS[TBANK[q % 5]][:, c_ * P:(c_ + 1) * P], src[:, HC * g + c_, :], ident)
                        t_.then_inc(g_tr, 1)

                def turn_x(z, s):
                    d, g = STREAMS[s]
                    for k in range(HC):
                        t_ = tr(PS[LBANK[s]][:, k * P:(k + 1) * P], z[d][:, HC * g + k, :], ident)
                    t_.then_inc(g_xt, 1)

                turned(range(0, 7))
                for s in range(2):
                    pe.wait_ge(g_to, 10 * i + 6 + s)
                    pe.wait_ge(g_z1, 4 * i + s + 1)
                    turn_x(zn, s)
                turned(range(7, 10))
                pe.wait_ge(g_aa, i + 1)
                for s in range(2, 4):
                    pe.wait_ge(g_z1, 4 * i + s + 1)
                    turn_x(zn, s)
                for l in range(LEVELS):
                    n = 4 * LEVELS * i + 4 * l
                    for s, (d, g) in enumerate(STREAMS):
                        pe.wait_ge(g_xo, n + s + 1)
                        for k in range(HC):
                            ck = HC * g + k
                            last = mm(PS[LBANK[s]][:, k * P:(k + 1) * P], dd[d][:, ck, :], bdk[d][:, ck, :], start=True, stop=True)
                        last.then_inc(g_tm, 1)
                    if prep and l == 0:
                        pe.wait_ge(g_to, 10 * i + 10)
                    if prep:
                        for step in PREP.get(l, ()):
                            step(i + 1)
                    for s, (d, g) in enumerate(STREAMS):
                        pe.wait_ge(g_te, n + s + 1)
                        for k in range(HC):
                            ck = HC * g + k
                            last = mm(PS[LBANK[s]][:, k * P:(k + 1) * P], bdb[d][:, ck, :], (zz if l else zn)[d][:, ck, :], start=True, stop=True)
                        last.then_inc(g_zm, 1)
                    if l < LEVELS - 1:
                        for s, (d, g) in enumerate(STREAMS):
                            pe.wait_ge(g_ze, n + s + 1)
                            turn_x(zz, s)
                pe.wait_ge(g_ze, 4 * LEVELS * i + 4 * LEVELS)
                pe.wait_ge(g_ba, 6 * i + 6)
                pe.wait_ge(g_ae, 2 * i + 2)

                def known_p(n, d):
                    ck = chunk(d, n)
                    return mm(PS[3 * d + 1][:, 0:P], aak[d][:, ck, :], vt[:, ck, :], start=True, stop=n == 0)

                for n in range(NCH):
                    for d in range(2):
                        ck = chunk(d, n)
                        if n:
                            pe.wait_ge(c_so, 2 * (NCH - 1) * i + 2 * n + d - 1)
                            mm(PS[3 * d + 1][:, 0:P], bda[d][:, ck, :], S_[d][:, :], start=False, stop=True).then_inc(c_p, 1)
                        else:
                            known_p(n, d).then_inc(c_p, 1)
                    if read and n == 0:
                        read_means(i - 1)
                    if read and n == 2:
                        read_variances(i - 1)
                    if prep and n == 5:
                        if read:
                            pe.wait_ge(r_vt, i)
                        pair_products(i + 1, 0)
                    for d in range(2):
                        ck = chunk(d, n)
                        pe.wait_ge(c_po, 2 * NCH * i + 2 * n + d + 1)
                        mm(PS[3 * d + 1][:, P:2 * P], zz[d][:, ck, :], P_[d][:, :], start=True, stop=True).then_inc(c_u, 1)
                    if n < NCH - 1:
                        for d in range(2):
                            ck = chunk(d, n)
                            mm(PS[3 * d][:, 0:P], bkt[d][:, ck, :], vt[:, ck, :], start=True, stop=False)
                    if n >= HC:
                        for d in range(2):
                            y_known(n, d)
                    for d in range(2):
                        pe.wait_ge(c_uo, 2 * NCH * i + 2 * n + d + 1)
                        if n < NCH - 1:
                            mm(PS[3 * d][:, 0:P], bbt[d][:, chunk(d, n), :], U_[d][:, :], start=False, stop=True).then_inc(c_s, 1)
                            known_p(n + 1, d)
                    if n >= HC:
                        for d in range(2):
                            y_last(n, d)

            for l in range(LEVELS):
                for step in PREP.get(l, ()):
                    step(0)
            pair_products(0, 0)
            turn(0, False, True)
            with pe.Fori(1, FT - 1) as i:
                turn(i, True, True)
            turn(FT - 1, True, False)
            read_means(FT - 1)
            for b in range(4):
                pe.wait_ge(d_dg, b + 1)
                mm(PS[(0, 1, 3, 4)[b]][:, :], ones[:, :], diag[:, 4 * b:4 * b + 4, :].rearrange("p k n -> p (k n)"),
                   start=True, stop=True).then_inc(d_gm, 1)
                if b == 2:
                    read_variances(FT - 1)
            pe.wait_ge(d_gt, 4)
            pe.wait_ge(r_vt, FT)
            for kt in range(KT):
                m = M_OUT + kt
                s = m % 2
                if kt % 4 == 0:
                    pe.wait_ge(d_ml, kt // 4 + 1)
                pe.wait_ge(wlo_ready, m + 1)
                for b in range(8):
                    ts = slice(b // 4 * P, (b // 4 + 1) * P)
                    w = slice(b % 4 * 512, b % 4 * 512 + 512)
                    for n, (a_, b_) in enumerate(parts(h2h[:, kt, ts], h2l[:, kt, ts], s, w)):
                        last = mm(PS[b][:, :], a_, b_, start=kt == 0 and n == 0, stop=kt == KT - 1 and n == 2)
                last.then_inc(w_used, 1)
            pe.wait_ge(d_x1, 2)
            pe.wait_ge(d_xh, 2)
            for kt in range(KT):
                if kt >= 4:
                    pe.wait_ge(d_hm, kt - 3)
                for t in range(2):
                    t_ = mm(PS[kt % 4][:, t * P:(t + 1) * P], x1[:, t, kt * P:(kt + 1) * P], dg2[:, t, :], start=True, stop=True)
                t_.then_inc(d_tr, 1)
            pe.wait_ge(d_hl, KT // 2)
            pe.wait_ge(hl2_pool, KT // 2)
            for cb in range(4):
                with pe.Fori(0, KT // 2) as i:
                    for j in range(2):
                        m = M_IN + KT * cb + j
                        s = m % 2
                        pe.wait_ge(wlo_ready, 2 * i + m + 1)
                        pe.wait_ge(e_re, 2 * i + (KT * cb + j + 1))
                        for kt in range(KT):
                            for k, (a_, b_) in enumerate(parts(h2h[:, kt, :], h2l[:, kt, :], s, slice(kt * P, (kt + 1) * P))):
                                last = mm(PS[j][:, 0:SEQ], b_, a_, start=kt == 0 and k == 0, stop=kt == KT - 1 and k == 2)
                        last.then_inc(w_used, 1)
                pe.wait_ge(e_acc, KT * (cb + 1) + 4)
                mm(PS[2 + cb][:, :], ones[:, :], gates[:, 1, cb * 512:(cb + 1) * 512], start=True, stop=True).then_inc(e_red, 1)
            pe.wait_ge(e_re, F_FF + 2)
            pe.wait_ge(e_gt, 4)

            def mlp_out(i, j, first=False, final=False):
                m = M_MO + j
                s = m % 2
                pe.wait_ge(f_fl, 2 * i + j + 1)
                pe.wait_ge(wlo_ready, 2 * i + m + 1)
                for b in range(8):
                    ts = slice(b // 4 * P, (b // 4 + 1) * P)
                    w = slice(b % 4 * 512, b % 4 * 512 + 512)
                    for n, (a_, b_) in enumerate(parts(fsh[j][:, ts], fsl[j][:, ts], s, w)):
                        last = mm(PS[b][:, :], a_, b_, start=first and n == 0, stop=final and n == 2)
                last.then_inc(w_used, 1)

            for j in range(2):
                mlp_out(0, j, first=j == 0)
            with pe.Fori(1, F_FF // 2 - 1) as i:
                for j in range(2):
                    mlp_out(i, j)
            for j in range(2):
                mlp_out(F_FF // 2 - 1, j, final=j == 1)


_INS = ["x", "c", "ctx", "c_ctx", "w_ada", "b_ada", "g_pre_mix", "g_post_mix", "g_pre_mlp", "g_post_mlp",
        "w_in", "attn_sink", "rwkv_mu_prev", "rwkv_mu_next", "rwkv_w0", "rwkv_w2", "rwkv_a0", "rwkv_a2",
        "rwkv_g2", "rwkv_k_k", "rwkv_k_a", "rwkv_r_k", "rwkv_ln_w", "rwkv_ln_b", "w_out", "w_mlp_in", "w_mlp_out"]


def kernel(**inputs):
    import numpy as _np
    import concourse.bacc as _bacc
    from concourse import mybir as _mybir
    from concourse.bass_utils import run_bass_kernel_spmd as _run

    nc = _bacc.Bacc("TRN2", target_bir_lowering=False, num_devices=1)
    arrays, args = {}, []
    named = [(name, inputs[name]) for name in _INS] + list(zip(("rec_const", "att_const"), shape_constants()))
    for name, a in named:
        a = _np.ascontiguousarray(a)
        arrays[f"in_{name}_dram"] = a
        args.append(nc.dram_tensor(f"in_{name}_dram", a.shape, _mybir.dt.from_np(a.dtype), kind="ExternalInput").ap())
    args.append(nc.dram_tensor("out_0_dram", (1, SEQ, D), F32, kind="ExternalOutput").ap())
    build_program(nc, *args)
    r = _run(nc, [arrays], core_ids=[0])
    return r.results[0]["out_0_dram"]
```
